# Optimizing a Trainium2 kernel written in Bass

```python
import jax, jax.numpy as jnp
from jax import lax
import numpy as np
import math

D_MODEL = 1024
BATCH = 1
SEQ = 512
DEPTH = 1

GRID_W = 64
HEAD_DIM = 64
RWKV_HEADS = 8
RWKV_WIDTH = RWKV_HEADS * HEAD_DIM
DECAY_RANK = 64
ICLR_RANK = 64
GATE_RANK = 128
NA_HEADS = 8
NA_WIDTH = NA_HEADS * HEAD_DIM
NA_MAX_WIN_ROWS = 8
NA_WIN_COLS = 16
N_GROUPS = 4
EXPERTS_PER_GROUP = 8
N_EXPERTS = N_GROUPS * EXPERTS_PER_GROUP
D_EXPERT = 256
TOP_K_IN_GROUP = 2
RMS_EPS = 1e-6
GN_EPS = 64e-5
NEG_INF = -1e30
RWKV_COLS = 3 * RWKV_WIDTH + 2 * DECAY_RANK + 2 * ICLR_RANK + GATE_RANK
NA_COLS = 3 * NA_WIDTH
GATE_COLS = 2 * D_MODEL
IN_COLS = RWKV_COLS + NA_COLS + GATE_COLS
RWKV_SPLITS = (RWKV_WIDTH, 2 * RWKV_WIDTH, 3 * RWKV_WIDTH,
               3 * RWKV_WIDTH + DECAY_RANK, 3 * RWKV_WIDTH + 2 * DECAY_RANK,
               3 * RWKV_WIDTH + 2 * DECAY_RANK + ICLR_RANK,
               3 * RWKV_WIDTH + 2 * DECAY_RANK + 2 * ICLR_RANK)
IN_SPLITS = (RWKV_COLS, RWKV_COLS + NA_WIDTH, RWKV_COLS + 2 * NA_WIDTH, RWKV_COLS + 3 * NA_WIDTH)


def rmsnorm(x, g):
    x32 = x.astype(jnp.float32)
    y = x32 * lax.rsqrt(jnp.mean(x32 * x32, axis=-1, keepdims=True) + RMS_EPS)
    return (y * g).astype(x.dtype)

def centred_token_shift(p, mu_prev, mu_next):
    prev = jnp.pad(p, ((0, 0), (1, 0), (0, 0)))[:, :-1]
    nxt = jnp.pad(p, ((0, 0), (0, 1), (0, 0)))[:, 1:]
    return p + mu_prev * (prev - p) + mu_next * (nxt - p)

def rwkv_log_decay(lora, w0, up):
    w_raw = (w0 + jnp.tanh(lora) @ up).astype(jnp.float32)
    return -jnp.exp(-jax.nn.softplus(-w_raw) - 0.5)

def rwkv_step(S, inp):
    r_t, w_t, k_t, v_t, kk_t, a_t = inp
    sa = jnp.einsum('dbhij,dbhj->dbhi', S, -kk_t)
    S = (S * w_t[..., None, :] + sa[..., :, None] * (kk_t * a_t)[..., None, :]
         + v_t[..., :, None] * k_t[..., None, :])
    y = jnp.einsum('dbhij,dbhj->dbhi', S, r_t)
    return S, y

def rwkv7_bidirectional(p, mu_prev, mu_next, w0_f, w_up_f, w0_b, w_up_b, a0_f, a_up_f,
                        a0_b, a_up_b, g_up, k_k, k_a, r_k, lnx_g, lnx_b):
    B, T, _ = p.shape
    dt = p.dtype
    p = centred_token_shift(p, mu_prev, mu_next)
    r, k, v, wl_f, wl_b, al_f, al_b, gl = jnp.split(p, RWKV_SPLITS, axis=-1)
    lw_f = rwkv_log_decay(wl_f, w0_f, w_up_f)
    lw_b = rwkv_log_decay(wl_b, w0_b, w_up_b)
    a_f = jax.nn.sigmoid(a0_f + al_f @ a_up_f)
    a_b = jax.nn.sigmoid(a0_b + al_b @ a_up_b)
    g = jax.nn.sigmoid(gl) @ g_up

    def heads(t):
        return t.reshape(B, T, RWKV_HEADS, HEAD_DIM).astype(jnp.float32)

    r_h, v_h = heads(r), heads(v)
    kk = heads(k * k_k)
    kk = kk * lax.rsqrt(jnp.sum(kk * kk, axis=-1, keepdims=True) + 1e-12)
    k_f = heads(k * (1.0 + (a_f - 1.0) * k_a))
    k_b = heads(k * (1.0 + (a_b - 1.0) * k_a))
    a_fh, a_bh = heads(a_f), heads(a_b)
    w_fh, w_bh = jnp.exp(heads(lw_f)), jnp.exp(heads(lw_b))

    def both(f, b):
        return jnp.stack([f, jnp.flip(b, axis=1)], axis=0).transpose(2, 0, 1, 3, 4)

    xs = (both(r_h, r_h), both(w_fh, w_bh), both(k_f, k_b), both(v_h, v_h),
          both(kk, kk), both(a_fh, a_bh))
    S0 = jnp.zeros((2, B, RWKV_HEADS, HEAD_DIM, HEAD_DIM), jnp.float32)
    _, ys = lax.scan(rwkv_step, S0, xs)
    y_f = ys[:, 0].transpose(1, 0, 2, 3)
    y_b = jnp.flip(ys[:, 1].transpose(1, 0, 2, 3), axis=1)
    y = y_f + y_b
    mean = jnp.mean(y, axis=-1, keepdims=True)
    var = jnp.mean(jnp.square(y - mean), axis=-1, keepdims=True)
    y = ((y - mean) * lax.rsqrt(var + GN_EPS)).reshape(B, T, RWKV_WIDTH) * lnx_g + lnx_b
    bonus = jnp.sum(r_h * (k_f + k_b) * r_k, axis=-1, keepdims=True) * v_h
    y = (y + bonus.reshape(B, T, RWKV_WIDTH)) * g
    return y.astype(dt)

def neighbourhood_attention_2d(q, k, v, q_gain, k_gain, rpb):
    B, T, _ = q.shape
    dt = q.dtype
    rows = T // GRID_W
    kh = min(NA_MAX_WIN_ROWS, rows)

    def qk_norm(t, g):
        t32 = t.reshape(B, T, NA_HEADS, HEAD_DIM).astype(jnp.float32)
        return t32 * lax.rsqrt(jnp.mean(t32 * t32, axis=-1, keepdims=True) + RMS_EPS) * g

    def grid(t):
        return t.reshape(B, rows, GRID_W, NA_HEADS, HEAD_DIM).transpose(0, 3, 1, 2, 4)

    qg = grid(qk_norm(q, q_gain) * (HEAD_DIM ** -0.5))
    kg = grid(qk_norm(k, k_gain))
    vg = grid(v.reshape(B, T, NA_HEADS, HEAD_DIM).astype(jnp.float32))

    cols = np.arange(GRID_W)
    col_start = np.clip(cols - NA_WIN_COLS // 2, 0, GRID_W - NA_WIN_COLS)
    col_mask = ((cols[None, :] >= col_start[:, None])
                & (cols[None, :] < col_start[:, None] + NA_WIN_COLS))
    col_off = np.clip(cols[None, :] - cols[:, None] + NA_WIN_COLS - 1, 0, 2 * NA_WIN_COLS - 2)

    def row_block(i):
        start = jnp.clip(i - kh // 2, 0, rows - kh)
        k_blk = lax.dynamic_slice_in_dim(kg, start, kh, axis=2)
        v_blk = lax.dynamic_slice_in_dim(vg, start, kh, axis=2)
        q_blk = lax.dynamic_index_in_dim(qg, i, axis=2, keepdims=False)
        s = jnp.einsum('bhqd,bhrkd->bhqrk', q_blk, k_blk)
        row_off = start + jnp.arange(kh) - i + NA_MAX_WIN_ROWS - 1
        bias = rpb.astype(jnp.float32)[:, row_off][:, :, col_off]
        s = s + bias.transpose(0, 2, 1, 3)[None]
        s = jnp.where(col_mask[:, None, :], s, NEG_INF)
        prob = jax.nn.softmax(s, axis=(-2, -1))
        return jnp.einsum('bhqrk,bhrkd->bhqd', prob, v_blk)

    out = lax.map(row_block, jnp.arange(rows))
    out = out.transpose(1, 0, 3, 2, 4).reshape(B, T, NA_WIDTH)
    return out.astype(dt)

def hierarchical_moe(h, w_rg, b_rg, w_re, b_re, w_gate_e, w_up_e, w_down_e):
    B, T, D = h.shape
    ht = h.reshape(B * T, D)
    n_tok = ht.shape[0]
    g_logits = (ht @ w_rg + b_rg).astype(jnp.float32)
    g_sel = jnp.argmax(g_logits, axis=-1)
    p_group = jnp.take_along_axis(jax.nn.softmax(g_logits, axis=-1), g_sel[:, None], axis=-1)
    e_logits = (ht @ w_re + b_re).astype(jnp.float32).reshape(n_tok, N_GROUPS, EXPERTS_PER_GROUP)
    e_in_group = jnp.take_along_axis(e_logits, g_sel[:, None, None], axis=1)[:, 0]
    top_val, top_idx = lax.top_k(e_in_group, TOP_K_IN_GROUP)
    weights = p_group * jax.nn.softmax(top_val, axis=-1)
    expert_id = g_sel[:, None] * EXPERTS_PER_GROUP + top_idx
    combine = jnp.sum(jax.nn.one_hot(expert_id, N_EXPERTS, dtype=jnp.float32) * weights[..., None], axis=1)
    combine = combine.astype(h.dtype)
    y = jnp.zeros_like(ht)
    for e in range(N_EXPERTS):
        he = jax.nn.silu(ht @ w_gate_e[e]) * (ht @ w_up_e[e])
        y = y + combine[:, e:e + 1] * (he @ w_down_e[e])
    return y.reshape(B, T, D)

def first_inputs(seed: int = 0) -> dict:
    key = jax.random.key(seed)
    ks = iter(jax.random.split(key, 40))
    L = DEPTH

    def nrm(shape, scale):
        return jax.random.normal(next(ks), shape, jnp.float32) * scale

    def unif(shape, lo, hi):
        return jax.random.uniform(next(ks), shape, jnp.float32, lo, hi)

    return {
        'x': nrm((BATCH, SEQ, D_MODEL), 1.0),
        'norm1_g': 1.0 + nrm((L, D_MODEL), 0.02),
        'w_in': nrm((L, D_MODEL, IN_COLS), D_MODEL ** -0.5),
        'mu_prev': unif((L, RWKV_COLS), 0.0, 0.5),
        'mu_next': unif((L, RWKV_COLS), 0.0, 0.5),
        'w0_f': unif((L, RWKV_WIDTH), -6.0, 1.0),
        'w_up_f': nrm((L, DECAY_RANK, RWKV_WIDTH), DECAY_RANK ** -0.5),
        'w0_b': unif((L, RWKV_WIDTH), -6.0, 1.0),
        'w_up_b': nrm((L, DECAY_RANK, RWKV_WIDTH), DECAY_RANK ** -0.5),
        'a0_f': nrm((L, RWKV_WIDTH), 0.5),
        'a_up_f': nrm((L, ICLR_RANK, RWKV_WIDTH), ICLR_RANK ** -0.5),
        'a0_b': nrm((L, RWKV_WIDTH), 0.5),
        'a_up_b': nrm((L, ICLR_RANK, RWKV_WIDTH), ICLR_RANK ** -0.5),
        'g_up': nrm((L, GATE_RANK, RWKV_WIDTH), GATE_RANK ** -0.5),
        'k_k': 0.85 + nrm((L, RWKV_WIDTH), 0.05),
        'k_a': 1.0 + nrm((L, RWKV_WIDTH), 0.05),
        'r_k': nrm((L, RWKV_HEADS, HEAD_DIM), 0.1),
        'lnx_g': 1.0 + nrm((L, RWKV_WIDTH), 0.02),
        'lnx_b': nrm((L, RWKV_WIDTH), 0.01),
        'q_gain': 1.0 + nrm((L, HEAD_DIM), 0.02),
        'k_gain': 1.0 + nrm((L, HEAD_DIM), 0.02),
        'rpb': nrm((L, NA_HEADS, 2 * NA_MAX_WIN_ROWS - 1, 2 * NA_WIN_COLS - 1), 0.1),
        'b_gate': nrm((L, GATE_COLS), 0.01),
        'w_o_rwkv': nrm((L, RWKV_WIDTH, D_MODEL), RWKV_WIDTH ** -0.5),
        'w_o_na': nrm((L, NA_WIDTH, D_MODEL), NA_WIDTH ** -0.5),
        'w_out': nrm((L, D_MODEL, D_MODEL), D_MODEL ** -0.5),
        'norm2_g': 1.0 + nrm((L, D_MODEL), 0.02),
        'w_router_group': nrm((L, D_MODEL, N_GROUPS), D_MODEL ** -0.5),
        'b_router_group': nrm((L, N_GROUPS), 0.01),
        'w_router_expert': nrm((L, D_MODEL, N_EXPERTS), D_MODEL ** -0.5),
        'b_router_expert': nrm((L, N_EXPERTS), 0.01),
        'w_gate_e': nrm((L, N_EXPERTS, D_MODEL, D_EXPERT), D_MODEL ** -0.5),
        'w_up_e': nrm((L, N_EXPERTS, D_MODEL, D_EXPERT), D_MODEL ** -0.5),
        'w_down_e': nrm((L, N_EXPERTS, D_EXPERT, D_MODEL), D_EXPERT ** -0.5),
    }

def first_block(x, norm1_g, w_in, mu_prev, mu_next, w0_f, w_up_f, w0_b, w_up_b, a0_f, a_up_f,
              a0_b, a_up_b, g_up, k_k, k_a, r_k, lnx_g, lnx_b, q_gain, k_gain, rpb, b_gate,
              w_o_rwkv, w_o_na, w_out, norm2_g, w_router_group, b_router_group,
              w_router_expert, b_router_expert, w_gate_e, w_up_e, w_down_e):
    for l in range(DEPTH):
        h = rmsnorm(x, norm1_g[l])
        p = h @ w_in[l]
        p_rwkv, q, k, v, gate_logits = jnp.split(p, IN_SPLITS, axis=-1)
        y_a = rwkv7_bidirectional(p_rwkv, mu_prev[l], mu_next[l], w0_f[l], w_up_f[l], w0_b[l],
                                  w_up_b[l], a0_f[l], a_up_f[l], a0_b[l], a_up_b[l], g_up[l],
                                  k_k[l], k_a[l], r_k[l], lnx_g[l], lnx_b[l]) @ w_o_rwkv[l]
        y_b = neighbourhood_attention_2d(q, k, v, q_gain[l], k_gain[l], rpb[l]) @ w_o_na[l]
        g_a, g_b = jnp.split(jax.nn.sigmoid(gate_logits + b_gate[l]), 2, axis=-1)
        x = x + (g_a * y_a + g_b * y_b) @ w_out[l]
        x = x + hierarchical_moe(rmsnorm(x, norm2_g[l]), w_router_group[l], b_router_group[l],
                                 w_router_expert[l], b_router_expert[l], w_gate_e[l],
                                 w_up_e[l], w_down_e[l])
    return x


CTX_LEN = 256
N_MOD = 6
D_FF = 4 * D_MODEL
CHUNK = 64
NORM_EPS = 1e-6

HY_C = D_MODEL // 4
HY_ORDER = 2
HY_SHORT = 3
HY_EMB = 33
HY_FH = 64
HY_DECAY_TARGET = 1e-2
HY_FAST_PCT = 0.3
HY_SLOW_PCT = 1.5

GLA_H = 4
GLA_VW = 3 * D_MODEL // 8
GLA_KW = GLA_VW // 2
GLA_DK = GLA_KW // GLA_H
GLA_DV = GLA_VW // GLA_H
GLA_RANK = 16
GLA_TAU = 16.0

GDN_H = 4
GDN_W = 3 * D_MODEL // 8
GDN_D = GDN_W // GDN_H
GDN_SHORT = 7

D_MIX = HY_C + GLA_VW + GDN_W
HY_IN = 3 * HY_C
GLA_IN = 2 * GLA_KW + 2 * GLA_VW + 2 * GLA_RANK
GDN_IN = 4 * GDN_W + 4 * GDN_H
IN_SIZES = (HY_IN, GLA_IN, GDN_IN)
N_IN = HY_IN + GLA_IN + GDN_IN


F32 = jnp.float32

def split_last(t, sizes):
    return jnp.split(t, np.cumsum(sizes)[:-1].tolist(), axis=-1)

def rmsnorm_2(x, g):
    xf = x.astype(F32)
    y = xf * lax.rsqrt(jnp.mean(xf * xf, axis=-1, keepdims=True) + NORM_EPS)
    return (y * g.astype(F32)).astype(x.dtype)

def modulate(x, g, shift, scale):
    return rmsnorm_2(x, g) * (1 + scale) + shift

def to_heads(t, n_heads):
    b, l, _ = t.shape
    return t.reshape(b, l, n_heads, -1).transpose(0, 2, 1, 3)

def from_heads(t):
    b, h, l, d = t.shape
    return t.transpose(0, 2, 1, 3).reshape(b, l, h * d)

def l2norm(t):
    return t * lax.rsqrt(jnp.sum(t * t, axis=-1, keepdims=True) + NORM_EPS)

def short_conv(u, w, n_seg, seg_len):
    b, l, ch = u.shape
    k = w.shape[0]
    us = u.reshape(b * n_seg, seg_len, ch)
    out = lax.conv_general_dilated(us, w[:, None, :].astype(u.dtype), window_strides=(1,),
                                   padding=[(k // 2, k // 2)], dimension_numbers=('NWC', 'WIO', 'NWC'),
                                   feature_group_count=ch)
    return out.reshape(b, l, ch)

def hyena_filters(length, w1, b1, w2, b2, w3, sin_freq):
    t = jnp.linspace(0.0, 1.0, length, dtype=F32)[:, None]
    bands = (HY_EMB - 1) // 2
    f = jnp.linspace(1e-4, bands - 1, bands, dtype=F32)
    w = 2 * math.pi * jnp.arange(length, dtype=F32) / length
    ang = w[:, None] * f[None, :]
    z = jnp.concatenate([t, jnp.cos(ang), -jnp.sin(ang)], axis=-1)
    h = jnp.sin(sin_freq[0].astype(F32) * (z @ w1.astype(F32) + b1.astype(F32)))
    h = jnp.sin(sin_freq[1].astype(F32) * (h @ w2.astype(F32) + b2.astype(F32)))
    h = (h @ w3.astype(F32)).reshape(length, HY_ORDER, 2, HY_C)
    deltas = jnp.abs(jnp.linspace(math.log(HY_DECAY_TARGET) / HY_SLOW_PCT,
                                  math.log(HY_DECAY_TARGET) / HY_FAST_PCT, HY_C, dtype=F32))
    h = h * jnp.exp(-t * deltas[None, :])[:, None, None, :]
    h_fwd, h_bwd = h[:, :, 0], h[:, :, 1]
    return jnp.concatenate([h_fwd, jnp.zeros_like(h_fwd[:1]), h_bwd[:0:-1]], axis=0)

def hyena_mix(z, n_seg, seg_len, conv_w, conv_b, filt, d_skip):
    u = (short_conv(z, conv_w, n_seg, seg_len) + conv_b).astype(F32)
    v, x1, x2 = jnp.split(u, 3, axis=-1)
    l = u.shape[1]
    filt_f = jnp.fft.rfft(filt, axis=0)
    y = v
    for o, gate in enumerate((x1, x2)):
        conv = jnp.fft.irfft(jnp.fft.rfft(y, n=2 * l, axis=1) * filt_f[None, :, o], n=2 * l, axis=1)[:, :l]
        y = gate * (conv + d_skip[o].astype(F32) * y)
    return y.astype(z.dtype)

def to_chunks(t, n):
    return jnp.moveaxis(t.reshape(t.shape[:2] + (n, CHUNK) + t.shape[3:]), 2, 0)

def from_chunks(t):
    t = jnp.moveaxis(t, 0, 2)
    return t.reshape(t.shape[:2] + (-1,) + t.shape[4:])

def gla_chunk_scan(q, k, v, log_a, s0):
    n = q.shape[2] // CHUNK
    mask = jnp.tril(jnp.ones((CHUNK, CHUNK), bool))[:, :, None]

    def step(s, xs):
        qc, kc, vc, ac = xs
        b = jnp.cumsum(ac, axis=2)
        diff = b[:, :, :, None, :] - b[:, :, None, :, :]
        decay = jnp.exp(jnp.where(mask, diff, -jnp.inf))
        attn = jnp.einsum('bhid,bhjd,bhijd->bhij', qc, kc, decay)
        o = jnp.einsum('bhid,bhde->bhie', qc * jnp.exp(b), s) + jnp.einsum('bhij,bhje->bhie', attn, vc)
        b_last = b[:, :, -1:, :]
        s_new = jnp.exp(b_last[:, :, 0, :])[..., None] * s + jnp.einsum(
            'bhjd,bhje->bhde', kc * jnp.exp(b_last - b), vc)
        return s_new, o

    s_fin, o = lax.scan(step, s0, (to_chunks(q, n), to_chunks(k, n), to_chunks(v, n), to_chunks(log_a, n)))
    return from_chunks(o), s_fin

def gdn_chunk_scan(q, k, v, g, beta, s0):
    n = q.shape[2] // CHUNK
    dk = q.shape[-1]
    strict = jnp.tril(jnp.ones((CHUNK, CHUNK), bool), -1)
    incl = jnp.tril(jnp.ones((CHUNK, CHUNK), bool))
    eye = jnp.eye(CHUNK, dtype=F32)

    def step(s, xs):
        qc, kc, vc, gc, bc = xs
        gcum = jnp.cumsum(gc, axis=-1)
        diff = gcum[..., :, None] - gcum[..., None, :]
        kb = kc * bc[..., None]
        a = -jnp.einsum('bhid,bhjd->bhij', kb, kc) * jnp.exp(jnp.where(strict, diff, -jnp.inf))
        rhs = jnp.concatenate([kb * jnp.exp(gcum)[..., None], vc * bc[..., None]], axis=-1)
        sol = lax.linalg.triangular_solve(eye - a, rhs, left_side=True, lower=True, unit_diagonal=True)
        w, u = sol[..., :dk], sol[..., dk:]
        v_new = u - w @ s
        attn = jnp.einsum('bhid,bhjd->bhij', qc, kc) * jnp.exp(jnp.where(incl, diff, -jnp.inf))
        o = (qc * jnp.exp(gcum)[..., None]) @ s + attn @ v_new
        g_last = gcum[..., -1:]
        s_new = jnp.exp(g_last)[..., None] * s + jnp.einsum(
            'bhjd,bhje->bhde', kc * jnp.exp(g_last - gcum)[..., None], v_new)
        return s_new, o

    s_fin, o = lax.scan(step, s0, (to_chunks(q, n), to_chunks(k, n), to_chunks(v, n),
                                   to_chunks(g, n), to_chunks(beta, n)))
    return from_chunks(o), s_fin

def bidir_scan(scan_fn, shared, fwd, bwd, s0_f, s0_b):
    o_f, s_f = scan_fn(*shared, *fwd, s0_f)
    flip = lambda a: jnp.flip(a, axis=2)
    o_b, s_b = scan_fn(*[flip(a) for a in shared], *[flip(a) for a in bwd], s0_b)
    return o_f + flip(o_b), s_f, s_b

def gated_head_norm(o, gate, g_norm):
    y = o * lax.rsqrt(jnp.mean(o * o, axis=-1, keepdims=True) + NORM_EPS) * g_norm.astype(F32)
    return from_heads(y) * jax.nn.silu(gate.astype(F32))

def gla_prep(z, w_a2, b_a):
    zf = z.astype(F32)
    q, k, v, gate, a_f, a_b = split_last(zf, (GLA_KW, GLA_KW, GLA_VW, GLA_VW, GLA_RANK, GLA_RANK))
    log_a = [to_heads(jax.nn.log_sigmoid(a @ w_a2[d].astype(F32) + b_a[d].astype(F32)) / GLA_TAU, GLA_H)
             for d, a in enumerate((a_f, a_b))]
    shared = (to_heads(q, GLA_H) * GLA_DK ** -0.5, to_heads(k, GLA_H), to_heads(v, GLA_H))
    return shared, (log_a[0],), (log_a[1],), gate

def gla_branch(z_lat, z_ctx, with_ctx_out, w_a2, b_a, norm_g):
    sh_c, fw_c, bw_c, gate_c = gla_prep(z_ctx, w_a2, b_a)
    s0 = jnp.zeros((z_ctx.shape[0], GLA_H, GLA_DK, GLA_DV), F32)
    o_c, s_f, s_b = bidir_scan(gla_chunk_scan, sh_c, fw_c, bw_c, s0, s0)
    sh_l, fw_l, bw_l, gate_l = gla_prep(z_lat, w_a2, b_a)
    o_l, _, _ = bidir_scan(gla_chunk_scan, sh_l, fw_l, bw_l, s_f, s_b)
    out_lat = gated_head_norm(o_l, gate_l, norm_g).astype(z_lat.dtype)
    out_ctx = gated_head_norm(o_c, gate_c, norm_g).astype(z_ctx.dtype) if with_ctx_out else None
    return out_lat, out_ctx

def gdn_prep(z, conv_w, a_log, dt_bias, n_seg, seg_len):
    qkv, gate, a_f, a_b, b_f, b_b = split_last(z, (3 * GDN_W, GDN_W, GDN_H, GDN_H, GDN_H, GDN_H))
    qkv = jax.nn.silu(short_conv(qkv, conv_w, n_seg, seg_len)).astype(F32)
    q, k, v = jnp.split(qkv, 3, axis=-1)
    shared = (l2norm(to_heads(q, GDN_H)) * GDN_D ** -0.5, l2norm(to_heads(k, GDN_H)), to_heads(v, GDN_H))

    def log_decay(a, d):
        return (-jnp.exp(a_log[d].astype(F32)) *
                jax.nn.softplus(a.astype(F32) + dt_bias[d].astype(F32))).transpose(0, 2, 1)

    def write_gate(b):
        return jax.nn.sigmoid(b.astype(F32)).transpose(0, 2, 1)

    return shared, (log_decay(a_f, 0), write_gate(b_f)), (log_decay(a_b, 1), write_gate(b_b)), gate

def gdn_branch(z_lat, z_ctx, rows, with_ctx_out, conv_w, a_log, dt_bias, norm_g):
    sh_c, fw_c, bw_c, gate_c = gdn_prep(z_ctx, conv_w, a_log, dt_bias, 1, z_ctx.shape[1])
    s0 = jnp.zeros((z_ctx.shape[0], GDN_H, GDN_D, GDN_D), F32)
    o_c, s_f, s_b = bidir_scan(gdn_chunk_scan, sh_c, fw_c, bw_c, s0, s0)
    sh_l, fw_l, bw_l, gate_l = gdn_prep(z_lat, conv_w, a_log, dt_bias, rows, GRID_W)
    o_l, _, _ = bidir_scan(gdn_chunk_scan, sh_l, fw_l, bw_l, s_f, s_b)
    out_lat = gated_head_norm(o_l, gate_l, norm_g).astype(z_lat.dtype)
    out_ctx = gated_head_norm(o_c, gate_c, norm_g).astype(z_ctx.dtype) if with_ctx_out else None
    return out_lat, out_ctx

def mixer(h, hc, rows, with_ctx_out, w_in, w_out, hy_conv_w, hy_conv_b, hy_filter, hy_d,
          gla_w_a2, gla_b_a, gla_norm_g, gdn_conv_w, gdn_a_log, gdn_dt_bias, gdn_norm_g):
    zl_hy, zl_gla, zl_gdn = split_last(h @ w_in, IN_SIZES)
    zc_hy, zc_gla, zc_gdn = split_last(hc @ w_in, IN_SIZES)
    hy_lat = hyena_mix(zl_hy, rows, GRID_W, hy_conv_w, hy_conv_b, hyena_filters(h.shape[1], *hy_filter), hy_d)
    gla_lat, gla_ctx = gla_branch(zl_gla, zc_gla, with_ctx_out, gla_w_a2, gla_b_a, gla_norm_g)
    gdn_lat, gdn_ctx = gdn_branch(zl_gdn, zc_gdn, rows, with_ctx_out, gdn_conv_w, gdn_a_log, gdn_dt_bias, gdn_norm_g)
    y_lat = jnp.concatenate([hy_lat, gla_lat, gdn_lat], axis=-1) @ w_out
    if not with_ctx_out:
        return y_lat, None
    hy_ctx = hyena_mix(zc_hy, 1, hc.shape[1], hy_conv_w, hy_conv_b, hyena_filters(hc.shape[1], *hy_filter), hy_d)
    y_ctx = jnp.concatenate([hy_ctx, gla_ctx, gdn_ctx], axis=-1) @ w_out
    return y_lat, y_ctx

def sq_relu_mlp(h, w1, w2):
    return jnp.square(jax.nn.relu(h @ w1)) @ w2

def second_inputs(seed: int = 0) -> dict:
    key = jax.random.key(seed)
    ks = iter(jax.random.split(key, 32))
    nrm = lambda shape, std: std * jax.random.normal(next(ks), shape, F32)
    dt = jnp.exp(jax.random.uniform(next(ks), (DEPTH, 2, GDN_H), F32, math.log(1e-3), math.log(1e-1)))
    return {
        'x': nrm((BATCH, SEQ, D_MODEL), 1.0),
        'c': nrm((BATCH, D_MODEL), 1.0),
        'ctx': nrm((BATCH, CTX_LEN, D_MODEL), 1.0),
        'c_ctx': nrm((D_MODEL,), 1.0),
        'norm1_g': 1.0 + nrm((DEPTH, D_MODEL), 0.05),
        'norm2_g': 1.0 + nrm((DEPTH, D_MODEL), 0.05),
        'w_mod': nrm((DEPTH, D_MODEL, N_MOD * D_MODEL), D_MODEL ** -0.5),
        'b_mod': nrm((DEPTH, N_MOD * D_MODEL), 0.02),
        'w_in': nrm((DEPTH, D_MODEL, N_IN), D_MODEL ** -0.5),
        'w_out': nrm((DEPTH, D_MIX, D_MODEL), D_MIX ** -0.5),
        'hy_conv_w': nrm((DEPTH, HY_SHORT, HY_IN), HY_SHORT ** -0.5),
        'hy_conv_b': nrm((DEPTH, HY_IN), 0.02),
        'hy_f_w1': nrm((DEPTH, HY_EMB, HY_FH), HY_EMB ** -0.5),
        'hy_f_b1': nrm((DEPTH, HY_FH), 0.02),
        'hy_f_w2': nrm((DEPTH, HY_FH, HY_FH), HY_FH ** -0.5),
        'hy_f_b2': nrm((DEPTH, HY_FH), 0.02),
        'hy_f_w3': nrm((DEPTH, HY_FH, HY_ORDER * 2 * HY_C), 0.05 * HY_FH ** -0.5),
        'hy_sin_freq': 1.0 + nrm((DEPTH, 2, HY_FH), 0.05),
        'hy_d': nrm((DEPTH, HY_ORDER, HY_C), 1.0),
        'gla_w_a2': nrm((DEPTH, 2, GLA_RANK, GLA_KW), GLA_RANK ** -0.5),
        'gla_b_a': nrm((DEPTH, 2, GLA_KW), 0.02),
        'gla_norm_g': 1.0 + nrm((DEPTH, GLA_DV), 0.05),
        'gdn_conv_w': nrm((DEPTH, GDN_SHORT, 3 * GDN_W), GDN_SHORT ** -0.5),
        'gdn_a_log': jnp.log(jax.random.uniform(next(ks), (DEPTH, 2, GDN_H), F32, 1.0, 16.0)),
        'gdn_dt_bias': dt + jnp.log(-jnp.expm1(-dt)),
        'gdn_norm_g': 1.0 + nrm((DEPTH, GDN_D), 0.05),
        'w_mlp1': nrm((DEPTH, D_MODEL, D_FF), D_MODEL ** -0.5),
        'w_mlp2': nrm((DEPTH, D_FF, D_MODEL), D_FF ** -0.5),
        'final_norm_g': 1.0 + nrm((D_MODEL,), 0.05),
    }

def second_block(x, c, ctx, c_ctx, norm1_g, norm2_g, w_mod, b_mod, w_in, w_out, hy_conv_w, hy_conv_b,
              hy_f_w1, hy_f_b1, hy_f_w2, hy_f_b2, hy_f_w3, hy_sin_freq, hy_d, gla_w_a2, gla_b_a, gla_norm_g,
              gdn_conv_w, gdn_a_log, gdn_dt_bias, gdn_norm_g, w_mlp1, w_mlp2, final_norm_g):
    rows = x.shape[1] // GRID_W
    silu_c = jax.nn.silu(c)
    silu_cc = jax.nn.silu(c_ctx)
    for l in range(DEPTH):
        with_ctx_out = l < DEPTH - 1
        sh1, sc1, g1, sh2, sc2, g2 = jnp.split((silu_c @ w_mod[l] + b_mod[l])[:, None, :], N_MOD, axis=-1)
        csh1, csc1, cg1, csh2, csc2, cg2 = jnp.split(silu_cc @ w_mod[l] + b_mod[l], N_MOD, axis=-1)
        h = modulate(x, norm1_g[l], sh1, sc1)
        hc = modulate(ctx, norm1_g[l], csh1, csc1)
        hy_filter = (hy_f_w1[l], hy_f_b1[l], hy_f_w2[l], hy_f_b2[l], hy_f_w3[l], hy_sin_freq[l])
        y, yc = mixer(h, hc, rows, with_ctx_out, w_in[l], w_out[l], hy_conv_w[l], hy_conv_b[l], hy_filter,
                      hy_d[l], gla_w_a2[l], gla_b_a[l], gla_norm_g[l], gdn_conv_w[l], gdn_a_log[l],
                      gdn_dt_bias[l], gdn_norm_g[l])
        x = x + g1 * y
        x = x + g2 * sq_relu_mlp(modulate(x, norm2_g[l], sh2, sc2), w_mlp1[l], w_mlp2[l])
        if with_ctx_out:
            ctx = ctx + cg1 * yc
            ctx = ctx + cg2 * sq_relu_mlp(modulate(ctx, norm2_g[l], csh2, csc2), w_mlp1[l], w_mlp2[l])
    return rmsnorm_2(x, final_norm_g)


def setup_inputs(seed=0):
    out = dict(first_inputs(seed))
    for name, value in second_inputs(seed + 1).items():
        if name != "x":
            out[name + "_2"] = value
    return out


def reference(
    x, norm1_g, w_in, mu_prev, mu_next, w0_f, w_up_f, w0_b, w_up_b, a0_f, a_up_f, a0_b, a_up_b,
    g_up, k_k, k_a, r_k, lnx_g, lnx_b, q_gain, k_gain, rpb, b_gate, w_o_rwkv, w_o_na, w_out,
    norm2_g, w_router_group, b_router_group, w_router_expert, b_router_expert, w_gate_e, w_up_e,
    w_down_e, c_2, ctx_2, c_ctx_2, norm1_g_2, norm2_g_2, w_mod_2, b_mod_2, w_in_2, w_out_2,
    hy_conv_w_2, hy_conv_b_2, hy_f_w1_2, hy_f_b1_2, hy_f_w2_2, hy_f_b2_2, hy_f_w3_2,
    hy_sin_freq_2, hy_d_2, gla_w_a2_2, gla_b_a_2, gla_norm_g_2, gdn_conv_w_2, gdn_a_log_2,
    gdn_dt_bias_2, gdn_norm_g_2, w_mlp1_2, w_mlp2_2, final_norm_g_2,
):
    x = first_block(
        x, norm1_g, w_in, mu_prev, mu_next, w0_f, w_up_f, w0_b, w_up_b, a0_f, a_up_f, a0_b,
        a_up_b, g_up, k_k, k_a, r_k, lnx_g, lnx_b, q_gain, k_gain, rpb, b_gate, w_o_rwkv,
        w_o_na, w_out, norm2_g, w_router_group, b_router_group, w_router_expert,
        b_router_expert, w_gate_e, w_up_e, w_down_e,
    )
    return second_block(
        x, c_2, ctx_2, c_ctx_2, norm1_g_2, norm2_g_2, w_mod_2, b_mod_2, w_in_2, w_out_2,
        hy_conv_w_2, hy_conv_b_2, hy_f_w1_2, hy_f_b1_2, hy_f_w2_2, hy_f_b2_2, hy_f_w3_2,
        hy_sin_freq_2, hy_d_2, gla_w_a2_2, gla_b_a_2, gla_norm_g_2, gdn_conv_w_2, gdn_a_log_2,
        gdn_dt_bias_2, gdn_norm_g_2, w_mlp1_2, w_mlp2_2, final_norm_g_2,
    )


_drawn_inputs = setup_inputs


def setup_inputs(seed=0):
    import zlib

    import numpy as np

    out = dict(_drawn_inputs(seed))
    spreads = {}
    factors = {'lnx_b': 6.333,
     'q_gain': 6.386,
     'k_gain': 5.107,
     'rpb': 3.18,
     'b_gate': 8.0,
     'b_router_group': 21.745,
     'b_router_expert': 3.629,
     'hy_conv_b_2': 3.984,
     'hy_f_b1_2': 2.867,
     'hy_sin_freq_2': 4.491,
     'gla_b_a_2': 8.0,
     'gla_norm_g_2': 6.554,
     'gdn_norm_g_2': 4.825,
     'lnx_g': 2.834,
     'norm2_g_2': 3.01,
     'hy_f_b2_2': 4.564}
    for name, (base, spread) in spreads.items():
        noise = np.random.default_rng([zlib.crc32(name.encode()), seed]).standard_normal(out[name].shape)
        drawn = base * np.exp(spread * noise) if base else spread * noise
        out[name] = __import__('jax').numpy.asarray(drawn.astype(out[name].dtype))
    for name, factor in factors.items():
        out[name] = (out[name] * factor).astype(out[name].dtype)
    return out
```

```python
from contextlib import ExitStack

import numpy as np
import concourse.bass as bass
from concourse import mybir

F32 = mybir.dt.float32
ACT = mybir.ActivationFunctionType
ALU = mybir.AluOpType
AX = mybir.AxisListType

P = 128
D = 1024
DB = D // P
T = 512
NT = T // P
CTX = 256
T2 = CTX + T
NT2 = T2 // P
GRID_W = 64
RH, HD = 8, 64
RW = RH * HD
RB = RW // P
NE = 32
RING = 8
UNIT = 1024
RMS_EPS, GN_EPS, L2_EPS = 1e-6, 64e-5, 1e-12
DECAY = float(np.exp(-0.5))
LEVELS = 7
HY_C = 256
NFREQ = 512
GLA_H, GLA_DK, GLA_DV = 4, 48, 96
GDN_H, GDN_D = 4, 96
VW = 384

def table(*items):
    at, out = 0, {}
    for name, n in items:
        out[name] = (at, n)
        at += n
    return out, at

CONST, N_CONST = table(("ident", P), ("ones", P), ("ones64", P), ("tri_f", 2 * P), ("tri_b", 2 * P),
                       ("attn_f", 4 * P), ("attn_b", 4 * P), ("level_f", LEVELS * P),
                       ("level_b", LEVELS * P))
COL, N_COL = table(("norm1_g", 8), ("mu_prev", 15), ("mu_next", 15), ("a0_f", 4), ("a0_b", 4),
                   ("k_k", 4), ("k_a", 4), ("r_k", 4), ("b_gate", 16), ("norm2_g", 8),
                   ("q_gain", 1), ("k_gain", 1), ("norm1_g_2", 8), ("norm2_g_2", 8), ("b_mod", 48),
                   ("cc", 16), ("hy_w", 18), ("hy_b", 6), ("hy_d", 4), ("gdn_w", 77),
                   ("final_g", 8), ("hy_b1", 1), ("hy_b2", 1), ("hy_f1", 1), ("hy_f2", 1))
ROW, N_ROW = table(("w0_f", RW), ("w0_b", RW), ("lnx_g", RW), ("lnx_b", RW), ("b_router", 36),
                   ("gla_b", 512), ("gla_g", 96), ("gdn_g", 96), ("a_log", 8), ("dt_bias", 8))
MAT, N_MAT = table(("w_up", RW), ("a_up", RW), ("g_up", RW), ("hsum", RB * 8), ("router", DB * 36),
                   ("hy_w1", 64), ("hy_w2", 64), ("hy_w3", 1024), ("gla_a2", 256), ("na_mask", 64),
                   ("gidx", 12))

STREAM, N_UNITS = table(("qk", 8), ("v", 4), ("rwkv", 15), ("gate", 16), ("o", 8), ("out", 8),
                        ("moe", NE * 6), ("mod", 48), ("hy", 6), ("misc2", 1), ("gla_q", 2), ("gla_k", 2),
                        ("gla_v", 3), ("gla_gate", 3), ("gdn_qk", 8), ("gdn_v", 3), ("gdn_gate", 3),
                        ("out2", 8), ("mlp1", 32), ("mlp2", 32))


class Signal:

    def __init__(self, sem):
        self.sem, self.base, self.n = sem, 0, 0

    def up(self, by=1):
        self.n += by
        return by

    def at(self, n):
        assert self.base + n > 0
        return self.base + n

    @property
    def last(self):
        return self.base + self.n


class Core:

    def __init__(self, nc, dram, ctx):
        self.nc, self.dram, self.ctx = nc, dram, ctx
        self.signals, self.names = {}, {}
        self.ring = self.sb("ring", [P, RING, UNIT])
        self.landed = [ctx.enter_context(nc.semaphore(f"unit_landed{s}")) for s in range(RING)]
        self.used = ctx.enter_context(nc.semaphore("unit_used"))
        self.issued = self.taken = 0
        self.const = self.sb("const", [P, N_CONST])
        self.cols = self.sb("cols", [P, N_COL])
        self.xT = self.sb("xT", [P, DB, T])
        self.ps = ctx.enter_context(nc.psum_tensor("ps", [P, 8, 512], F32))

    def sb(self, name, shape, ctx=None):
        self.names[name] = n = self.names.setdefault(name, 0) + 1
        return (ctx or self.ctx).enter_context(self.nc.sbuf_tensor(f"{name}_{n}" if n > 1 else name, shape, F32))

    def sig(self, name):
        if name not in self.signals:
            self.signals[name] = Signal(self.ctx.enter_context(self.nc.semaphore(name)))
        return self.signals[name]

    def stage_end(self):
        for s in self.signals.values():
            s.base, s.n = s.base + s.n, 0

    def c(self, name):
        a, n = CONST[name]
        return self.const[:, a:a + n]

    def col(self, name, i=0, p0=0, p1=P):
        a, n = COL[name]
        return self.cols[p0:p1, a + i:a + i + 1]

    def stream(self, sp, units):
        end = min(self.taken_at_stage + units + RING, N_UNITS)
        while self.issued < end:
            u = self.issued
            if u >= RING:
                sp.wait_ge(self.used, u - RING + 1)
            sp.dma_start(self.ring[:, u % RING, :], self.dram["stream"][u]).then_inc(self.landed[u % RING], 16)
            self.issued += 1

    def take(self):
        u = self.taken
        self.taken += 1
        return self.ring[:, u % RING, :], self.landed[u % RING], 16 * (u // RING + 1)

    def after(self, i):
        return self.taken_at_stage + i + 1

    def block(self):
        self.taken_at_stage = self.taken
        return self.nc.Block()


def stage_load(k):
    with k.block() as block:
        @block.sync
        def _(sp):
            got = k.sig("load")
            sp.dma_start(k.xT[:, :, :], k.dram["xT"]).then_inc(got.sem, got.up(16))
            sp.dma_start(k.cols[:, :], k.dram["cols"]).then_inc(got.sem, got.up(16))
            sp.dma_start(k.const[:, :], k.dram["const"]).then_inc(got.sem, got.up(16))
            k.stream(sp, 0)
            sp.wait_ge(got.sem, got.at(48))
    k.stage_end()


def stage_norm(k, name, src, dst, n, gain, eps=RMS_EPS, shift=None):
    with ExitStack() as st:
        sq = k.sb(name + "_sq", [P, DB, n], st)
        std = k.sb(name + "_std", [P, n], st)
        with k.block() as block:
            squared, summed, rooted, chain = (k.sig(x) for x in ("squared", "summed", "rooted", "chain_v"))

            @block.scalar
            def _(act):
                for b in range(DB):
                    act.activation(sq[:, b, :], src(b), ACT.Square).then_inc(squared.sem, squared.up())
                act.wait_ge(summed.sem, summed.at(1))
                act.activation(std[:, :], k.ps[:, 0, 0:n], ACT.Sqrt, scale=1.0 / D, bias=eps).then_inc(rooted.sem, rooted.up())

            @block.tensor
            def _(pe):
                for b in range(DB):
                    pe.wait_ge(squared.sem, squared.at(b + 1))
                    mm = pe.matmul(k.ps[:, 0, 0:n], k.c("ones"), sq[:, b, :], start=b == 0, stop=b == DB - 1)
                mm.then_inc(summed.sem, summed.up())

            @block.vector
            def _(dve):
                dve.wait_ge(rooted.sem, rooted.at(1))
                dve.reciprocal(std[:, :], std[:, :]).then_inc(chain.sem, chain.up())
                dve.wait_ge(chain.sem, chain.last)
                for b in range(DB):
                    dve.scalar_tensor_tensor(dst(b), src(b), gain(b), std[:, :], ALU.mult, ALU.mult).then_inc(chain.sem, chain.up())
                if shift:
                    for b in range(DB):
                        dve.wait_ge(chain.sem, chain.at(2 + b))
                        dve.tensor_scalar(dst(b), dst(b), shift(b), None, ALU.add).then_inc(chain.sem, chain.up())

            @block.sync
            def _(sp):
                k.stream(sp, 0)
        k.stage_end()


def stage_qkv(k, hT, qT, kT, vt):
    with k.block() as block:
        copied = [k.sig("copied_act"), k.sig("copied_dve")]

        @block.tensor
        def _(pe):
            for g in range(8):
                w, landed, full = k.take()
                pe.wait_ge(landed, full)
                for kt in range(DB):
                    mm = pe.matmul(k.ps[:, g, :], w[:, kt * P:(kt + 1) * P], hT[:, kt, :],
                                   start=kt == 0, stop=kt == DB - 1)
                mm.then_inc(k.used, 1)
            for u in range(4):
                w, landed, full = k.take()
                pe.wait_ge(landed, full)
                for j in range(2):
                    kt = 2 * u + j
                    for t in range(NT):
                        if kt == 0:
                            pe.wait_ge(copied[t % 2].sem, copied[t % 2].at(t // 2 + 1))
                        mm = pe.matmul(k.ps[:, t, :], hT[:, kt, t * P:(t + 1) * P], w[:, j * 512:(j + 1) * 512],
                                       start=kt == 0, stop=kt == DB - 1, skip_group_check=True)
                mm.then_inc(k.used, 1)

        def dst(g):
            return qT[:, g, :] if g < 4 else kT[:, g - 4, :] if g < 8 else vt[:, g - 8, :]

        @block.scalar
        def _(act):
            for g in range(0, 12, 2):
                act.wait_ge(k.used, k.after(g if g < 8 else 11))
                act.copy(dst(g), k.ps[:, g % 8, :]).then_inc(copied[0].sem, copied[0].up())

        @block.vector
        def _(dve):
            for g in range(1, 12, 2):
                dve.wait_ge(k.used, k.after(g if g < 8 else 11))
                dve.tensor_copy(dst(g), k.ps[:, g % 8, :]).then_inc(copied[1].sem, copied[1].up())

        @block.sync
        def _(sp):
            k.stream(sp, 12)
    k.stage_end()


def stage_qk_norm(k, qT, kT):
    with ExitStack() as st:
        sq = k.sb("qk_sq", [P, 8, T], st)
        std = k.sb("qk_std", [P, 8, T], st)
        with k.block() as block:
            squared, summed, rooted, chain = (k.sig(x) for x in ("squared", "summed", "rooted", "chain_v"))

            def src(g):
                return qT[:, g, :] if g < 4 else kT[:, g - 4, :]

            @block.scalar
            def _(act):
                for g in range(8):
                    act.activation(sq[:, g, :], src(g), ACT.Square).then_inc(squared.sem, squared.up())
                for g in range(8):
                    act.wait_ge(summed.sem, summed.at(g + 1))
                    f = 1.0 if g < 4 else 1.0 / HD
                    act.activation(std[:, g, :], k.ps[:, g, :], ACT.Sqrt, scale=f, bias=f * HD * RMS_EPS).then_inc(rooted.sem, rooted.up())

            @block.tensor
            def _(pe):
                for g in range(8):
                    pe.wait_ge(squared.sem, squared.at(g + 1))
                    pe.matmul(k.ps[:, g, :], k.c("ones64"), sq[:, g, :], start=True, stop=True).then_inc(summed.sem, summed.up())

            @block.vector
            def _(dve):
                for g in range(8):
                    dve.wait_ge(rooted.sem, rooted.at(g + 1))
                    dve.reciprocal(std[:, g, :], std[:, g, :]).then_inc(chain.sem, chain.up())
                    dve.wait_ge(chain.sem, chain.last)
                    dve.scalar_tensor_tensor(src(g), src(g), k.col("q_gain" if g < 4 else "k_gain"),
                                             std[:, g, :], ALU.mult, ALU.mult).then_inc(chain.sem, chain.up())
        k.stage_end()


def stage_attention(k, qT, kT, vt, yT):
    OFFS = 14
    with ExitStack() as st:
        rel = k.sb("na_rel", [P, RH, OFFS * GRID_W], st)
        mask = k.sb("na_mask", [P, GRID_W], st)
        s_sb = k.sb("na_s", [P, 2, T], st)
        p_sb = k.sb("na_p", [P, 2, T], st)
        pT = k.sb("na_pT", [P, 2, T], st)
        y = k.sb("na_y", [P, NT, RW], st)
        stat = k.sb("na_stat", [P, 4, RH * NT], st)
        N = RH * NT
        with k.block() as block:
            got, masked = k.sig("load"), k.sig("masked")
            s_ready, biased, p_ready = k.sig("s_ready"), k.sig("biased"), k.sig("p_ready")
            t_ready, pt_ready, o_ready, o_done = (k.sig(x) for x in ("t_ready", "pt_ready", "o_ready", "o_done"))
            chain, y_ready, y_copied = k.sig("chain_v"), k.sig("y_ready"), k.sig("y_copied")

            @block.sync
            def _(sp):
                sp.dma_start(rel[:, :, :], k.dram["rel"]).then_inc(got.sem, got.up(16))
                a, n = MAT["na_mask"]
                sp.dma_start(mask[:, :], k.dram["mats"][:, a:a + n]).then_inc(got.sem, got.up(16))

            @block.gpsimd
            def _(pool):
                pool.wait_ge(got.sem, got.at(32))
                v = rel[:, :, :].rearrange("p h (o c) -> p (h o) c", c=GRID_W)
                pool.tensor_tensor(v, v, mask[:, :].unsqueeze(1).broadcast_to([P, RH * OFFS, GRID_W]), ALU.add).then_inc(masked.sem, masked.up())

            @block.tensor
            def _(pe):
                for i in range(N + 2):
                    if i < N:
                        h, t = divmod(i, NT)
                        a = HD * (h % 2)
                        if i >= 2:
                            pe.wait_ge(biased.sem, biased.at(i - 1))
                        pe.matmul(k.ps[:, i % 2, :], qT[a:a + HD, h // 2, t * P:(t + 1) * P],
                                  kT[a:a + HD, h // 2, :], start=True, stop=True).then_inc(s_ready.sem, s_ready.up())
                    if 1 <= i <= N:
                        j = i - 1
                        pe.wait_ge(p_ready.sem, p_ready.at(j + 1))
                        if j >= 2:
                            pe.wait_ge(pt_ready.sem, pt_ready.at(j - 1))
                        for q in range(NT):
                            mm = pe.transpose(k.ps[:, 2 + j % 2, q * P:(q + 1) * P],
                                              p_sb[:, j % 2, q * P:(q + 1) * P], k.c("ident"))
                        mm.then_inc(t_ready.sem, t_ready.up())
                    if i >= 2:
                        j = i - 2
                        h = j // NT
                        pe.wait_ge(pt_ready.sem, pt_ready.at(j + 1))
                        if j >= 2:
                            pe.wait_ge(o_done.sem, o_done.at(j - 1))
                        for q in range(NT):
                            mm = pe.matmul(k.ps[:, 4 + j % 2, 0:HD], pT[:, j % 2, q * P:(q + 1) * P],
                                           vt[:, q, h * HD:(h + 1) * HD], start=q == 0, stop=q == NT - 1)
                        mm.then_inc(o_ready.sem, o_ready.up())
                pe.wait_ge(o_done.sem, o_done.at(N))
                for b in range(RB):
                    for t in range(NT):
                        mm = pe.transpose(k.ps[:, b, t * P:(t + 1) * P], y[:, t, b * P:(b + 1) * P], k.c("ident"))
                    mm.then_inc(y_ready.sem, y_ready.up())

            @block.vector
            def _(dve):
                dve.wait_ge(masked.sem, masked.at(1))
                for i in range(N + 1):
                    if i < N:
                        h, t = divmod(i, NT)
                        dve.wait_ge(s_ready.sem, s_ready.at(i + 1))
                        if i >= 2:
                            dve.wait_ge(p_ready.sem, p_ready.at(i - 1))
                        off = (6 - 2 * t) * GRID_W
                        dve.tensor_tensor(s_sb[:, i % 2, :], k.ps[:, i % 2, :],
                                          rel[:, h, off:off + T], ALU.add).then_inc(biased.sem, biased.up())
                        dve.wait_ge(biased.sem, biased.at(i + 1))
                        dve.tensor_reduce(stat[:, 0, i:i + 1], s_sb[:, i % 2, :], AX.X, ALU.max, negate=True).then_inc(chain.sem, chain.up())
                    if i >= 1:
                        j = i - 1
                        h, t = divmod(j, NT)
                        dve.wait_ge(p_ready.sem, p_ready.at(j + 1))
                        dve.reciprocal(stat[:, 2, j:j + 1], stat[:, 1, j:j + 1]).then_inc(k.sig("chain_w").sem, k.sig("chain_w").up())
                        dve.wait_ge(k.sig("chain_w").sem, k.sig("chain_w").last)
                        dve.wait_ge(o_ready.sem, o_ready.at(j + 1))
                        dve.tensor_scalar(y[:, t, h * HD:(h + 1) * HD], k.ps[:, 4 + j % 2, 0:HD],
                                          stat[:, 2, j:j + 1], None, ALU.mult).then_inc(o_done.sem, o_done.up())

            @block.scalar
            def _(act):
                for i in range(N + 1):
                    if i < N:
                        act.wait_ge(chain.sem, chain.at(i + 1))
                        if i >= 2:
                            act.wait_ge(t_ready.sem, t_ready.at(i - 1))
                        act.activation(p_sb[:, i % 2, :], s_sb[:, i % 2, :], ACT.Exp,
                                       bias=stat[:, 0, i:i + 1], accum_out=stat[:, 1, i:i + 1]).then_inc(p_ready.sem, p_ready.up())
                    if i >= 1:
                        j = i - 1
                        act.wait_ge(t_ready.sem, t_ready.at(j + 1))
                        if j >= 2:
                            act.wait_ge(o_ready.sem, o_ready.at(j - 1))
                        act.copy(pT[:, j % 2, :], k.ps[:, 2 + j % 2, :]).then_inc(pt_ready.sem, pt_ready.up())
                for b in range(RB):
                    act.wait_ge(y_ready.sem, y_ready.at(b + 1))
                    act.copy(yT[:, b, :], k.ps[:, b, :]).then_inc(y_copied.sem, y_copied.up())
        k.stage_end()


def stage_rwkv_in(k, hT, rT, kT, vT, lora):
    with ExitStack() as st:
        keep = k.sb("keep", [P, 15], st)
        with k.block() as block:
            kept, scaled, shifted = k.sig("kept"), k.sig("scaled"), k.sig("shifted")

            def dst(g):
                return [rT, kT, vT][g // 4][:, g % 4, :] if g < 12 else lora[:, g - 12, :]

            @block.tensor
            def _(pe):
                for g in range(15):
                    w, landed, full = k.take()
                    pe.wait_ge(landed, full)
                    if g >= 8:
                        pe.wait_ge(shifted.sem, shifted.at(2 * (g - 7)))
                    for kt in range(DB):
                        mm = pe.matmul(k.ps[:, g % 8, :], w[:, kt * P:(kt + 1) * P], hT[:, kt, :],
                                       start=kt == 0, stop=kt == DB - 1)
                    mm.then_inc(k.used, 1)

            @block.scalar
            def _(act):
                act.wait_ge(kept.sem, kept.at(2))
                for g in range(15):
                    act.wait_ge(k.used, k.after(g))
                    act.activation(dst(g), k.ps[:, g % 8, :], ACT.Copy, scale=keep[:, g:g + 1]).then_inc(scaled.sem, scaled.up())

            @block.vector
            def _(dve):
                a, b = COL["mu_prev"][0], COL["mu_next"][0]
                dve.tensor_scalar(keep[:, :], k.cols[:, a:a + 15], -1.0, 1.0, ALU.mult, ALU.add).then_inc(kept.sem, kept.up())
                dve.wait_ge(kept.sem, kept.last)
                dve.tensor_tensor(keep[:, :], keep[:, :], k.cols[:, b:b + 15], ALU.subtract).then_inc(kept.sem, kept.up())
                for g in range(15):
                    dve.wait_ge(scaled.sem, scaled.at(g + 1))
                    src, out = k.ps[:, g % 8, :], dst(g)
                    dve.scalar_tensor_tensor(out[:, 1:], src[:, :T - 1], k.col("mu_prev", g),
                                             out[:, 1:], ALU.mult, ALU.add).then_inc(shifted.sem, shifted.up())
                    dve.wait_ge(shifted.sem, shifted.last)
                    dve.scalar_tensor_tensor(out[:, :T - 1], src[:, 1:], k.col("mu_next", g),
                                             out[:, :T - 1], ALU.mult, ALU.add).then_inc(shifted.sem, shifted.up())

            @block.sync
            def _(sp):
                k.stream(sp, 15)
        k.stage_end()


def solve_pe(k, pe, n, n_half, w, start):
    masked, y_ready, y_copied, z_ready, updated = (k.sig(x) for x in SOLVE)
    for lv in range(LEVELS):
        for h2 in range(2):
            i = 2 * lv + h2
            pe.wait_ge(masked.sem, masked.at(i + 1))
            pe.wait_ge(updated.sem, updated.at(2 * i if i >= 2 else 2))
            for j in range(n_half):
                h = h2 * n_half + j
                mm = pe.matmul(k.ps[:, h2, j * P:(j + 1) * P], w["M"][:, h, :], w["X"][:, h, :], start=True, stop=True)
            mm.then_inc(y_ready.sem, y_ready.up())
        for h2 in range(2):
            i = 2 * lv + h2
            pe.wait_ge(y_copied.sem, y_copied.at(i + 1))
            for j in range(n_half):
                h = h2 * n_half + j
                pe.matmul(k.ps[:, 2 + h2, j * P:(j + 1) * P], w["XT"][:, h, :], w["Y"][:, h, :], start=True, stop=True)
                mm = pe.matmul(k.ps[:, 4 + h2, j * P:(j + 1) * P], w["Y"][:, h, :], w["XT"][:, h, :], start=True, stop=True)
            mm.then_inc(z_ready.sem, z_ready.up())


SOLVE = ("solve_masked", "solve_y_ready", "solve_y_copied", "solve_z_ready", "solve_updated")


def solve_act(k, act, n_half, w):
    masked, y_ready, y_copied, z_ready, updated = (k.sig(x) for x in SOLVE)
    for i in range(2 * LEVELS):
        h2 = i % 2
        act.wait_ge(y_ready.sem, y_ready.at(i + 1))
        act.copy(w["Y"][:, h2 * n_half:(h2 + 1) * n_half, :],
                 k.ps[:, h2, 0:n_half * P].rearrange("p (h t) -> p h t", t=P)).then_inc(y_copied.sem, y_copied.up())


def solve_pool(k, pool, n_half, w, lt, lower, ready):
    masked, y_ready, y_copied, z_ready, updated = (k.sig(x) for x in SOLVE)
    ready(pool)
    for i in range(2 * LEVELS):
        lv, h2 = divmod(i, 2)
        hs = slice(h2 * n_half, (h2 + 1) * n_half)
        if lv:
            pool.wait_ge(y_ready.sem, y_ready.at(i - 1))
        a = CONST["level_b" if lower else "level_f"][0] + lv * P
        m = k.const[:, a:a + P].unsqueeze(1).broadcast_to([P, n_half, P])
        pool.tensor_tensor(w["M"][:, hs, :], lt(h2), m, ALU.mult).then_inc(masked.sem, masked.up())


def solve_dve(k, dve, n_half, w):
    masked, y_ready, y_copied, z_ready, updated = (k.sig(x) for x in SOLVE)
    one = k.c("ident").unsqueeze(1).broadcast_to([P, 2 * n_half, P])
    dve.tensor_copy(w["X"][:, :, :], one).then_inc(updated.sem, updated.up())
    dve.tensor_copy(w["XT"][:, :, :], one).then_inc(updated.sem, updated.up())
    for i in range(2 * LEVELS):
        h2 = i % 2
        hs = slice(h2 * n_half, (h2 + 1) * n_half)
        dve.wait_ge(z_ready.sem, z_ready.at(i + 1))
        if i < 2:
            dve.wait_ge(updated.sem, updated.at(2))
        else:
            dve.wait_ge(updated.sem, updated.at(2 * i))
        for bank, x in ((2 + h2, "X"), (4 + h2, "XT")):
            z = k.ps[:, bank, 0:n_half * P].rearrange("p (h t) -> p h t", t=P)
            dve.tensor_tensor(w[x][:, hs, :], w[x][:, hs, :], z, ALU.subtract).then_inc(updated.sem, updated.up())


def stage_solve(k, w, n, lt, lower):
    with k.block() as block:
        @block.gpsimd
        def _(pool):
            solve_pool(k, pool, n // 2, w, lt, lower, lambda e: None)

        @block.tensor
        def _(pe):
            solve_pe(k, pe, n, n // 2, w, None)

        @block.scalar
        def _(act):
            solve_act(k, act, n // 2, w)

        @block.vector
        def _(dve):
            solve_dve(k, dve, n // 2, w)
    k.stage_end()


def stage_rwkv(k, rT, kT, vT, lora, yT):
    with ExitStack() as st:
        up = k.sb("w_up", [P, 3, RW], st)
        hsum = k.sb("hsum", [P, RB * 8], st)
        row = k.sb("rw_rows", [P, 4, RW], st)
        kkT = k.sb("kkT", [P, RB, T], st)
        aT = k.sb("aT", [P, RB, T], st)
        vt = k.sb("rw_v", [P, NT, RW], st)
        y = yT
        bonus = k.sb("bonus", [P, NT, RH], st)
        lora_prep(k, st, up, hsum, row, lora, rT, kT, vT, kkT, vt)
        M = k.sb("rw_state", [P, RB, HD], st)
        refs = k.sb("rw_refs", [P, 4, RB], st)
        for d, order in (("f", range(NT)), ("b", range(NT - 1, -1, -1))):
            stage_rwkv_dir(k, d, aT, lora, up, kT, rT, kkT, bonus, hsum)
            for n, c in enumerate(order):
                with ExitStack() as s2:
                    A = k.sb("rw_A", [P, RH, 4 * P], s2)
                    kr = k.sb("rw_kr", [P, RB, 2, P], s2)
                    tok = k.sb("rw_tok", [P, 2, RW], s2)
                    with ExitStack() as s3:
                        stage_rwkv_chunk(k, d, c, row, up, lora, aT, kT, rT, kkT, A, kr, tok, refs, s3)
                    w = {x: k.sb("rw_" + x, [P, RH, P], s2) for x in ("X", "XT")}
                    with ExitStack() as s3:
                        w["M"] = k.sb("rw_M", [P, RH, P], s3)
                        w["Y"] = k.sb("rw_Y", [P, RH, P], s3)
                        stage_solve(k, w, RH, lambda h2: A[:, 4 * h2:4 * h2 + 4, 0:P], d == "b")
                    with ExitStack() as s3:
                        stage_rwkv_step(k, d, c, n, A, w["XT"], kr, tok, vt, M, refs, y, s3)
        stage_rwkv_out(k, y, vt, bonus, row, up, lora, yT, st)


def lora_prep(k, st, up, hsum, row, lora, rT, kT, vT, kkT, vt):
    with ExitStack() as s2:
        sq = k.sb("kk_sq", [P, RB, T], s2)
        with k.block() as block:
            got, squashed, scaled = k.sig("load"), k.sig("squashed"), k.sig("scaled")
            squared, summed, rooted, chain = (k.sig(x) for x in ("squared", "summed", "rooted", "chain_v"))
            v_ready, v_copied = k.sig("v_ready"), k.sig("v_copied")

            @block.sync
            def _(sp):
                for i, name in enumerate(("w_up", "a_up", "g_up")):
                    a, n = MAT[name]
                    sp.dma_start(up[:, i, :], k.dram["mats"][:, a:a + n]).then_inc(got.sem, got.up(16))
                a, n = MAT["hsum"]
                sp.dma_start(hsum[:, :], k.dram["mats"][:, a:a + n]).then_inc(got.sem, got.up(16))
                for i, name in enumerate(("w0_f", "w0_b", "lnx_g", "lnx_b")):
                    a, n = ROW[name]
                    sp.dma_start(row[:, i, :], k.dram["rows"][:, a:a + n].broadcast_to([P, n])).then_inc(got.sem, got.up(16))
                sp.wait_ge(got.sem, got.at(128))

            @block.scalar
            def _(act):
                act.activation(lora[:, 0, :], lora[:, 0, :], ACT.Tanh).then_inc(squashed.sem, squashed.up())
                act.activation(lora[:, 2, :], lora[:, 2, :], ACT.Sigmoid).then_inc(squashed.sem, squashed.up())
                for b in range(RB):
                    act.wait_ge(scaled.sem, scaled.at(b + 1))
                    act.activation(sq[:, b, :], kkT[:, b, :], ACT.Square).then_inc(squared.sem, squared.up())
                for b in range(RB):
                    act.wait_ge(summed.sem, summed.at(b + 1))
                    act.activation(sq[:, b, :], k.ps[:, b, :], ACT.Sqrt, bias=L2_EPS).then_inc(rooted.sem, rooted.up())

            @block.tensor
            def _(pe):
                for b in range(RB):
                    pe.wait_ge(squared.sem, squared.at(b + 1))
                    pe.matmul(k.ps[:, b, :], k.c("ones64"), sq[:, b, :], start=True, stop=True).then_inc(summed.sem, summed.up())
                for t in range(NT):
                    for b in range(RB):
                        mm = pe.transpose(k.ps[:, 4 + t, b * P:(b + 1) * P], vT[:, b, t * P:(t + 1) * P], k.c("ident"))
                    mm.then_inc(v_ready.sem, v_ready.up())

            @block.vector
            def _(dve):
                for b in range(RB):
                    dve.tensor_scalar(kkT[:, b, :], kT[:, b, :], k.col("k_k", b), None, ALU.mult).then_inc(scaled.sem, scaled.up())
                for b in range(RB):
                    dve.wait_ge(rooted.sem, rooted.at(b + 1))
                    dve.reciprocal(sq[:, b, :], sq[:, b, :]).then_inc(chain.sem, chain.up())
                    dve.wait_ge(chain.sem, chain.last)
                    dve.tensor_tensor(kkT[:, b, :], kkT[:, b, :], sq[:, b, :], ALU.mult).then_inc(chain.sem, chain.up())
                for t in range(NT):
                    dve.wait_ge(v_ready.sem, v_ready.at(t + 1))
                    dve.tensor_copy(vt[:, t, :], k.ps[:, 4 + t, :]).then_inc(v_copied.sem, v_copied.up())
        k.stage_end()


def stage_rwkv_dir(k, d, aT, lora, up, kT, rT, kkT, bonus, hsum):
    p0 = 0 if d == "f" else HD
    with ExitStack() as st:
        prod = k.sb("bonus_prod", [P, RB, T], st)
        ka1 = k.sb("ka1", [P, RB], st)
        with k.block() as block:
            a_ready, a_done, chain = k.sig("a_ready"), k.sig("a_done"), k.sig("chain_v")
            prod_done, b_ready, b_done = k.sig("prod_done"), k.sig("bonus_ready"), k.sig("bonus_done")

            @block.tensor
            def _(pe):
                for b in range(RB):
                    pe.matmul(k.ps[:, b, :], up[p0:p0 + HD, 1, b * P:(b + 1) * P],
                              lora[p0:p0 + HD, 1, :], start=True, stop=True).then_inc(a_ready.sem, a_ready.up())
                pe.wait_ge(prod_done.sem, prod_done.at(RB))
                for t in range(NT):
                    for b in range(RB):
                        mm = pe.matmul(k.ps[:, 4, t * 8:t * 8 + 8], prod[:, b, t * P:(t + 1) * P],
                                       hsum[:, b * 8:b * 8 + 8], start=b == 0, stop=b == RB - 1)
                mm.then_inc(b_ready.sem, b_ready.up())

            @block.scalar
            def _(act):
                for b in range(RB):
                    act.wait_ge(a_ready.sem, a_ready.at(b + 1))
                    act.activation(aT[:, b, :], k.ps[:, b, :], ACT.Sigmoid, bias=k.col("a0_" + d, b)).then_inc(a_done.sem, a_done.up())

            @block.vector
            def _(dve):
                a = COL["k_a"][0]
                dve.tensor_scalar(ka1[:, :], k.cols[:, a:a + RB], -1.0, 1.0, ALU.mult, ALU.add).then_inc(chain.sem, chain.up())
                dve.wait_ge(chain.sem, chain.last)
                for b in range(RB):
                    dve.wait_ge(a_done.sem, a_done.at(b + 1))
                    dve.tensor_scalar(prod[:, b, :], aT[:, b, :], k.col("k_a", b), ka1[:, b:b + 1],
                                      ALU.mult, ALU.add).then_inc(chain.sem, chain.up())
                    dve.wait_ge(chain.sem, chain.last)
                    dve.tensor_tensor(prod[:, b, :], prod[:, b, :], kT[:, b, :], ALU.mult).then_inc(chain.sem, chain.up())
                    dve.wait_ge(chain.sem, chain.last)
                    dve.scalar_tensor_tensor(prod[:, b, :], prod[:, b, :], k.col("r_k", b),
                                             rT[:, b, :], ALU.mult, ALU.mult).then_inc(prod_done.sem, prod_done.up())
                dve.wait_ge(b_ready.sem, b_ready.at(1))
                flat = bonus[:, :, :].rearrange("p t h -> p (t h)")
                if d == "f":
                    dve.tensor_copy(flat, k.ps[:, 4, 0:NT * 8]).then_inc(b_done.sem, b_done.up())
                else:
                    dve.tensor_tensor(flat, flat, k.ps[:, 4, 0:NT * 8], ALU.add).then_inc(b_done.sem, b_done.up())
        k.stage_end()


def stage_rwkv_chunk(k, d, c, row, up, lora, aT, kT, rT, kkT, A, kr, tok, refs, st):
    p0 = 0 if d == "f" else HD
    mid, end = (P // 2, P - 1) if d == "f" else (P // 2 - 1, 0)
    ts = slice(c * P, (c + 1) * P)
    lw = k.sb("rw_lw", [P, RW], st)
    ex = k.sb("rw_ex", [P, RB, 2, P], st)
    ek = k.sb("rw_ek", [P, RB, P], st)
    bk = k.sb("rw_bk", [P, 2, RB, P], st)
    kd = k.sb("rw_kd", [P, RB, P], st)
    ka1 = k.sb("rw_ka1", [P, RB], st)
    with k.block() as block:
        w_ready, w_biased, w_done = k.sig("w_ready"), k.sig("w_biased"), k.sig("w_done")
        g_ready, ref_done, ex_done, ends_done = k.sig("g_ready"), k.sig("ref_done"), k.sig("ex_done"), k.sig("ends_done")
        chain, kr_done, bk_done = k.sig("chain_v"), k.sig("kr_done"), k.sig("bk_done")
        s_ready, s_masked, t_ready, t_copied = k.sig("s_ready"), k.sig("s_masked"), k.sig("t_ready"), k.sig("t_copied")
        kd_done = k.sig("kd_done")

        @block.tensor
        def _(pe):
            pe.matmul(k.ps[:, 0, :], lora[p0:p0 + HD, 0, ts], up[p0:p0 + HD, 0, :], start=True, stop=True).then_inc(w_ready.sem, w_ready.up())
            pe.wait_ge(w_done.sem, w_done.at(1))
            for b in range(RB):
                mm = pe.matmul(k.ps[:, 1 + b // 2, (b % 2) * 256:(b % 2) * 256 + 256], lw[:, b * P:(b + 1) * P],
                               k.c("tri_" + d), start=True, stop=True)
            mm.then_inc(g_ready.sem, g_ready.up())
            pe.wait_ge(bk_done.sem, bk_done.at(2))
            for i in range(2):
                for b in range(RB):
                    mm = pe.transpose(k.ps[:, 3 + i, b * P:(b + 1) * P], bk[:, i, b, :], k.c("ident"))
                mm.then_inc(t_ready.sem, t_ready.up())
            pe.wait_ge(kr_done.sem, kr_done.at(2))
            for h in range(RH):
                a, b = HD * (h % 2), h // 2
                if h >= 3:
                    pe.wait_ge(s_masked.sem, s_masked.at(h - 2))
                bank = 5 + h % 3
                for i in range(2):
                    mm = pe.matmul(k.ps[:, bank, i * 256:(i + 1) * 256], bk[a:a + HD, i, b, :],
                                   kr[a:a + HD, b, :, :].rearrange("p i t -> p (i t)"), start=True, stop=True)
                mm.then_inc(s_ready.sem, s_ready.up())

        @block.scalar
        def _(act):
            act.wait_ge(w_biased.sem, w_biased.at(1))
            act.activation(lw[:, :], lw[:, :], ACT.Sigmoid).then_inc(w_done.sem, w_done.up())
            act.wait_ge(ref_done.sem, ref_done.at(2))
            for b in range(RB):
                g = k.ps[:, 1 + b // 2, (b % 2) * 256:(b % 2) * 256 + 256]
                act.activation(ex[:, b, :, :].rearrange("p i t -> p (i t)"), g, ACT.Exp,
                               scale=-DECAY, bias=refs[:, 1, b:b + 1]).then_inc(ex_done.sem, ex_done.up())
                act.activation(ek[:, b, :], g[:, 0:P], ACT.Exp, scale=DECAY, bias=refs[:, 0, b:b + 1]).then_inc(ex_done.sem, ex_done.up())
            act.activation(refs[:, 2, :], refs[:, 0, :], ACT.Exp).then_inc(ends_done.sem, ends_done.up())
            for i in range(2):
                act.wait_ge(t_ready.sem, t_ready.at(i + 1))
                act.copy(tok[:, i, :], k.ps[:, 3 + i, :]).then_inc(t_copied.sem, t_copied.up())

        @block.vector
        def _(dve):
            dve.wait_ge(w_ready.sem, w_ready.at(1))
            dve.tensor_tensor(lw[:, :], k.ps[:, 0, :], row[:, 0 if d == "f" else 1, :], ALU.add).then_inc(w_biased.sem, w_biased.up())
            dve.wait_ge(g_ready.sem, g_ready.at(1))
            gm = k.ps[:, 1:3, :].rearrange("p a (b n) -> p a b n", n=256)
            for i, f in ((0, -DECAY), (1, DECAY)):
                dve.tensor_scalar(refs[:, i, :].rearrange("p (a b) -> p a b", a=2), gm[:, :, :, mid],
                                  f, None, ALU.mult).then_inc(ref_done.sem, ref_done.up())
            dve.wait_ge(ex_done.sem, ex_done.at(2 * RB))
            dve.tensor_copy(refs[:, 3, :], ex[:, :, 0, end]).then_inc(ends_done.sem, ends_done.up())
            dve.tensor_tensor(kr[:, :, 0, :], kkT[:, :, ts], ex[:, :, 1, :], ALU.mult).then_inc(kr_done.sem, kr_done.up())
            dve.tensor_tensor(kr[:, :, 1, :], rT[:, :, ts], ex[:, :, 0, :], ALU.mult).then_inc(kr_done.sem, kr_done.up())
            for h in range(RH):
                dve.wait_ge(s_ready.sem, s_ready.at(h + 1))
                dve.tensor_tensor(A[:, h, :], k.ps[:, 5 + h % 3, :], k.c("attn_" + d), ALU.mult).then_inc(s_masked.sem, s_masked.up())

        @block.gpsimd
        def _(pool):
            a0 = COL["k_a"][0]
            pool.tensor_scalar(ka1[:, :], k.cols[:, a0:a0 + RB], -1.0, 1.0, ALU.mult, ALU.add).then_inc(kd_done.sem, kd_done.up())
            pool.wait_ge(kd_done.sem, kd_done.last)
            for b in range(RB):
                pool.tensor_scalar(kd[:, b, :], aT[:, b, ts], k.col("k_a", b), ka1[:, b:b + 1], ALU.mult, ALU.add).then_inc(kd_done.sem, kd_done.up())
            pool.wait_ge(kd_done.sem, kd_done.at(1 + RB))
            pool.tensor_tensor(kd[:, :, :], kd[:, :, :], kT[:, :, ts], ALU.mult).then_inc(kd_done.sem, kd_done.up())
            pool.wait_ge(kd_done.sem, kd_done.last)
            pool.tensor_tensor(bk[:, 0, :, :], kkT[:, :, ts], aT[:, :, ts], ALU.mult).then_inc(kd_done.sem, kd_done.up())
            pool.wait_ge(kd_done.sem, kd_done.last)
            pool.wait_ge(ex_done.sem, ex_done.at(2 * RB))
            pool.tensor_tensor(bk[:, 0, :, :], bk[:, 0, :, :], ek[:, :, :], ALU.mult).then_inc(bk_done.sem, bk_done.up())
            pool.tensor_tensor(bk[:, 1, :, :], kd[:, :, :], ek[:, :, :], ALU.mult).then_inc(bk_done.sem, bk_done.up())
    k.stage_end()


def stage_rwkv_step(k, d, c, n, A, XT, kr, tok, vt, M, refs, y, st):
    w_sb = k.sb("rw_w", [P, 2, RB, HD], st)
    u_sb = k.sb("rw_u", [P, RW], st)
    Ms = k.sb("rw_Ms", [P, RB, HD], st)
    with k.block() as block:
        scaled, w_ready, w_done, u_ready, u_done = (k.sig(x) for x in ("state_scaled", "w_ready", "w_done", "u_ready", "u_done"))
        y_ready, y_done, m_ready, m_done = (k.sig(x) for x in ("y_ready", "y_done", "m_ready", "m_done"))

        @block.tensor
        def _(pe):
            pe.wait_ge(scaled.sem, scaled.at(1))
            for h in range(RH):
                a, b = HD * (h % 2), h // 2
                out = k.ps[:, h % 2, b * HD:(b + 1) * HD]
                pe.matmul(out, kr[a:a + HD, b, 0, :], Ms[a:a + HD, b, :], start=True, stop=False)
                mm = pe.matmul(out, A[:, h, 2 * P:3 * P], vt[:, c, h * HD:(h + 1) * HD], start=False, stop=True)
            mm.then_inc(w_ready.sem, w_ready.up())
            pe.wait_ge(w_done.sem, w_done.at(1))
            for h in range(RH):
                hs = slice(h * HD, (h + 1) * HD)
                mm = pe.matmul(k.ps[:, 2, hs], XT[:, h, :], w_sb[:, h % 2, h // 2, :], start=True, stop=True)
            mm.then_inc(u_ready.sem, u_ready.up())
            pe.wait_ge(u_done.sem, u_done.at(1))
            for h in range(RH):
                a, b = HD * (h % 2), h // 2
                hs = slice(h * HD, (h + 1) * HD)
                pe.matmul(k.ps[a:a + HD, 3, b * HD:(b + 1) * HD], tok[:, 0, hs], u_sb[:, hs], start=True, stop=False)
                mm = pe.matmul(k.ps[a:a + HD, 3, b * HD:(b + 1) * HD], tok[:, 1, hs], vt[:, c, hs], start=False, stop=True)
            mm.then_inc(m_ready.sem, m_ready.up())
            for h in range(RH):
                a, b = HD * (h % 2), h // 2
                hs = slice(h * HD, (h + 1) * HD)
                out = k.ps[:, 4 + h % 2, b * HD:(b + 1) * HD]
                pe.matmul(out, kr[a:a + HD, b, 1, :], Ms[a:a + HD, b, :], start=True, stop=False)
                pe.matmul(out, A[:, h, P:2 * P], u_sb[:, hs], start=False, stop=False)
                mm = pe.matmul(out, A[:, h, 3 * P:4 * P], vt[:, c, hs], start=False, stop=True)
            mm.then_inc(y_ready.sem, y_ready.up())

        def halves(bank):
            return k.ps[:, bank:bank + 2, 0:RB * HD].rearrange("p i (b v) -> p i b v", v=HD)

        @block.scalar
        def _(act):
            act.wait_ge(w_ready.sem, w_ready.at(1))
            act.activation(w_sb[:, :, :, :], halves(0), ACT.Copy, scale=-1.0).then_inc(w_done.sem, w_done.up())
            act.wait_ge(u_ready.sem, u_ready.at(1))
            act.copy(u_sb[:, :], k.ps[:, 2, :]).then_inc(u_done.sem, u_done.up())

        @block.vector
        def _(dve):
            if n == 0:
                dve.memset(Ms[:, :, :], 0.0).then_inc(scaled.sem, scaled.up())
            else:
                dve.tensor_tensor(Ms[:, :, :], M[:, :, :],
                                  refs[:, 2, :].unsqueeze(2).broadcast_to([P, RB, HD]), ALU.mult).then_inc(scaled.sem, scaled.up())
            dve.wait_ge(m_ready.sem, m_ready.at(1))
            dve.wait_ge(scaled.sem, scaled.at(1))
            dve.tensor_tensor(M[:, :, :], Ms[:, :, :],
                              k.ps[:, 3, 0:RB * HD].rearrange("p (b v) -> p b v", v=HD), ALU.add).then_inc(m_done.sem, m_done.up())
            dve.wait_ge(m_done.sem, m_done.last)
            dve.tensor_tensor(M[:, :, :], M[:, :, :],
                              refs[:, 3, :].unsqueeze(2).broadcast_to([P, RB, HD]), ALU.mult).then_inc(m_done.sem, m_done.up())
            dve.wait_ge(y_ready.sem, y_ready.at(1))
            out = y[:, c, :].rearrange("p (b i v) -> p i b v", i=2, v=HD)
            if d == "f":
                dve.tensor_copy(out, halves(4)).then_inc(y_done.sem, y_done.up())
            else:
                dve.tensor_tensor(out, out, halves(4), ALU.add).then_inc(y_done.sem, y_done.up())
    k.stage_end()


def stage_rwkv_out(k, y, vt, bonus, row, up, lora, yT, st):
    sq = k.sb("gn_sq", [P, NT, RW], st)
    stat = k.sb("gn_stat", [P, 2, NT * RH], st)
    with k.block() as block:
        g_ready, chain, rooted, y_done, y_ready, y_copied, var_done = (
            k.sig(x) for x in ("g_ready", "chain_v", "rooted", "y_done", "y_ready", "y_copied", "var_done"))

        @block.tensor
        def _(pe):
            for t in range(NT):
                pe.matmul(k.ps[:, t, :], lora[:, 2, t * P:(t + 1) * P], up[:, 2, :], start=True, stop=True).then_inc(g_ready.sem, g_ready.up())
            pe.wait_ge(y_done.sem, y_done.at(NT))
            for b in range(RB):
                for t in range(NT):
                    mm = pe.transpose(k.ps[:, 4 + b, t * P:(t + 1) * P], y[:, t, b * P:(b + 1) * P], k.c("ident"))
                mm.then_inc(y_ready.sem, y_ready.up())

        @block.scalar
        def _(act):
            act.wait_ge(var_done.sem, var_done.at(1))
            act.activation(stat[:, 1, :], stat[:, 1, :], ACT.Sqrt, scale=1.0 / HD, bias=GN_EPS).then_inc(rooted.sem, rooted.up())
            act.wait_ge(y_ready.sem, y_ready.at(RB))
            for b in range(RB):
                act.copy(yT[:, b, :], k.ps[:, 4 + b, :]).then_inc(y_copied.sem, y_copied.up())

        @block.vector
        def _(dve):
            yh = y[:, :, :].rearrange("p t (h c) -> p (t h) c", c=HD)
            vh = vt[:, :, :].rearrange("p t (h c) -> p (t h) c", c=HD)
            sh = sq[:, :, :].rearrange("p t (h c) -> p (t h) c", c=HD)

            def wide(x):
                return x.unsqueeze(2).broadcast_to([P, NT * RH, HD])
            dve.tensor_reduce(stat[:, 0, :], yh, AX.X, ALU.add).then_inc(chain.sem, chain.up())
            dve.wait_ge(chain.sem, chain.last)
            dve.tensor_scalar(stat[:, 0, :], stat[:, 0, :], 1.0 / HD, None, ALU.mult).then_inc(chain.sem, chain.up())
            dve.wait_ge(chain.sem, chain.last)
            dve.tensor_tensor(yh, yh, wide(stat[:, 0, :]), ALU.subtract).then_inc(chain.sem, chain.up())
            dve.wait_ge(chain.sem, chain.last)
            dve.tensor_tensor(sh, yh, yh, ALU.mult).then_inc(chain.sem, chain.up())
            dve.wait_ge(chain.sem, chain.last)
            dve.tensor_reduce(stat[:, 1, :], sh, AX.X, ALU.add).then_inc(var_done.sem, var_done.up())
            dve.wait_ge(rooted.sem, rooted.at(1))
            dve.reciprocal(stat[:, 1, :], stat[:, 1, :]).then_inc(chain.sem, chain.up())
            dve.wait_ge(chain.sem, chain.last)
            dve.tensor_tensor(yh, yh, wide(stat[:, 1, :]), ALU.mult).then_inc(chain.sem, chain.up())
            dve.wait_ge(chain.sem, chain.last)
            dve.tensor_tensor(y[:, :, :], y[:, :, :], row[:, 2:3, :].broadcast_to([P, NT, RW]), ALU.mult).then_inc(chain.sem, chain.up())
            dve.wait_ge(chain.sem, chain.last)
            dve.tensor_tensor(y[:, :, :], y[:, :, :], row[:, 3:4, :].broadcast_to([P, NT, RW]), ALU.add).then_inc(chain.sem, chain.up())
            dve.wait_ge(chain.sem, chain.last)
            dve.tensor_tensor(sh, vh, wide(bonus[:, :, :].rearrange("p t h -> p (t h)")), ALU.mult).then_inc(chain.sem, chain.up())
            dve.wait_ge(chain.sem, chain.last)
            dve.tensor_tensor(y[:, :, :], y[:, :, :], sq[:, :, :], ALU.add).then_inc(chain.sem, chain.up())
            dve.wait_ge(chain.sem, chain.last)
            dve.wait_ge(g_ready.sem, g_ready.at(NT))
            for t in range(NT):
                dve.tensor_tensor(y[:, t, :], y[:, t, :], k.ps[:, t, :], ALU.mult).then_inc(y_done.sem, y_done.up())
    k.stage_end()


def stage_merge(k, hT, yaT, ybT):
    with ExitStack() as st:
        g = k.sb("gates", [P, 16, T], st)
        mix = k.sb("mix", [P, DB, T], st)
        with k.block() as block:
            g_done, m_done, h_done, x_done = k.sig("g_done"), k.sig("mix_done"), k.sig("half_done"), k.sig("x_done")

            @block.tensor
            def _(pe):
                for i in range(16):
                    w, landed, full = k.take()
                    pe.wait_ge(landed, full)
                    if i >= 8:
                        pe.wait_ge(g_done.sem, g_done.at(i - 7))
                    for kt in range(DB):
                        mm = pe.matmul(k.ps[:, i % 8, :], w[:, kt * P:(kt + 1) * P], hT[:, kt, :],
                                       start=kt == 0, stop=kt == DB - 1)
                    mm.then_inc(k.used, 1)
                for i in range(8):
                    w, landed, full = k.take()
                    pe.wait_ge(landed, full)
                    pe.wait_ge(g_done.sem, g_done.at(10 + 2 * (i % 4)))
                    if i >= 4:
                        pe.wait_ge(m_done.sem, m_done.at(i - 3))
                    for j, src in ((0, yaT), (1, ybT)):
                        for kt in range(4):
                            mm = pe.matmul(k.ps[:, 2 * (i % 4) + j, :], w[:, (4 * j + kt) * P:(4 * j + kt + 1) * P],
                                           src[:, kt, :], start=kt == 0, stop=kt == 3)
                    mm.then_inc(k.used, 1)
                pe.wait_ge(m_done.sem, m_done.at(8))
                for i in range(8):
                    w, landed, full = k.take()
                    pe.wait_ge(landed, full)
                    for kt in range(DB):
                        mm = pe.matmul(k.ps[:, i, :], w[:, kt * P:(kt + 1) * P], mix[:, kt, :],
                                       start=kt == 0, stop=kt == DB - 1)
                    mm.then_inc(k.used, 1)

            @block.scalar
            def _(act):
                for i in range(16):
                    act.wait_ge(k.used, k.after(i))
                    act.activation(g[:, i, :], k.ps[:, i % 8, :], ACT.Sigmoid, bias=k.col("b_gate", i)).then_inc(g_done.sem, g_done.up())

            @block.vector
            def _(dve):
                for i in range(8):
                    dve.wait_ge(k.used, k.after(16 + i))
                    for j in range(2):
                        dve.tensor_tensor(g[:, 8 * j + i, :], g[:, 8 * j + i, :], k.ps[:, 2 * (i % 4) + j, :], ALU.mult).then_inc(h_done.sem, h_done.up())
                    dve.wait_ge(h_done.sem, h_done.at(2 * i + 2))
                    dve.tensor_tensor(mix[:, i, :], g[:, i, :], g[:, 8 + i, :], ALU.add).then_inc(m_done.sem, m_done.up())
                for i in range(8):
                    dve.wait_ge(k.used, k.after(24 + i))
                    dve.tensor_tensor(k.xT[:, i, :], k.xT[:, i, :], k.ps[:, i, :], ALU.add).then_inc(x_done.sem, x_done.up())

            @block.sync
            def _(sp):
                k.stream(sp, 32)
        k.stage_end()


def stage_router(k, hT, comb):
    with ExitStack() as st:
        wr = k.sb("w_router", [P, DB, 36], st)
        br = k.sb("b_router", [P, 36], st)
        gidx = k.sb("gidx", [P, 12], st)
        lg = k.sb("logits", [P, NT, 36], st)
        small = k.sb("router_small", [P, 8, NT], st)
        g4 = k.sb("router_g4", [P, 3, NT, 4], st)
        e8 = k.sb("router_e8", [P, 5, NT, 8], st)
        pick = k.sb("router_pick", [P, NT * 4, 8], st)
        with k.block() as block:
            got, l_ready, chain = k.sig("load"), k.sig("l_ready"), k.sig("chain_v")
            diff_done, exp_done = k.sig("diff_done"), k.sig("exp_done")

            @block.sync
            def _(sp):
                for dst, src in ((wr[:, :, :].rearrange("p b n -> p (b n)"), ("mats", MAT["router"])),
                                 (gidx[:, :], ("mats", MAT["gidx"]))):
                    a, n = src[1]
                    sp.dma_start(dst, k.dram["mats"][:, a:a + n]).then_inc(got.sem, got.up(16))
                a, n = ROW["b_router"]
                sp.dma_start(br[:, :], k.dram["rows"][:, a:a + n].broadcast_to([P, n])).then_inc(got.sem, got.up(16))

            @block.tensor
            def _(pe):
                pe.wait_ge(got.sem, got.at(48))
                for t in range(NT):
                    for b in range(DB):
                        mm = pe.matmul(k.ps[:, 0, t * 36:(t + 1) * 36], hT[:, b, t * P:(t + 1) * P], wr[:, b, :],
                                       start=b == 0, stop=b == DB - 1)
                mm.then_inc(l_ready.sem, l_ready.up())

            @block.scalar
            def _(act):
                act.wait_ge(diff_done.sem, diff_done.at(1))
                act.activation(g4[:, 0, :, :], g4[:, 0, :, :], ACT.Exp).then_inc(exp_done.sem, exp_done.up())
                act.wait_ge(diff_done.sem, diff_done.at(2))
                act.activation(small[:, 4, :], small[:, 4, :], ACT.Exp).then_inc(exp_done.sem, exp_done.up())

            @block.vector
            def _(dve):
                def go(ins):
                    ins.then_inc(chain.sem, chain.up())
                    dve.wait_ge(chain.sem, chain.last)

                def over(x, n):
                    return x.unsqueeze(2).broadcast_to([P, NT, n])

                def one_hot(out, values, top, order, n):
                    go(dve.tensor_tensor(out, values, over(top, n), ALU.is_equal))
                    go(dve.tensor_tensor(out, out, order.unsqueeze(1).broadcast_to([P, NT, n]), ALU.mult))
                    go(dve.tensor_reduce(small[:, 7, :], out, AX.X, ALU.max))
                    go(dve.tensor_tensor(out, out, over(small[:, 7, :], n), ALU.is_equal))

                dve.wait_ge(got.sem, got.at(48))
                dve.wait_ge(l_ready.sem, l_ready.at(1))
                go(dve.tensor_tensor(lg[:, :, :], k.ps[:, 0, 0:NT * 36].rearrange("p (t n) -> p t n", n=36),
                                     br[:, :].unsqueeze(1).broadcast_to([P, NT, 36]), ALU.add))
                gmax, gsum, v1, v2, ediff, w1, w2 = (small[:, i, :] for i in range(7))
                go(dve.tensor_reduce(gmax, lg[:, :, 0:4], AX.X, ALU.max))
                dve.tensor_tensor(g4[:, 0, :, :], lg[:, :, 0:4], over(gmax, 4), ALU.subtract).then_inc(diff_done.sem, diff_done.up())
                one_hot(g4[:, 1, :, :], lg[:, :, 0:4], gmax, gidx[:, 0:4], 4)
                dve.wait_ge(exp_done.sem, exp_done.at(1))
                go(dve.tensor_reduce(gsum, g4[:, 0, :, :], AX.X, ALU.add))
                go(dve.reciprocal(gsum, gsum))
                go(dve.tensor_copy(pick[:, :, :].rearrange("p (t g) e -> p t (g e)", g=4), lg[:, :, 4:36]))
                hot = g4[:, 1, :, :].rearrange("p t g -> p (t g)").unsqueeze(2).broadcast_to([P, NT * 4, 8])
                go(dve.tensor_tensor(pick[:, :, :], pick[:, :, :], hot, ALU.mult))
                go(dve.tensor_reduce(e8[:, 0, :, :], pick[:, :, :].rearrange("p (t g) e -> p t e g", g=4), AX.X, ALU.add))
                go(dve.tensor_reduce(v1, e8[:, 0, :, :], AX.X, ALU.max))
                one_hot(e8[:, 1, :, :], e8[:, 0, :, :], v1, gidx[:, 4:12], 8)
                go(dve.tensor_scalar(e8[:, 3, :, :], e8[:, 1, :, :], -1e30, None, ALU.mult))
                go(dve.tensor_tensor(e8[:, 3, :, :], e8[:, 3, :, :], e8[:, 0, :, :], ALU.add))
                go(dve.tensor_reduce(v2, e8[:, 3, :, :], AX.X, ALU.max))
                one_hot(e8[:, 2, :, :], e8[:, 3, :, :], v2, gidx[:, 4:12], 8)
                dve.tensor_tensor(ediff, v2, v1, ALU.subtract).then_inc(diff_done.sem, diff_done.up())
                dve.wait_ge(exp_done.sem, exp_done.at(2))
                go(dve.tensor_scalar(w1, ediff, 1.0, None, ALU.add))
                go(dve.reciprocal(w1, w1))
                go(dve.tensor_tensor(w1, w1, gsum, ALU.mult))
                go(dve.tensor_tensor(w2, w1, ediff, ALU.mult))
                go(dve.tensor_tensor(e8[:, 1, :, :], e8[:, 1, :, :], over(w1, 8), ALU.mult))
                go(dve.tensor_tensor(e8[:, 2, :, :], e8[:, 2, :, :], over(w2, 8), ALU.mult))
                go(dve.tensor_tensor(e8[:, 1, :, :], e8[:, 1, :, :], e8[:, 2, :, :], ALU.add))
                for g in range(4):
                    go(dve.tensor_tensor(comb[:, :, g * 8:(g + 1) * 8], e8[:, 1, :, :], over(g4[:, 1, :, g], 8), ALU.mult))
        k.stage_end()


def stage_moe(k, hT, comb, acc):
    PER, UPE = 4, 6
    U = PER * UPE
    ROUNDS = NE // PER
    first = STREAM["moe"][0]
    with ExitStack() as st:
        sg = k.sb("moe_silu", [P, 2, T], st)
        heT = k.sb("moe_he", [P, 2, 2, T], st)
        with k.block() as block:
            silu_done, he_done, d_ready, acc_done = (k.sig(x) for x in ("silu_done", "he_done", "down_ready", "acc_done"))
            assert k.taken == first and first > 2 * UPE

            def rounds(eng, body, *signals):
                before = [s.n for s in signals]
                with eng.Fori(0, ROUNDS) as r:
                    for j in range(PER):
                        body(r, j)
                for s, n in zip(signals, before):
                    s.n += (ROUNDS - 1) * (s.n - n)

            @block.sync
            def _(sp):
                with sp.Fori(0, ROUNDS) as r:
                    for i in range(U):
                        sp.wait_ge(k.used, r * U + (first + i + 1))
                        s = (first + i) % RING
                        sp.dma_start(k.ring[:, s, :], k.dram["stream"][bass.ds(r * U + (first + RING + i), 1)]
                                     .rearrange("a p n -> (a p) n")).then_inc(k.landed[s], 16)
                k.issued += ROUNDS * U

            @block.tensor
            def _(pe):
                def landed(r, u):
                    return r * (16 * U // RING) + 16 * (u // RING + 1)

                def expert(r, j):
                    for g in range(4):
                        u = first + j * UPE + g
                        pe.wait_ge(k.landed[u % RING], landed(r, u))
                        w = k.ring[:, u % RING, :]
                        pe.wait_ge(he_done.sem, r * (2 * PER) + (he_done.base + 2 * j + g // 2 + 1))
                        for kt in range(DB):
                            mm = pe.matmul(k.ps[:, g, :], w[:, kt * P:(kt + 1) * P], hT[:, kt, :],
                                           start=kt == 0, stop=kt == DB - 1)
                        mm.then_inc(k.used, 1)
                    for half in range(2):
                        for f in range(2):
                            u = first + j * UPE + 4 + f
                            pe.wait_ge(k.landed[u % RING], landed(r, u))
                            w = k.ring[:, u % RING, :]
                            pe.wait_ge(he_done.sem, r * (2 * PER) + (he_done.base + 2 * j + f + 3))
                            for i in range(4):
                                t, n = divmod(4 * half + i, 2)
                                if f == 0:
                                    pe.wait_ge(acc_done.sem, r * (8 * PER) + (acc_done.base + 8 * j + 4 * half + i + 5))
                                mm = pe.matmul(k.ps[:, 4 + i, :], heT[:, j % 2, f, t * P:(t + 1) * P],
                                               w[:, n * 512:(n + 1) * 512], start=f == 0, stop=f == 1)
                                if f == 1 and (half, i) != (1, 3):
                                    mm.then_inc(d_ready.sem, d_ready.up())
                                elif (half, i) == (1, 3):
                                    mm.then_inc(k.used, 1)

                rounds(pe, expert, d_ready)
                k.taken += ROUNDS * U

            @block.scalar
            def _(act):
                def expert(r, j):
                    for f in range(2):
                        act.wait_ge(k.used, r * U + (first + j * UPE + 2 * f + 1))
                        act.wait_ge(he_done.sem, r * (2 * PER) + (he_done.base + 2 * j + f + 1))
                        act.activation(sg[:, f, :], k.ps[:, 2 * f, :], ACT.Silu).then_inc(silu_done.sem, silu_done.up())
                rounds(act, expert, silu_done)

            @block.vector
            def _(dve):
                for f in range(2):
                    dve.memset(heT[:, :, f, :], 0.0).then_inc(he_done.sem, he_done.up())
                for i in range(8):
                    t, n = divmod(i, 2)
                    dve.memset(acc[:, t, n * 512:(n + 1) * 512], 0.0).then_inc(acc_done.sem, acc_done.up())

                def expert(r, j):
                    dve.wait_ge(k.used, r * U + (first + (j - 1) * UPE))
                    dve.wait_ge(he_done.sem, r * (2 * PER) + (he_done.base + 2 * j + 2))
                    for f in range(2):
                        dve.wait_ge(silu_done.sem, r * (2 * PER) + (silu_done.base + 2 * j + f + 1))
                        dve.wait_ge(k.used, r * U + (first + j * UPE + 2 * f + 2))
                        dve.tensor_tensor(heT[:, j % 2, f, :], sg[:, f, :], k.ps[:, 2 * f + 1, :], ALU.mult).then_inc(he_done.sem, he_done.up())
                    for i in range(8):
                        t, n = divmod(i, 2)
                        if i < 7:
                            dve.wait_ge(d_ready.sem, r * (7 * PER) + (d_ready.base + 7 * j + i + 1))
                        else:
                            dve.wait_ge(k.used, r * U + (first + (j + 1) * UPE))
                        a = acc[:, t, n * 512:(n + 1) * 512]
                        dve.wait_ge(acc_done.sem, r * (8 * PER) + (acc_done.base + 8 * j + i + 1))
                        dve.scalar_tensor_tensor(a, k.ps[:, 4 + i % 4, :], comb[:, t, bass.ds(r * PER + j, 1)],
                                                 a, ALU.mult, ALU.add).then_inc(acc_done.sem, acc_done.up())
                rounds(dve, expert, he_done, acc_done)
        k.stage_end()


def stage_add_tokens(k, acc):
    with k.block() as block:
        ready, done = k.sig("y_ready"), k.sig("x_done")

        @block.tensor
        def _(pe):
            for b in range(DB):
                for t in range(NT):
                    mm = pe.transpose(k.ps[:, b, t * P:(t + 1) * P], acc[:, t, b * P:(b + 1) * P], k.c("ident"))
                mm.then_inc(ready.sem, ready.up())

        @block.vector
        def _(dve):
            for b in range(DB):
                dve.wait_ge(ready.sem, ready.at(b + 1))
                dve.tensor_tensor(k.xT[:, b, :], k.xT[:, b, :], k.ps[:, b, :], ALU.add).then_inc(done.sem, done.up())
    k.stage_end()


def stage_mod(k, mod, gain):
    with ExitStack() as st:
        cs = k.sb("silu_c", [P, DB, 2], st)
        with k.block() as block:
            c_done, m_done, chain = k.sig("silu_done"), k.sig("mod_done"), k.sig("chain_v")

            @block.scalar
            def _(act):
                a = COL["cc"][0]
                act.activation(cs[:, :, :].rearrange("p b i -> p (b i)"), k.cols[:, a:a + 16], ACT.Silu).then_inc(c_done.sem, c_done.up())

            @block.tensor
            def _(pe):
                pe.wait_ge(c_done.sem, c_done.at(1))
                for m in range(48):
                    w, landed, full = k.take()
                    pe.wait_ge(landed, full)
                    for kt in range(DB):
                        mm = pe.matmul(k.ps[:, 0, 2 * m:2 * m + 2], w[:, kt * P:(kt + 1) * P], cs[:, kt, :],
                                       start=kt == 0, stop=kt == DB - 1)
                    mm.then_inc(k.used, 1)

            @block.vector
            def _(dve):
                dve.wait_ge(k.used, k.after(47))
                a = COL["b_mod"][0]
                dve.tensor_tensor(mod[:, :, :], k.ps[:, 0, 0:96].rearrange("p (m i) -> p m i", i=2),
                                  k.cols[:, a:a + 48].unsqueeze(2).broadcast_to([P, 48, 2]), ALU.add).then_inc(chain.sem, chain.up())
                dve.wait_ge(chain.sem, chain.last)
                for i, (name, scale, which) in enumerate((("norm1_g_2", 8, 0), ("norm1_g_2", 8, 1), ("norm2_g_2", 32, 0))):
                    g = COL[name][0]
                    dve.tensor_scalar(gain[:, i, :], mod[:, scale:scale + 8, which], 1.0, None, ALU.add).then_inc(chain.sem, chain.up())
                    dve.wait_ge(chain.sem, chain.last)
                    dve.tensor_tensor(gain[:, i, :], gain[:, i, :], k.cols[:, g:g + 8], ALU.mult).then_inc(m_done.sem, m_done.up())

            @block.sync
            def _(sp):
                k.stream(sp, 48)
        k.stage_end()


def stage_load_ctx(k, hT2):
    with k.block() as block:
        @block.sync
        def _(sp):
            got = k.sig("load")
            sp.dma_start(hT2[:, :, 0:CTX], k.dram["ctxT"]).then_inc(got.sem, got.up(16))
            sp.wait_ge(got.sem, got.at(16))
    k.stage_end()


def stage_project(k, hT2, items):
    N = len(items)
    with k.block() as block:
        done, done2, ready = k.sig("proj_done"), k.sig("proj_ctx_done"), k.sig("proj_ready")
        ctx_before = np.cumsum([0] + [it[1] is not None for it in items]).tolist()

        @block.tensor
        def _(pe):
            for i, (lat, cx, _, _) in enumerate(items):
                w, landed, full = k.take()
                pe.wait_ge(landed, full)
                if i >= 4:
                    pe.wait_ge(done.sem, done.at(i - 3))
                    if ctx_before[i - 3]:
                        pe.wait_ge(done2.sem, done2.at(ctx_before[i - 3]))
                for kt in range(DB):
                    mm = pe.matmul(k.ps[:, 2 * (i % 4), :], w[:, kt * P:(kt + 1) * P], hT2[:, kt, CTX:T2],
                                   start=kt == 0, stop=kt == DB - 1)
                if cx is not None:
                    for kt in range(DB):
                        mm = pe.matmul(k.ps[:, 2 * (i % 4) + 1, 0:CTX], w[:, kt * P:(kt + 1) * P], hT2[:, kt, 0:CTX],
                                       start=kt == 0, stop=kt == DB - 1)
                mm.then_inc(k.used, 1)

        @block.scalar
        def _(act):
            for i, (lat, cx, func, factor) in enumerate(items):
                act.wait_ge(k.used, k.after(i))
                act.activation(lat, k.ps[:, 2 * (i % 4), :], func, scale=factor).then_inc(done.sem, done.up())

        @block.vector
        def _(dve):
            for i, (lat, cx, func, factor) in enumerate(items):
                if cx is not None:
                    dve.wait_ge(k.used, k.after(i))
                    dve.tensor_scalar(cx, k.ps[:, 2 * (i % 4) + 1, 0:CTX], factor, None, ALU.mult).then_inc(done2.sem, done2.up())

        @block.sync
        def _(sp):
            k.stream(sp, N)
    k.stage_end()


def stage_conv(k, blocks, taps, bias=None):
    with k.block() as block:
        first, chain = k.sig("conv_first"), k.sig("chain_v")
        K = taps.count

        @block.scalar
        def _(act):
            for dst, src, seg, i, np_ in blocks:
                act.activation(dst, src, ACT.Identity, scale=taps(i, K // 2)[0:np_, :],
                               bias=bias(i)[0:np_, :] if bias else 0.0).then_inc(first.sem, first.up())

        @block.vector
        def _(dve):
            for n, (dst, src, seg, i, np_) in enumerate(blocks):
                dve.wait_ge(first.sem, first.at(n + 1))
                d = dst.rearrange("p (s x) -> p s x", s=seg)
                s = src.rearrange("p (s x) -> p s x", s=seg)
                L = s.shape[2]
                for j in range(K):
                    o = j - K // 2
                    if o:
                        lo, hi = max(0, -o), L - max(0, o)
                        dve.scalar_tensor_tensor(d[:, :, lo:hi], s[:, :, lo + o:hi + o],
                                                 taps(i, j)[0:np_, :], d[:, :, lo:hi], ALU.mult, ALU.add).then_inc(chain.sem, chain.up())
                        dve.wait_ge(chain.sem, chain.last)
    k.stage_end()


class Taps:
    def __init__(self, k, name, count):
        self.k, self.name, self.count = k, name, count

    def __call__(self, i, j):
        return self.k.col(self.name, i * self.count + j)


def stage_hyena(k, u, yT):
    TWO_PI = 2 * float(np.pi)
    HI = 6.28125
    LO = TWO_PI - HI
    ROUND = 1.5 * 2 ** 23
    with ExitStack() as st:
        dft = k.sb("hy_dft", [P, NT, 2 * NFREQ], st)
        H = k.sb("hy_H", [P, 8, 512], st)
        with ExitStack() as s2:
            win = k.sb("hy_win", [P, NT, 512], s2)
            w1, w2 = k.sb("hy_w1", [P, 64], s2), k.sb("hy_w2", [P, 64], s2)
            w3 = k.sb("hy_w3", [P, 1024], s2)
            z = k.sb("hy_z", [P, T], s2)
            h = k.sb("hy_h", [P, 3, T], s2)
            taps = k.sb("hy_taps", [P, 2, 512], s2)
            both = k.sb("hy_both", [P, NT, 2, 512], s2)
            with k.block() as block:
                got, chain = k.sig("load"), k.sig("chain_v")
                a_ready, a_done, sin_done = k.sig("a_ready"), k.sig("a_done"), k.sig("sin_done")
                t_ready, t_done, both_done = k.sig("t_ready"), k.sig("taps_done"), k.sig("both_done")
                H_ready, H_done = k.sig("H_ready"), [k.sig("H_done_a"), k.sig("H_done_v")]

                @block.sync
                def _(sp):
                    for dst, name in ((w1, "hy_w1"), (w2, "hy_w2"), (w3, "hy_w3")):
                        a, n = MAT[name]
                        sp.dma_start(dst[:, :], k.dram["mats"][:, a:a + n]).then_inc(got.sem, got.up(16))
                    sp.dma_start(z[:, :], k.dram["hy_z"]).then_inc(got.sem, got.up(16))
                    sp.dma_start(win[:, :, :], k.dram["hy_win"]).then_inc(got.sem, got.up(16))
                    sp.dma_start(dft[:, :, :], k.dram["dft"]).then_inc(got.sem, got.up(16))

                @block.tensor
                def _(pe):
                    pe.wait_ge(got.sem, got.at(96))
                    pe.matmul(k.ps[0:64, 0, :], w1[0:33, :], z[0:33, :], start=True, stop=True).then_inc(a_ready.sem, a_ready.up())
                    pe.wait_ge(sin_done.sem, sin_done.at(1))
                    pe.matmul(k.ps[0:64, 0, :], w2[0:64, :], h[0:64, 0, :], start=True, stop=True).then_inc(a_ready.sem, a_ready.up())
                    pe.wait_ge(sin_done.sem, sin_done.at(2))
                    for t in range(NT):
                        if t >= 2:
                            pe.wait_ge(t_done.sem, t_done.at(2 * (t - 1)))
                        for o in range(2):
                            mm = pe.matmul(k.ps[:, 2 * (t % 2) + o, :], h[0:64, 0, t * P:(t + 1) * P],
                                           w3[0:64, o * 512:(o + 1) * 512], start=True, stop=True)
                        mm.then_inc(t_ready.sem, t_ready.up())
                    pe.wait_ge(both_done.sem, both_done.at(4 * NT))
                    for f in range(8):
                        for t in range(NT):
                            mm = pe.matmul(k.ps[:, f, :], dft[:, t, f * P:(f + 1) * P], both[:, t, f // 4, :],
                                           start=t == 0, stop=t == NT - 1)
                        mm.then_inc(H_ready.sem, H_ready.up())

                @block.scalar
                def _(act):
                    for i in range(2):
                        act.wait_ge(a_done.sem, a_done.at(i + 1))
                        act.activation(h[0:64, 0, :], h[0:64, 1, :], ACT.Sin).then_inc(sin_done.sem, sin_done.up())
                    for f in range(0, 8, 2):
                        act.wait_ge(H_ready.sem, H_ready.at(f + 1))
                        act.copy(H[:, f, :], k.ps[:, f, :]).then_inc(H_done[0].sem, H_done[0].up())

                @block.vector
                def _(dve):
                    dve.wait_ge(got.sem, got.at(96))
                    for i, (b, f) in enumerate((("hy_b1", "hy_f1"), ("hy_b2", "hy_f2"))):
                        dve.wait_ge(a_ready.sem, a_ready.at(i + 1))
                        arg, n = h[0:64, 1, :], h[0:64, 2, :]
                        dve.tensor_scalar(arg, k.ps[0:64, 0, :], k.col(b, 0, 0, 64), k.col(f, 0, 0, 64),
                                          ALU.add, ALU.mult).then_inc(chain.sem, chain.up())
                        dve.wait_ge(chain.sem, chain.last)
                        dve.tensor_scalar(n, arg, 1 / TWO_PI, ROUND, ALU.mult, ALU.add).then_inc(chain.sem, chain.up())
                        dve.wait_ge(chain.sem, chain.last)
                        dve.tensor_scalar(n, n, ROUND, None, ALU.subtract).then_inc(chain.sem, chain.up())
                        dve.wait_ge(chain.sem, chain.last)
                        dve.scalar_tensor_tensor(arg, n, -HI, arg, ALU.mult, ALU.add).then_inc(chain.sem, chain.up())
                        dve.wait_ge(chain.sem, chain.last)
                        dve.scalar_tensor_tensor(arg, n, -LO, arg, ALU.mult, ALU.add).then_inc(chain.sem, chain.up())
                        dve.wait_ge(chain.sem, chain.last)
                        lim = float(np.float32(3.1415925))
                        dve.tensor_scalar(arg, arg, lim, -lim, ALU.min, ALU.max).then_inc(a_done.sem, a_done.up())
                    for t in range(NT):
                        dve.wait_ge(t_ready.sem, t_ready.at(t + 1))
                        if t:
                            dve.wait_ge(both_done.sem, both_done.at(4 * t))
                        for o in range(2):
                            dve.tensor_tensor(taps[:, o, :], k.ps[:, 2 * (t % 2) + o, :], win[:, t, :], ALU.mult).then_inc(t_done.sem, t_done.up())
                        dve.wait_ge(t_done.sem, t_done.at(2 * t + 2))
                        for o in range(2):
                            for i, op in ((0, ALU.add), (1, ALU.subtract)):
                                dve.tensor_tensor(both[:, t, i, o * HY_C:(o + 1) * HY_C], taps[:, o, 0:HY_C],
                                                  taps[:, o, HY_C:512], op).then_inc(both_done.sem, both_done.up())
                    for f in range(1, 8, 2):
                        dve.wait_ge(H_ready.sem, H_ready.at(f + 1))
                        dve.tensor_copy(H[:, f, :], k.ps[:, f, :]).then_inc(H_done[1].sem, H_done[1].up())
            k.stage_end()
        with ExitStack() as s2:
            inv = k.sb("hy_inv", [P, 8, T], s2)
            vt = k.sb("hy_vt", [P, NT, HY_C], s2)
            Y = k.sb("hy_Y", [P, 8, HY_C], s2)
            tmp = k.sb("hy_tmp", [P, 2, 4, HY_C], s2)
            for o in range(2):
                src = u[:, 0:2, :]
                gate, dst = (u[:, 2:4, :], src) if o == 0 else (u[:, 4:6, :], yT)
                with k.block() as block:
                    got, chain = k.sig("load"), k.sig("chain_v")
                    v_ready, v_done, V_ready = k.sig("v_ready"), k.sig("v_copied"), k.sig("V_ready")
                    Y_done, c_ready, y_done = k.sig("Y_done"), k.sig("c_ready"), k.sig("y_done")

                    @block.sync
                    def _(sp):
                        if o == 0:
                            sp.dma_start(inv[:, :, :], k.dram["inv"]).then_inc(got.sem, got.up(16))

                    @block.tensor
                    def _(pe):
                        for b in range(2):
                            for t in range(NT):
                                mm = pe.transpose(k.ps[:, b, t * P:(t + 1) * P], src[:, b, t * P:(t + 1) * P], k.c("ident"))
                            mm.then_inc(v_ready.sem, v_ready.up())
                        pe.wait_ge(v_done.sem, v_done.at(2))
                        for f in range(4):
                            for i in range(2):
                                for t in range(NT):
                                    mm = pe.matmul(k.ps[:, 2 + f, i * HY_C:(i + 1) * HY_C],
                                                   dft[:, t, (4 * i + f) * P:(4 * i + f + 1) * P], vt[:, t, :],
                                                   start=t == 0, stop=t == NT - 1)
                        mm.then_inc(V_ready.sem, V_ready.up())
                        if o == 0:
                            pe.wait_ge(got.sem, got.at(16))
                        pe.wait_ge(Y_done.sem, Y_done.at(2))
                        for b in range(2):
                            for f in range(8):
                                mm = pe.matmul(k.ps[:, b, :], Y[:, f, b * P:(b + 1) * P], inv[:, f, :],
                                               start=f == 0, stop=f == 7)
                            mm.then_inc(c_ready.sem, c_ready.up())

                    @block.scalar
                    def _(act):
                        for b in range(2):
                            act.wait_ge(v_ready.sem, v_ready.at(b + 1))
                            act.copy(vt[:, :, b * P:(b + 1) * P], k.ps[:, b, :].rearrange("p (t c) -> p t c", c=P)).then_inc(v_done.sem, v_done.up())

                    @block.vector
                    def _(dve):
                        dve.wait_ge(V_ready.sem, V_ready.at(1))
                        re, im = (k.ps[:, 2:6, i * HY_C:(i + 1) * HY_C] for i in range(2))
                        Hr, Hi = (H[:, 4 * i:4 * i + 4, o * HY_C:(o + 1) * HY_C] for i in range(2))
                        dve.tensor_tensor(tmp[:, 0, :, :], re, Hr, ALU.mult).then_inc(chain.sem, chain.up())
                        dve.tensor_tensor(tmp[:, 1, :, :], im, Hi, ALU.mult).then_inc(chain.sem, chain.up())
                        dve.wait_ge(chain.sem, chain.last)
                        dve.tensor_tensor(Y[:, 0:4, :], tmp[:, 0, :, :], tmp[:, 1, :, :], ALU.subtract).then_inc(Y_done.sem, Y_done.up())
                        dve.wait_ge(Y_done.sem, Y_done.at(1))
                        dve.tensor_tensor(tmp[:, 0, :, :], re, Hi, ALU.mult).then_inc(chain.sem, chain.up())
                        dve.tensor_tensor(tmp[:, 1, :, :], im, Hr, ALU.mult).then_inc(chain.sem, chain.up())
                        dve.wait_ge(chain.sem, chain.last)
                        dve.tensor_tensor(Y[:, 4:8, :], tmp[:, 0, :, :], tmp[:, 1, :, :], ALU.add).then_inc(Y_done.sem, Y_done.up())
                        for b in range(2):
                            dve.wait_ge(c_ready.sem, c_ready.at(b + 1))
                            dve.scalar_tensor_tensor(dst[:, b, :], src[:, b, :], k.col("hy_d", 2 * o + b),
                                                     k.ps[:, b, :], ALU.mult, ALU.add).then_inc(chain.sem, chain.up())
                            dve.wait_ge(chain.sem, chain.last)
                            dve.tensor_tensor(dst[:, b, :], dst[:, b, :], gate[:, b, :], ALU.mult).then_inc(y_done.sem, y_done.up())
                k.stage_end()


def stage_to_tokens(k, jobs):
    with k.block() as block:
        ready, done = k.sig("y_ready"), [k.sig("turned_act"), k.sig("turned_dve")]

        @block.tensor
        def _(pe):
            for i, (dst, src, *at) in enumerate(jobs):
                if i >= 8:
                    pe.wait_ge(done[i % 2].sem, done[i % 2].at((i - 8) // 2 + 1))
                n, p0 = src.shape[0], at[0] if at else 0
                pe.transpose(k.ps[:, i % 8, 0:n], src, k.c("ident")[p0:p0 + n, p0:p0 + n]).then_inc(ready.sem, ready.up())

        @block.scalar
        def _(act):
            for i in range(0, len(jobs), 2):
                act.wait_ge(ready.sem, ready.at(i + 1))
                dst = jobs[i][0]
                act.copy(dst, k.ps[:, i % 8, 0:dst.shape[1]]).then_inc(done[0].sem, done[0].up())

        @block.vector
        def _(dve):
            for i in range(1, len(jobs), 2):
                dve.wait_ge(ready.sem, ready.at(i + 1))
                dst = jobs[i][0]
                dve.tensor_copy(dst, k.ps[:, i % 8, 0:dst.shape[1]]).then_inc(done[1].sem, done[1].up())
    k.stage_end()


def stage_gates(k, aT, gt, la, ldec, beta):
    with ExitStack() as st:
        a2 = k.sb("gla_a2", [P, 256], st)
        row = k.sb("gate_rows", [P, 512 + 16], st)
        sp1 = k.sb("softplus", [P, NT2, 256], st)
        d1 = k.sb("gdn_pre", [P, 3, NT2, 8], st)
        with k.block() as block:
            got, chain = k.sig("load"), k.sig("chain_v")
            x_ready, x_done, e_done, d_done = k.sig("x_ready"), k.sig("x_done"), k.sig("e_done"), k.sig("d_done")

            @block.sync
            def _(sp):
                a, n = MAT["gla_a2"]
                sp.dma_start(a2[:, :], k.dram["mats"][:, a:a + n]).then_inc(got.sem, got.up(16))
                a, n = ROW["gla_b"]
                sp.dma_start(row[:, 0:512], k.dram["rows"][:, a:a + n].broadcast_to([P, n])).then_inc(got.sem, got.up(16))
                a, n = ROW["a_log"][0], 16
                sp.dma_start(row[:, 512:528], k.dram["rows"][:, a:a + n].broadcast_to([P, n])).then_inc(got.sem, got.up(16))

            @block.tensor
            def _(pe):
                pe.wait_ge(got.sem, got.at(48))
                for d in range(2):
                    p0 = 32 * d
                    for t in range(NT2):
                        mm = pe.matmul(k.ps[:, 4 * d + t // 2, (t % 2) * 256:(t % 2) * 256 + 256],
                                       aT[p0:p0 + 16, t * P:(t + 1) * P], a2[p0:p0 + 16, :], start=True, stop=True)
                    mm.then_inc(x_ready.sem, x_ready.up())

            @block.vector
            def _(dve):
                dve.wait_ge(got.sem, got.at(48))
                x, ax, sp_ = d1[:, 0, :, :], d1[:, 1, :, :], d1[:, 2, :, :]
                dve.tensor_tensor(x, gt[:, :, 0:8], row[:, 520:528].unsqueeze(1).broadcast_to([P, NT2, 8]), ALU.add).then_inc(chain.sem, chain.up())
                dve.wait_ge(chain.sem, chain.last)
                dve.tensor_scalar(ax, x, -1.0, None, ALU.mult).then_inc(chain.sem, chain.up())
                dve.wait_ge(chain.sem, chain.last)
                dve.tensor_tensor(ax, ax, x, ALU.min).then_inc(d_done.sem, d_done.up())
                for d in range(2):
                    dve.wait_ge(x_ready.sem, x_ready.at(d + 1))
                    bias = row[:, d * 256:(d + 1) * 256]
                    l = la[:, d, :, :]
                    for a in range(3):
                        xx = k.ps[:, 4 * d + a, :].rearrange("p (t n) -> p t n", n=256)
                        dve.tensor_tensor(l[:, 2 * a:2 * a + 2, :], xx,
                                          bias.unsqueeze(1).broadcast_to([P, 2, 256]), ALU.add).then_inc(x_done.sem, x_done.up())
                    dve.wait_ge(x_done.sem, x_done.at(3 * d + 3))
                    dve.wait_ge(e_done.sem, e_done.at(3 * d + 3))
                    dve.tensor_scalar(l, l, 0.0, None, ALU.min).then_inc(chain.sem, chain.up())
                    dve.wait_ge(chain.sem, chain.last)
                    dve.tensor_tensor(l, l, sp1[:, :, :], ALU.subtract).then_inc(chain.sem, chain.up())
                    dve.wait_ge(chain.sem, chain.last)
                dve.wait_ge(e_done.sem, e_done.at(10))
                dve.tensor_scalar(x, x, 0.0, None, ALU.max).then_inc(chain.sem, chain.up())
                dve.wait_ge(chain.sem, chain.last)
                dve.tensor_tensor(x, x, sp_, ALU.add).then_inc(chain.sem, chain.up())
                dve.wait_ge(chain.sem, chain.last)
                dve.scalar_tensor_tensor(ldec[:, :, :], x, -1.0, row[:, 512:520].unsqueeze(1).broadcast_to([P, NT2, 8]),
                                         ALU.mult, ALU.mult).then_inc(chain.sem, chain.up())
                dve.wait_ge(chain.sem, chain.last)

            @block.scalar
            def _(act):
                for d in range(2):
                    act.wait_ge(x_done.sem, x_done.at(3 * d + 3))
                    if d:
                        act.wait_ge(chain.sem, chain.at(4))
                    l = la[:, d, :, :]
                    for f, src, kw in ((ACT.Abs, l, {}), (ACT.Exp, sp1[:, :, :], {"scale": -1.0}),
                                       (ACT.Ln, sp1[:, :, :], {"bias": 1.0})):
                        act.activation(sp1[:, :, :], src, f, **kw).then_inc(e_done.sem, e_done.up())
                        act.wait_ge(e_done.sem, e_done.last)
                act.wait_ge(got.sem, got.at(48))
                act.wait_ge(d_done.sem, d_done.at(1))
                act.activation(d1[:, 2, :, :], d1[:, 1, :, :], ACT.Exp).then_inc(e_done.sem, e_done.up())
                act.wait_ge(e_done.sem, e_done.last)
                act.activation(d1[:, 2, :, :], d1[:, 2, :, :], ACT.Ln, bias=1.0).then_inc(e_done.sem, e_done.up())
                act.wait_ge(e_done.sem, e_done.last)
                act.activation(row[:, 512:520], row[:, 512:520], ACT.Exp).then_inc(e_done.sem, e_done.up())
                act.wait_ge(e_done.sem, e_done.last)
                act.activation(beta[:, :, :], gt[:, :, 8:16], ACT.Sigmoid).then_inc(e_done.sem, e_done.up())
                act.wait_ge(e_done.sem, e_done.last)
        k.stage_end()


def stage_gla_chunk(k, d, c, n, qT, kT, vt, la, S, y):
    mid, end = (P // 2, P - 1) if d == "f" else (P // 2 - 1, 0)
    lat = c >= 2
    di = 0 if d == "f" else 1
    H2 = GLA_H // 2
    V = GLA_DV
    with ExitStack() as st:
        refs = k.sb("gla_refs", [P, 4, H2], st)
        ex = k.sb("gla_ex", [P, 2, H2, P], st)
        qs = k.sb("gla_qs", [P, 2, H2, P], st)
        A = k.sb("gla_A", [P, 2, H2, P], st)
        tok = k.sb("gla_tok", [P, H2 * P], st)
        Ss = k.sb("gla_Ss", [P, H2, V], st)
        with k.block() as block:
            g_ready, ref_done, ex_done, chain, scaled = (k.sig(x) for x in ("g_ready", "ref_done", "ex_done", "chain_v", "state_scaled"))
            qk_done, s_ready, s_masked, t_ready, t_copied = (k.sig(x) for x in ("qk_done", "s_ready", "s_masked", "t_ready", "t_copied"))
            m_ready, y_ready, y_done = k.sig("m_ready"), k.sig("y_ready"), k.sig("y_done")

            @block.tensor
            def _(pe):
                for b in range(H2):
                    mm = pe.matmul(k.ps[:, 0, b * P:(b + 1) * P], la[:, di, c, b * P:(b + 1) * P],
                                   k.c("tri_" + d)[:, 0:P], start=True, stop=True)
                mm.then_inc(g_ready.sem, g_ready.up())
                pe.wait_ge(qk_done.sem, qk_done.at(2 if lat else 1))
                for b in range(H2):
                    mm = pe.transpose(k.ps[:, 1, b * P:(b + 1) * P], qs[:, 1, b, :], k.c("ident"))
                mm.then_inc(t_ready.sem, t_ready.up())
                if lat:
                    for h in range(GLA_H):
                        a, b = 64 * (h % 2), h // 2
                        mm = pe.matmul(k.ps[:, 2 + h % 2, b * P:(b + 1) * P], qs[a:a + 64, 1, b, :], qs[a:a + 64, 0, b, :],
                                       start=True, stop=True)
                    mm.then_inc(s_ready.sem, s_ready.up())
                pe.wait_ge(t_copied.sem, t_copied.at(1))
                for h in range(GLA_H):
                    a, b = 64 * (h % 2), h // 2
                    mm = pe.matmul(k.ps[a:a + 64, 6, b * V:(b + 1) * V], tok[:, h * 64:(h + 1) * 64],
                                   vt[:, c, h * V:(h + 1) * V], start=True, stop=True)
                mm.then_inc(m_ready.sem, m_ready.up())
                if lat:
                    pe.wait_ge(s_masked.sem, s_masked.at(1))
                    pe.wait_ge(scaled.sem, scaled.at(1))
                    for h in range(GLA_H):
                        a, b = 64 * (h % 2), h // 2
                        out = k.ps[:, 4 + h % 2, b * V:(b + 1) * V]
                        pe.matmul(out, qs[a:a + 64, 0, b, :], Ss[a:a + 64, b, :], start=True, stop=False)
                        mm = pe.matmul(out, A[:, h % 2, b, :], vt[:, c, h * V:(h + 1) * V], start=False, stop=True)
                    mm.then_inc(y_ready.sem, y_ready.up())

            @block.scalar
            def _(act):
                act.wait_ge(ref_done.sem, ref_done.at(2))
                g = k.ps[:, 0, 0:H2 * P].rearrange("p (b t) -> p b t", t=P)
                for b in range(H2):
                    act.activation(ex[:, 0, b, :], g[:, b, :], ACT.Exp, scale=1 / 16, bias=refs[:, 1, b:b + 1]).then_inc(ex_done.sem, ex_done.up())
                    act.activation(ex[:, 1, b, :], g[:, b, :], ACT.Exp, scale=-1 / 16, bias=refs[:, 0, b:b + 1]).then_inc(ex_done.sem, ex_done.up())
                act.activation(refs[:, 2, :], refs[:, 0, :], ACT.Exp).then_inc(ex_done.sem, ex_done.up())
                act.wait_ge(t_ready.sem, t_ready.at(1))
                act.copy(tok[:, :], k.ps[:, 1, 0:H2 * P]).then_inc(t_copied.sem, t_copied.up())

            @block.vector
            def _(dve):
                dve.wait_ge(g_ready.sem, g_ready.at(1))
                g = k.ps[:, 0, 0:H2 * P].rearrange("p (b t) -> p b t", t=P)
                for i, f in ((0, 1 / 16), (1, -1 / 16)):
                    dve.tensor_scalar(refs[:, i, :], g[:, :, mid], f, None, ALU.mult).then_inc(ref_done.sem, ref_done.up())
                dve.wait_ge(ex_done.sem, ex_done.at(2 * H2 + 1))
                ts = slice(c * P, (c + 1) * P)
                if lat:
                    dve.tensor_tensor(qs[:, 0, :, :], qT[:, :, (c - 2) * P:(c - 1) * P], ex[:, 0, :, :], ALU.mult).then_inc(qk_done.sem, qk_done.up())
                dve.tensor_tensor(qs[:, 1, :, :], kT[:, :, ts], ex[:, 1, :, :], ALU.mult).then_inc(qk_done.sem, qk_done.up())
                if n == 0:
                    dve.memset(Ss[:, :, :], 0.0).then_inc(scaled.sem, scaled.up())
                else:
                    dve.tensor_tensor(Ss[:, :, :], S[:, :, :], refs[:, 2, :].unsqueeze(2).broadcast_to([P, H2, V]), ALU.mult).then_inc(scaled.sem, scaled.up())
                if lat:
                    dve.wait_ge(s_ready.sem, s_ready.at(1))
                    m = k.c("attn_" + d)[:, P:2 * P].unsqueeze(1).broadcast_to([P, H2, P])
                    for i in range(2):
                        ins = dve.tensor_tensor(A[:, i, :, :], k.ps[:, 2 + i, 0:H2 * P].rearrange("p (b t) -> p b t", t=P), m, ALU.mult)
                    ins.then_inc(s_masked.sem, s_masked.up())
                dve.wait_ge(m_ready.sem, m_ready.at(1))
                dve.wait_ge(scaled.sem, scaled.at(1))
                dve.tensor_tensor(S[:, :, :], Ss[:, :, :], k.ps[:, 6, 0:H2 * V].rearrange("p (b v) -> p b v", v=V), ALU.add).then_inc(chain.sem, chain.up())
                dve.wait_ge(chain.sem, chain.last)
                dve.tensor_tensor(S[:, :, :], S[:, :, :], ex[:, 0, :, end].unsqueeze(2).broadcast_to([P, H2, V]), ALU.mult).then_inc(chain.sem, chain.up())
                if lat:
                    dve.wait_ge(y_ready.sem, y_ready.at(1))
                    out = y[:, c - 2, :].rearrange("p (b i v) -> p i b v", i=2, v=V)
                    got = k.ps[:, 4:6, 0:H2 * V].rearrange("p i (b v) -> p i b v", v=V)
                    if d == "f":
                        dve.tensor_copy(out, got).then_inc(y_done.sem, y_done.up())
                    else:
                        dve.tensor_tensor(out, out, got, ALU.add).then_inc(y_done.sem, y_done.up())
        k.stage_end()


def stage_head_norm(k, y, name, gateT, yT, b0):
    HV = 96
    N = NT * 4
    with ExitStack() as st:
        sq = k.sb("hn_sq", [P, NT, VW], st)
        stat = k.sb("hn_stat", [P, N], st)
        row = k.sb("hn_row", [P, HV], st)
        with k.block() as block:
            got, chain, v_done, rooted, y_done, y_ready, y_copied = (
                k.sig(x) for x in ("load", "chain_v", "var_done", "rooted", "y_done", "y_ready", "y_copied"))

            @block.sync
            def _(sp):
                a, n = ROW[name]
                sp.dma_start(row[:, :], k.dram["rows"][:, a:a + n].broadcast_to([P, n])).then_inc(got.sem, got.up(16))

            @block.tensor
            def _(pe):
                pe.wait_ge(y_done.sem, y_done.at(1))
                for b in range(3):
                    for t in range(NT):
                        mm = pe.transpose(k.ps[:, b, t * P:(t + 1) * P], y[:, t, b * P:(b + 1) * P], k.c("ident"))
                    mm.then_inc(y_ready.sem, y_ready.up())

            @block.scalar
            def _(act):
                act.wait_ge(v_done.sem, v_done.at(1))
                act.activation(stat[:, :], stat[:, :], ACT.Sqrt, scale=1.0 / HV, bias=RMS_EPS).then_inc(rooted.sem, rooted.up())

            @block.vector
            def _(dve):
                yh = y[:, :, :].rearrange("p t (h c) -> p (t h) c", c=HV)
                sh = sq[:, :, :].rearrange("p t (h c) -> p (t h) c", c=HV)
                dve.tensor_tensor(sh, yh, yh, ALU.mult).then_inc(chain.sem, chain.up())
                dve.wait_ge(chain.sem, chain.last)
                dve.tensor_reduce(stat[:, :], sh, AX.X, ALU.add).then_inc(v_done.sem, v_done.up())
                dve.wait_ge(rooted.sem, rooted.at(1))
                dve.reciprocal(stat[:, :], stat[:, :]).then_inc(chain.sem, chain.up())
                dve.wait_ge(chain.sem, chain.last)
                dve.tensor_tensor(yh, yh, stat[:, :].unsqueeze(2).broadcast_to([P, N, HV]), ALU.mult).then_inc(chain.sem, chain.up())
                dve.wait_ge(chain.sem, chain.last)
                dve.wait_ge(got.sem, got.at(16))
                dve.tensor_tensor(yh, yh, row[:, :].unsqueeze(1).broadcast_to([P, N, HV]), ALU.mult).then_inc(y_done.sem, y_done.up())
                for b in range(3):
                    dve.wait_ge(y_ready.sem, y_ready.at(b + 1))
                    dve.tensor_tensor(yT[:, b0 + b, :], k.ps[:, b, :], gateT[:, b, :], ALU.mult).then_inc(y_copied.sem, y_copied.up())
        k.stage_end()


def stage_l2(k, qT, kT):
    D6 = GDN_D
    with ExitStack() as st:
        sq = k.sb("l2_sq", [P, GDN_H, T2], st)
        with k.block() as block:
            silu_done, squared, summed, rooted, chain = (k.sig(x) for x in ("silu_done", "squared", "summed", "rooted", "chain_v"))
            @block.scalar
            def _(act):
                for i, (x, n, f) in enumerate(((kT, T2, 1.0), (qT, T, float(D6)))):
                    act.activation(x[0:D6, :, :], x[0:D6, :, :], ACT.Silu).then_inc(silu_done.sem, silu_done.up())
                    act.wait_ge(silu_done.sem, silu_done.last)
                    if i:
                        act.wait_ge(chain.sem, chain.at(2))
                    act.activation(sq[0:D6, :, 0:n], x[0:D6, :, :], ACT.Square).then_inc(squared.sem, squared.up())
                    act.wait_ge(summed.sem, summed.at(i + 1))
                    act.wait_ge(squared.sem, squared.at(i + 1))
                    act.activation(sq[0:D6, :, 0:512], k.ps[0:D6, 0:4, :], ACT.Sqrt, scale=f, bias=f * 1e-6).then_inc(rooted.sem, rooted.up())
                    if n > 512:
                        act.activation(sq[0:D6, :, 512:n], k.ps[0:D6, 4:8, 0:n - 512], ACT.Sqrt, scale=f, bias=f * 1e-6).then_inc(rooted.sem, rooted.up())

            @block.tensor
            def _(pe):
                for i, n in enumerate((T2, T)):
                    pe.wait_ge(squared.sem, squared.at(i + 1))
                    if i:
                        pe.wait_ge(rooted.sem, rooted.at(2))
                    for h in range(GDN_H):
                        mm = pe.matmul(k.ps[0:D6, h, :], k.c("ones")[0:D6, 0:D6], sq[0:D6, h, 0:512], start=True, stop=True)
                        if n > 512:
                            mm = pe.matmul(k.ps[0:D6, 4 + h, 0:n - 512], k.c("ones")[0:D6, 0:D6], sq[0:D6, h, 512:n],
                                           start=True, stop=True)
                    mm.then_inc(summed.sem, summed.up())

            @block.vector
            def _(dve):
                for i, (x, n) in enumerate(((kT, T2), (qT, T))):
                    dve.wait_ge(rooted.sem, rooted.at(2 + i))
                    dve.reciprocal(sq[0:D6, :, 0:n], sq[0:D6, :, 0:n]).then_inc(chain.sem, chain.up())
                    dve.wait_ge(chain.sem, chain.last)
                    dve.tensor_tensor(x[0:D6, :, :], x[0:D6, :, :], sq[0:D6, :, 0:n], ALU.mult).then_inc(chain.sem, chain.up())
                    dve.wait_ge(chain.sem, chain.last)
        k.stage_end()


def stage_gdn_chunk(k, d, c, qT, kT, ldec, beta, LT, AT, eg):
    di = 0 if d == "f" else 1
    lat = c >= 2
    hs = slice(4 * di, 4 * di + 4)
    with ExitStack() as st:
        dec = k.sb("gdn_dec", [P, GDN_H, P], st)
        decs = k.sb("gdn_decs", [P, GDN_H, P], st)
        with k.block() as block:
            g_ready, g_done, r_done, ex_done, chain = (k.sig(x) for x in ("g_ready", "ref_done", "row_done", "ex_done", "chain_v"))
            s_ready, s_masked = k.sig("s_ready"), k.sig("s_masked")

            @block.tensor
            def _(pe):
                tri = k.c("tri_" + d)[:, 0:P]
                pe.matmul(k.ps[:, 0, 0:4], tri, ldec[:, c, hs], start=True, stop=True)
                pe.matmul(k.ps[:, 0, 4:8], k.c("ones"), ldec[:, c, hs], start=True, stop=True)
                for h in range(GDN_H):
                    g = ldec[:, c, 4 * di + h:4 * di + h + 1].broadcast_to([P, P])
                    mm = pe.matmul(k.ps[:, 1, h * P:(h + 1) * P], g, tri, start=True, stop=True)
                mm.then_inc(g_ready.sem, g_ready.up())
                ts = slice(c * P, (c + 1) * P)
                for h in range(GDN_H):
                    kk = kT[0:GDN_D, h, ts]
                    mm = pe.matmul(k.ps[:, 2, h * P:(h + 1) * P], kk, kk, start=True, stop=True)
                    if lat:
                        mm = pe.matmul(k.ps[:, 3, h * P:(h + 1) * P], kk, qT[0:GDN_D, h, (c - 2) * P:(c - 1) * P],
                                       start=True, stop=True)
                mm.then_inc(s_ready.sem, s_ready.up())

            @block.scalar
            def _(act):
                act.wait_ge(g_done.sem, g_done.at(2))
                act.activation(eg[:, 1, :], eg[:, 1, :], ACT.Exp).then_inc(ex_done.sem, ex_done.up())
                act.activation(eg[:, 0, :], eg[:, 3, :], ACT.Exp).then_inc(ex_done.sem, ex_done.up())
                act.activation(eg[:, 2, :], k.ps[:, 0, 4:8], ACT.Exp).then_inc(ex_done.sem, ex_done.up())
                act.wait_ge(r_done.sem, r_done.at(GDN_H))
                act.activation(dec[:, :, :], dec[:, :, :], ACT.Exp).then_inc(ex_done.sem, ex_done.up())

            @block.vector
            def _(dve):
                dve.wait_ge(g_ready.sem, g_ready.at(1))
                dve.tensor_copy(eg[:, 3, :], k.ps[:, 0, 0:4]).then_inc(g_done.sem, g_done.up())
                dve.wait_ge(g_done.sem, g_done.last)
                dve.tensor_tensor(eg[:, 1, :], k.ps[:, 0, 4:8], eg[:, 3, :], ALU.subtract).then_inc(g_done.sem, g_done.up())
                for h in range(GDN_H):
                    dve.tensor_scalar(dec[:, h, :], k.ps[:, 1, h * P:(h + 1) * P], eg[:, 3, h:h + 1], 0.0,
                                      ALU.subtract, ALU.min).then_inc(r_done.sem, r_done.up())
                dve.wait_ge(ex_done.sem, ex_done.at(4))
                m = k.c("attn_" + d)
                dve.tensor_tensor(decs[:, :, :], dec[:, :, :], m[:, 0:P].unsqueeze(1).broadcast_to([P, GDN_H, P]), ALU.mult).then_inc(chain.sem, chain.up())
                dve.wait_ge(chain.sem, chain.last)
                dve.wait_ge(s_ready.sem, s_ready.at(1))
                for h in range(GDN_H):
                    dve.scalar_tensor_tensor(LT[:, h, :], k.ps[:, 2, h * P:(h + 1) * P],
                                             beta[:, c, 4 * di + h:4 * di + h + 1], decs[:, h, :], ALU.mult, ALU.mult).then_inc(s_masked.sem, s_masked.up())
                if lat:
                    dve.tensor_tensor(dec[:, :, :], dec[:, :, :], m[:, P:2 * P].unsqueeze(1).broadcast_to([P, GDN_H, P]), ALU.mult).then_inc(chain.sem, chain.up())
                    dve.wait_ge(chain.sem, chain.last)
                    dve.tensor_tensor(AT[:, :, :], k.ps[:, 3, :].rearrange("p (h t) -> p h t", t=P), dec[:, :, :], ALU.mult).then_inc(s_masked.sem, s_masked.up())
        k.stage_end()


def stage_gdn_step(k, d, c, n, qT, kT, kt, vt, XT, AT, eg, beta, S, y):
    di = 0 if d == "f" else 1
    lat = c >= 2
    V = GDN_D
    with ExitStack() as st:
        W = k.sb("gdn_W", [P, GDN_H, V], st)
        U = k.sb("gdn_U", [P, 2, GDN_H, V], st)
        o1 = k.sb("gdn_o", [P, GDN_H, V], st)
        with k.block() as block:
            z_done, w_ready, w_done, u_ready, u_done, chain = (k.sig(x) for x in ("state_scaled", "w_ready", "w_done", "u_ready", "u_done", "chain_v"))
            m_ready, y_ready, y_done = k.sig("m_ready"), k.sig("y_ready"), k.sig("y_done")

            def bank(i):
                return k.ps[:, i, 0:GDN_H * V].rearrange("p (h v) -> p h v", v=V)

            def wide(x, p=P):
                return x.unsqueeze(2).broadcast_to([p, GDN_H, V])

            @block.tensor
            def _(pe):
                ts = slice(c * P, (c + 1) * P)
                if n == 0:
                    pe.wait_ge(z_done.sem, z_done.at(1))
                for h in range(GDN_H):
                    if lat:
                        pe.matmul(bank(3)[:, h, :], qT[0:V, h, (c - 2) * P:(c - 1) * P], S[0:V, h, :], start=True, stop=True)
                    mm = pe.matmul(bank(0)[:, h, :], kT[0:V, h, ts], S[0:V, h, :], start=True, stop=True)
                mm.then_inc(w_ready.sem, w_ready.up())
                pe.wait_ge(w_done.sem, w_done.at(2))
                for h in range(GDN_H):
                    mm = pe.matmul(bank(1)[:, h, :], XT[:, h, :], W[:, h, :], start=True, stop=True)
                mm.then_inc(u_ready.sem, u_ready.up())
                pe.wait_ge(u_done.sem, u_done.at(2))
                for h in range(GDN_H):
                    mm = pe.matmul(bank(2)[0:V, h, :], kt[:, c, h, :], U[:, 1, h, :], start=True, stop=True)
                mm.then_inc(m_ready.sem, m_ready.up())
                if lat:
                    for h in range(GDN_H):
                        mm = pe.matmul(bank(4)[:, h, :], AT[:, h, :], U[:, 0, h, :], start=True, stop=True)
                    mm.then_inc(y_ready.sem, y_ready.up())

            @block.vector
            def _(dve):
                if n == 0:
                    dve.memset(S[:, :, :], 0.0).then_inc(z_done.sem, z_done.up())
                dve.wait_ge(w_ready.sem, w_ready.at(1))
                dve.tensor_tensor(W[:, :, :], bank(0), wide(eg[:, 0, :]), ALU.mult).then_inc(chain.sem, chain.up())
                dve.wait_ge(chain.sem, chain.last)
                dve.tensor_tensor(W[:, :, :], vt[:, c, :].rearrange("p (h v) -> p h v", v=V), W[:, :, :], ALU.subtract).then_inc(w_done.sem, w_done.up())
                if lat:
                    dve.tensor_tensor(o1[:, :, :], bank(3), wide(eg[:, 0, :]), ALU.mult).then_inc(w_done.sem, w_done.up())
                else:
                    dve.tensor_tensor(o1[:, :, :], bank(0), wide(eg[:, 0, :]), ALU.mult).then_inc(w_done.sem, w_done.up())
                dve.wait_ge(u_ready.sem, u_ready.at(1))
                dve.tensor_tensor(U[:, 0, :, :], bank(1), wide(beta[:, c, 4 * di:4 * di + 4]), ALU.mult).then_inc(u_done.sem, u_done.up())
                dve.wait_ge(u_done.sem, u_done.last)
                dve.tensor_tensor(U[:, 1, :, :], U[:, 0, :, :], wide(eg[:, 1, :]), ALU.mult).then_inc(u_done.sem, u_done.up())
                dve.wait_ge(m_ready.sem, m_ready.at(1))
                dve.tensor_tensor(S[0:V, :, :], S[0:V, :, :], wide(eg[0:V, 2, :], V), ALU.mult).then_inc(chain.sem, chain.up())
                dve.wait_ge(chain.sem, chain.last)
                dve.tensor_tensor(S[0:V, :, :], S[0:V, :, :], bank(2)[0:V], ALU.add).then_inc(chain.sem, chain.up())
                dve.wait_ge(chain.sem, chain.last)
                if lat:
                    dve.wait_ge(y_ready.sem, y_ready.at(1))
                    dve.wait_ge(w_done.sem, w_done.at(2))
                    dve.tensor_tensor(o1[:, :, :], o1[:, :, :], bank(4), ALU.add).then_inc(chain.sem, chain.up())
                    dve.wait_ge(chain.sem, chain.last)
                    out = y[:, c - 2, :].rearrange("p (h v) -> p h v", v=V)
                    if d == "f":
                        dve.tensor_copy(out, o1[:, :, :]).then_inc(y_done.sem, y_done.up())
                    else:
                        dve.tensor_tensor(out, out, o1[:, :, :], ALU.add).then_inc(y_done.sem, y_done.up())
        k.stage_end()


def stage_out(k, src, factor):
    with k.block() as block:
        x_done = k.sig("x_done")

        @block.tensor
        def _(pe):
            for i in range(DB):
                w, landed, full = k.take()
                pe.wait_ge(landed, full)
                for kt in range(DB):
                    mm = pe.matmul(k.ps[:, i, :], w[:, kt * P:(kt + 1) * P], src[:, kt, :], start=kt == 0, stop=kt == DB - 1)
                mm.then_inc(k.used, 1)

        @block.vector
        def _(dve):
            for i in range(DB):
                dve.wait_ge(k.used, k.after(i))
                dve.scalar_tensor_tensor(k.xT[:, i, :], k.ps[:, i, :], factor(i), k.xT[:, i, :], ALU.mult, ALU.add).then_inc(x_done.sem, x_done.up())

        @block.sync
        def _(sp):
            k.stream(sp, DB)
    k.stage_end()


def stage_mlp(k, hT, factor):
    FB = 32
    with ExitStack() as st:
        hid = k.sb("mlp_hid", [P, FB, T], st)
        with k.block() as block:
            relu_done, h_done, x_done = k.sig("relu_done"), k.sig("he_done"), k.sig("x_done")

            @block.tensor
            def _(pe):
                for i in range(FB):
                    w, landed, full = k.take()
                    pe.wait_ge(landed, full)
                    if i >= 8:
                        pe.wait_ge(relu_done.sem, relu_done.at(i - 7))
                    for kt in range(DB):
                        mm = pe.matmul(k.ps[:, i % 8, :], w[:, kt * P:(kt + 1) * P], hT[:, kt, :], start=kt == 0, stop=kt == DB - 1)
                    mm.then_inc(k.used, 1)
                pe.wait_ge(relu_done.sem, relu_done.at(FB))
                for i in range(DB):
                    for u in range(4):
                        w, landed, full = k.take()
                        pe.wait_ge(landed, full)
                        for kt in range(8):
                            f = 8 * u + kt
                            if i == 0:
                                pe.wait_ge(h_done.sem, h_done.at(f + 1))
                            mm = pe.matmul(k.ps[:, i, :], w[:, kt * P:(kt + 1) * P], hid[:, f, :], start=f == 0, stop=f == FB - 1)
                        mm.then_inc(k.used, 1)

            @block.scalar
            def _(act):
                for i in range(FB):
                    act.wait_ge(k.used, k.after(i))
                    act.activation(hid[:, i, :], k.ps[:, i % 8, :], ACT.Relu).then_inc(relu_done.sem, relu_done.up())

            @block.gpsimd
            def _(pool):
                for i in range(FB):
                    pool.wait_ge(relu_done.sem, relu_done.at(i + 1))
                    pool.tensor_tensor(hid[:, i, :], hid[:, i, :], hid[:, i, :], ALU.mult).then_inc(h_done.sem, h_done.up())

            @block.vector
            def _(dve):
                for i in range(DB):
                    dve.wait_ge(k.used, k.after(FB + 4 * i + 3))
                    dve.scalar_tensor_tensor(k.xT[:, i, :], k.ps[:, i, :], factor(i), k.xT[:, i, :], ALU.mult, ALU.add).then_inc(x_done.sem, x_done.up())

            @block.sync
            def _(sp):
                k.stream(sp, 2 * FB)
        k.stage_end()


def stage_store(k):
    with k.block() as block:
        @block.sync
        def _(sp):
            stored = k.sig("stored")
            sp.dma_start(k.dram["out"], k.xT[:, :, :]).then_inc(stored.sem, stored.up(16))
            sp.wait_ge(stored.sem, stored.at(16))
    k.stage_end()


def stage_silu(k, x):
    with k.block() as block:
        @block.scalar
        def _(act):
            act.activation(x[:, :, :], x[:, :, :], ACT.Silu).then_inc(k.sig("silu_done").sem, k.sig("silu_done").up())
    k.stage_end()


def program(nc, dram):
    with ExitStack() as ctx:
        k = Core(nc, dram, ctx)
        stage_load(k)
        with ExitStack() as b1:
            hT = k.sb("hT", [P, DB, T], b1)
            stage_norm(k, "n1", lambda b: k.xT[:, b, :], lambda b: hT[:, b, :], T, lambda b: k.col("norm1_g", b))
            ybT = k.sb("ybT", [P, RB, T], b1)
            with ExitStack() as na:
                qT, kT, vt = (k.sb(n, [P, 4, T], na) for n in ("qT", "kT", "vt"))
                stage_qkv(k, hT, qT, kT, vt)
                stage_qk_norm(k, qT, kT)
                stage_attention(k, qT, kT, vt, ybT)
            yaT = k.sb("yaT", [P, RB, T], b1)
            with ExitStack() as rw:
                rT, kT = (k.sb(n, [P, RB, T], rw) for n in ("rT", "rkT"))
                lora = k.sb("lora", [P, 3, T], rw)
                stage_rwkv_in(k, hT, rT, kT, yaT, lora)
                stage_rwkv(k, rT, kT, yaT, lora, yaT)
            stage_merge(k, hT, yaT, ybT)
        with ExitStack() as b1:
            hT = k.sb("h2T", [P, DB, T], b1)
            comb = k.sb("comb", [P, NT, NE], b1)
            stage_norm(k, "n2", lambda b: k.xT[:, b, :], lambda b: hT[:, b, :], T, lambda b: k.col("norm2_g", b))
            stage_router(k, hT, comb)
            acc = k.sb("acc", [P, NT, D], b1)
            stage_moe(k, hT, comb, acc)
            stage_add_tokens(k, acc)
        with ExitStack() as b2:
            mod, gain = k.sb("mod", [P, 48, 2], b2), k.sb("gain", [P, 3, DB], b2)
            stage_mod(k, mod, gain)
            with ExitStack() as mixer:
                mixT = k.sb("mixT", [P, DB, T], mixer)
                hT = k.sb("hmT", [P, DB, T2], mixer)
                stage_load_ctx(k, hT)
                stage_norm(k, "n3", lambda b: hT[:, b, 0:CTX], lambda b: hT[:, b, 0:CTX], CTX,
                           lambda b: gain[:, 1, b:b + 1], shift=lambda b: mod[:, b, 1:2])
                stage_norm(k, "n4", lambda b: k.xT[:, b, :], lambda b: hT[:, b, CTX:T2], T,
                           lambda b: gain[:, 0, b:b + 1], shift=lambda b: mod[:, b, 0:1])
                with ExitStack() as hy:
                    u = k.sb("hy_u", [P, 6, T], hy)
                    with ExitStack() as raw:
                        z = k.sb("hy_raw", [P, 6, T], raw)
                        stage_project(k, hT, [(z[:, i, :], None, ACT.Copy, 1.0) for i in range(6)])
                        stage_conv(k, [(u[:, i, :], z[:, i, :], T // GRID_W, i, P) for i in range(6)], Taps(k, "hy_w", 3),
                                   lambda i: k.col("hy_b", i))
                    stage_hyena(k, u, mixT)
                ldec, beta = k.sb("ldec", [P, NT2, 8], mixer), k.sb("beta", [P, NT2, 8], mixer)
                with ExitStack() as gla:
                    la = k.sb("gla_la", [P, 2, NT2, 256], gla)
                    with ExitStack() as pre:
                        aT = k.sb("aT2", [P, T2], pre)
                        gt = k.sb("gt", [P, NT2, 16], pre)
                        stage_project(k, hT, [(aT[:, CTX:T2], aT[:, 0:CTX], ACT.Copy, 1.0)])
                        stage_to_tokens(k, [(gt[:, t, :], aT[64:80, t * P:(t + 1) * P], 64) for t in range(NT2)])
                        stage_gates(k, aT, gt, la, ldec, beta)
                    qT, kT = k.sb("gla_q", [P, 2, T], gla), k.sb("gla_k", [P, 2, T2], gla)
                    vt, gateT = k.sb("gla_v", [P, NT2, VW], gla), k.sb("gla_gate", [P, 3, T], gla)
                    y = k.sb("gla_y", [P, NT, VW], gla)
                    with ExitStack() as pre:
                        vT = k.sb("gla_vT", [P, 3, T2], pre)
                        stage_project(k, hT, [(qT[:, b, :], None, ACT.Copy, GLA_DK ** -0.5) for b in range(2)] +
                                      [(kT[:, b, CTX:T2], kT[:, b, 0:CTX], ACT.Copy, 1.0) for b in range(2)] +
                                      [(vT[:, b, CTX:T2], vT[:, b, 0:CTX], ACT.Copy, 1.0) for b in range(3)] +
                                      [(gateT[:, b, :], None, ACT.Silu, 1.0) for b in range(3)])
                        stage_to_tokens(k, [(vt[:, t, b * P:(b + 1) * P], vT[:, b, t * P:(t + 1) * P])
                                            for t in range(NT2) for b in range(3)])
                    S = k.sb("gla_S", [P, 2, GLA_DV], gla)
                    for d, order in (("f", (0, 1, 2, 3, 4, 5)), ("b", (1, 0, 5, 4, 3, 2))):
                        for n, c in enumerate(order):
                            stage_gla_chunk(k, d, c, n, qT, kT, vt, la, S, y)
                    stage_head_norm(k, y, "gla_g", gateT, mixT, 2)
                with ExitStack() as gdn:
                    qT, kT = k.sb("gdn_q", [P, 4, T], gdn), k.sb("gdn_k", [P, 4, T2], gdn)
                    vt, gateT = k.sb("gdn_v", [P, NT2, VW], gdn), k.sb("gdn_gate", [P, 3, T], gdn)
                    taps = Taps(k, "gdn_w", 7)

                    def conv(dst, z, b, i, n):
                        return [(dst[0:n, b, CTX:T2], z[0:n, b, CTX:T2], T // GRID_W, i, n),
                                (dst[0:n, b, 0:CTX], z[0:n, b, 0:CTX], 1, i, n)]
                    with ExitStack() as pre:
                        z = k.sb("gdn_z", [P, 4, T2], pre)
                        stage_project(k, hT, [(z[:, b, CTX:T2], None, ACT.Copy, 1.0) for b in range(4)])
                        stage_conv(k, [(qT[0:96, b, :], z[0:96, b, CTX:T2], T // GRID_W, b, 96) for b in range(4)], taps)
                        stage_project(k, hT, [(z[:, b, CTX:T2], z[:, b, 0:CTX], ACT.Copy, 1.0) for b in range(4)])
                        stage_conv(k, [x for b in range(4) for x in conv(kT, z, b, 4 + b, 96)], taps)
                        vT = k.sb("gdn_vT", [P, 3, T2], pre)
                        stage_project(k, hT, [(z[:, b, CTX:T2], z[:, b, 0:CTX], ACT.Copy, 1.0) for b in range(3)] +
                                      [(gateT[:, b, :], None, ACT.Silu, 1.0) for b in range(3)])
                        stage_conv(k, [x for b in range(3) for x in conv(vT, z, b, 8 + b, P)], taps)
                        stage_to_tokens(k, [(vt[:, t, b * P:(b + 1) * P], vT[:, b, t * P:(t + 1) * P])
                                            for t in range(NT2) for b in range(3)])
                        stage_silu(k, vt)
                        stage_l2(k, qT, kT)
                    kt = k.sb("gdn_kt", [P, NT2, GDN_H, GDN_D], gdn)
                    stage_to_tokens(k, [(kt[:, t, h, :], kT[0:GDN_D, h, t * P:(t + 1) * P])
                                        for t in range(NT2) for h in range(GDN_H)])
                    y = k.sb("gdn_y", [P, NT, VW], gdn)
                    S = k.sb("gdn_S", [P, GDN_H, GDN_D], gdn)
                    LT, AT = k.sb("gdn_LT", [P, GDN_H, P], gdn), k.sb("gdn_AT", [P, GDN_H, P], gdn)
                    eg = k.sb("gdn_eg", [P, 4, GDN_H], gdn)
                    w = {x: k.sb("gdn_" + x, [P, GDN_H, P], gdn) for x in ("X", "XT", "M", "Y")}
                    for d, order in (("f", (0, 1, 2, 3, 4, 5)), ("b", (1, 0, 5, 4, 3, 2))):
                        for n, c in enumerate(order):
                            stage_gdn_chunk(k, d, c, qT, kT, ldec, beta, LT, AT, eg)
                            stage_solve(k, w, GDN_H, lambda h2: LT[:, 2 * h2:2 * h2 + 2, :], d == "b")
                            stage_gdn_step(k, d, c, n, qT, kT, kt, vt, w["XT"], AT, eg, beta, S, y)
                    stage_head_norm(k, y, "gdn_g", gateT, mixT, 5)
                stage_out(k, mixT, lambda i: mod[:, 16 + i, 0:1])
            with ExitStack() as ml:
                hT = k.sb("h4T", [P, DB, T], ml)
                stage_norm(k, "n5", lambda b: k.xT[:, b, :], lambda b: hT[:, b, :], T,
                           lambda b: gain[:, 2, b:b + 1], shift=lambda b: mod[:, 24 + b, 0:1])
                stage_mlp(k, hT, lambda i: mod[:, 40 + i, 0:1])
        stage_norm(k, "n6", lambda b: k.xT[:, b, :], lambda b: k.xT[:, b, :], T, lambda b: k.col("final_g", b))
        stage_store(k)
        assert k.taken == k.issued == N_UNITS


def _blocks(w, cols=P):
    kk, n = w.shape
    return w.reshape(kk // P, P, n // P, P).transpose(2, 1, 0, 3).reshape(n // P, P, kk)


def _tok_units(w):
    n = w.shape[1]
    return w.reshape(DB, P, n).transpose(1, 0, 2).reshape(P, -1, UNIT).transpose(1, 0, 2)


def _slots(w, heads, width, slot):
    out = np.zeros((w.shape[0], heads, slot), np.float32)
    out[:, :, :width] = w.reshape(w.shape[0], heads, width)
    return out.reshape(w.shape[0], heads * slot)


def _colmajor(v):
    return v.reshape(-1, P).T


def host_constants():
    i = np.arange(P)
    s, t = i[:, None], i[None, :]
    f = np.float32
    part = {"ident": s == t, "ones": np.ones((P, P)), "ones64": s // HD == t // HD}
    lvl = []
    for lv in range(LEVELS):
        half = 1 << lv
        lvl.append((s // (2 * half) == t // (2 * half)) & (s % (2 * half) < half) & (t % (2 * half) >= half))
    part["tri_f"] = np.hstack([s <= t, s < t])
    part["tri_b"] = np.hstack([s >= t, s > t])
    part["attn_f"] = np.hstack([s < t, s <= t] * 2)
    part["attn_b"] = np.hstack([s > t, s >= t] * 2)
    part["level_f"] = np.hstack(lvl)
    part["level_b"] = np.hstack([m.T for m in lvl])
    const = np.hstack([part[n] for n in CONST]).astype(f)
    hsum = np.zeros((P, RB, 8), f)
    for b in range(RB):
        hsum[i, b, 2 * b + i // HD] = 1
    cols = np.arange(GRID_W)
    start = np.clip(cols - 8, 0, GRID_W - 16)
    seen = (cols[None] >= start[:, None]) & (cols[None] < start[:, None] + 16)
    na = np.where(seen, 0, -1e30).astype(f)
    gidx = np.broadcast_to(np.concatenate([4 - np.arange(4), 8 - np.arange(8)]), (P, 12)).astype(f)
    n = 2 * T - 1
    ang = 2 * np.pi * ((np.arange(T)[:, None] * np.arange(NFREQ)[None]) % n) / n
    dft = np.hstack([np.cos(ang), -np.sin(ang)])
    wt = np.where(np.arange(NFREQ) == 0, 1.0, 2.0)[:, None] / n
    inv = np.vstack([np.cos(ang.T) * wt, -np.sin(ang.T) * wt])
    dft = dft.reshape(NT, P, 2 * NFREQ).transpose(1, 0, 2)
    inv = inv.reshape(8, P, T).transpose(1, 0, 2)
    tl = np.linspace(0.0, 1.0, T, dtype=f)[:, None]
    fr = np.linspace(1e-4, 15, 16, dtype=f)
    w = (2 * np.pi * np.arange(T, dtype=f) / T).astype(f)
    an = w[:, None] * fr[None]
    z = np.concatenate([tl, np.cos(an), -np.sin(an)], -1).T
    deltas = np.abs(np.linspace(np.log(1e-2) / 1.5, np.log(1e-2) / 0.3, HY_C, dtype=f))
    win = np.exp(-tl * deltas[None])
    back = win.copy()
    back[0] = 0
    win = np.hstack([win, back]).reshape(NT, P, 2 * HY_C).transpose(1, 0, 2)
    hy = np.zeros((P, T), f)
    hy[:33] = z
    return {"const": const, "hsum": hsum.reshape(P, -1), "na_mask": np.vstack([na, na]), "gidx": gidx,
            "dft": dft.astype(f), "inv": inv.astype(f), "hy_z": hy, "hy_win": win.astype(f)}


def host_layout(a):
    f = np.float32
    hc = host_constants()
    l = {n: (v[0] if n not in ("x", "c_2", "ctx_2", "c_ctx_2", "final_norm_g_2") else v) for n, v in a.items()}
    w_in, w_in2 = l["w_in"], l["w_in_2"]
    o = 1920
    q, kk, v, gate = w_in[:, o:o + 512], w_in[:, o + 512:o + 1024], w_in[:, o + 1024:o + 1536], w_in[:, o + 1536:]
    wo = np.concatenate([l["w_o_rwkv"], l["w_o_na"]])
    moe = np.concatenate([
        l["w_gate_e"].reshape(NE, DB, P, 2, P).transpose(0, 3, 2, 1, 4).reshape(NE, 2, 1, P, UNIT),
        l["w_up_e"].reshape(NE, DB, P, 2, P).transpose(0, 3, 2, 1, 4).reshape(NE, 2, 1, P, UNIT)], 2)
    moe = np.concatenate([moe.reshape(NE, 4, P, UNIT), l["w_down_e"].reshape(NE, 2, P, D)], 1)
    hy, gla, gdn = w_in2[:, :768], w_in2[:, 768:768 + 1184], w_in2[:, 768 + 1184:]
    misc = np.zeros((D, P), f)
    misc[:, 0:16], misc[:, 32:48], misc[:, 64:80] = gla[:, 1152:1168], gla[:, 1168:1184], gdn[:, 1536:1552]
    parts = {
        "qk": _blocks(np.hstack([q, kk])), "v": _tok_units(v), "rwkv": _blocks(w_in[:, :o]),
        "gate": _blocks(gate), "o": _blocks(wo), "out": _blocks(l["w_out"]), "moe": moe.reshape(-1, P, UNIT),
        "mod": _blocks(l["w_mod_2"]), "hy": _blocks(hy), "misc2": _blocks(misc),
        "gla_q": _blocks(_slots(gla[:, 0:192], 4, 48, 64)), "gla_k": _blocks(_slots(gla[:, 192:384], 4, 48, 64)),
        "gla_v": _blocks(gla[:, 384:768]), "gla_gate": _blocks(gla[:, 768:1152]),
        "gdn_qk": _blocks(_slots(gdn[:, 0:768], 8, 96, 128)), "gdn_v": _blocks(gdn[:, 768:1152]),
        "gdn_gate": _blocks(gdn[:, 1152:1536]),
        "out2": _blocks(l["w_out_2"]), "mlp1": _blocks(l["w_mlp1_2"]),
        "mlp2": l["w_mlp2_2"].reshape(4, 8, P, 8, P).transpose(3, 0, 2, 1, 4).reshape(32, P, UNIT),
    }
    for n, (at, units) in STREAM.items():
        assert parts[n].shape == (units, P, UNIT), (n, parts[n].shape)
    stream = np.concatenate([parts[n] for n in STREAM])

    def pad(v, n=P):
        out = np.zeros((n, v.shape[1]), f)
        out[:len(v)] = v
        return out
    gw = l["gdn_conv_w_2"]
    gdn_w = np.zeros((P, 11, 7), f)
    gdn_w[:96, :8] = gw[:, :768].reshape(7, 8, 96).transpose(2, 1, 0)
    gdn_w[:, 8:] = gw[:, 768:].reshape(7, 3, P).transpose(2, 1, 0)
    col = {
        **{n: _colmajor(l[n]) for n in ("norm1_g", "mu_prev", "mu_next", "a0_f", "a0_b", "k_k", "k_a", "b_gate",
                                        "norm2_g", "norm1_g_2", "norm2_g_2")},
        "r_k": _colmajor(l["r_k"].reshape(-1)), "b_mod": _colmajor(l["b_mod_2"]),
        "q_gain": np.concatenate([l["q_gain"]] * 2)[:, None], "k_gain": np.concatenate([l["k_gain"]] * 2)[:, None],
        "cc": np.stack([_colmajor(l["c_2"][0]), _colmajor(l["c_ctx_2"])], 2).reshape(P, 16),
        "hy_w": l["hy_conv_w_2"].reshape(3, 6, P).transpose(2, 1, 0).reshape(P, 18),
        "hy_b": _colmajor(l["hy_conv_b_2"]), "hy_d": _colmajor(l["hy_d_2"].reshape(-1)),
        "gdn_w": gdn_w.reshape(P, 77), "final_g": _colmajor(l["final_norm_g_2"]),
        "hy_b1": pad(l["hy_f_b1_2"][:, None]), "hy_b2": pad(l["hy_f_b2_2"][:, None]),
        "hy_f1": pad(l["hy_sin_freq_2"][0][:, None]), "hy_f2": pad(l["hy_sin_freq_2"][1][:, None]),
    }
    row = {
        "w0_f": l["w0_f"], "w0_b": l["w0_b"], "lnx_g": l["lnx_g"], "lnx_b": l["lnx_b"],
        "b_router": np.concatenate([l["b_router_group"], l["b_router_expert"]]),
        "gla_b": np.concatenate([_slots(l["gla_b_a_2"][d][None], 4, 48, 64)[0] for d in range(2)]),
        "gla_g": l["gla_norm_g_2"], "gdn_g": l["gdn_norm_g_2"], "a_log": l["gdn_a_log_2"].reshape(-1),
        "dt_bias": l["gdn_dt_bias_2"].reshape(-1),
    }
    router = np.hstack([l["w_router_group"], l["w_router_expert"]]).reshape(DB, P, 36).transpose(1, 0, 2)
    a2 = np.zeros((P, 256), f)
    a2[0:16], a2[32:48] = (_slots(l["gla_w_a2_2"][d], 4, 48, 64) for d in range(2))
    mat = {
        "w_up": np.vstack([l["w_up_f"], l["w_up_b"]]), "a_up": np.vstack([l["a_up_f"], l["a_up_b"]]),
        "g_up": l["g_up"], "hsum": hc["hsum"], "router": router.reshape(P, -1), "hy_w1": pad(l["hy_f_w1_2"]),
        "hy_w2": pad(l["hy_f_w2_2"]), "hy_w3": pad(l["hy_f_w3_2"]), "gla_a2": a2, "na_mask": hc["na_mask"],
        "gidx": hc["gidx"],
    }
    rpb = l["rpb"]
    cols = np.arange(GRID_W)
    off = np.clip(cols[None] - cols[:, None] + 15, 0, 30)
    e = rpb[:, :, off]
    rel = np.stack([e[:, 1:15], e[:, 0:14]]).transpose(0, 3, 1, 2, 4).reshape(P, RH, 14 * GRID_W)

    def chan(x):
        return x.T.reshape(DB, P, -1).transpose(1, 0, 2)
    return {"stream": stream, "xT": chan(l["x"][0]), "ctxT": chan(l["ctx_2"][0]), "const": hc["const"],
            "cols": np.hstack([col[n] for n in COL]), "rows": np.concatenate([row[n] for n in ROW])[None],
            "mats": np.hstack([mat[n] for n in MAT]), "rel": rel,
            "dft": hc["dft"], "inv": hc["inv"], "hy_z": hc["hy_z"], "hy_win": hc["hy_win"]}


def kernel(**inputs):
    import concourse.bacc as bacc
    from concourse.bass_utils import run_bass_kernel_spmd

    nc = bacc.Bacc("TRN2", target_bir_lowering=False, num_devices=1)
    arrays, dram = {}, {}
    for name, a in host_layout({n: np.asarray(v) for n, v in inputs.items()}).items():
        a = np.ascontiguousarray(a, dtype=np.float32)
        arrays[name + "_in"] = a
        dram[name] = nc.dram_tensor(name + "_in", a.shape, F32, kind="ExternalInput").ap()
    dram["out"] = nc.dram_tensor("out_0", (P, DB, T), F32, kind="ExternalOutput").ap()
    program(nc, dram)
    r = run_bass_kernel_spmd(nc, [arrays], core_ids=[0])
    out = r.results[0]["out_0"]
    return out.transpose(2, 1, 0).reshape(1, T, D)
```

```python
from contextlib import ExitStack

import numpy as np
import concourse.bass as bass
from concourse import mybir

F32 = mybir.dt.float32
U32 = mybir.dt.uint32
F32R = mybir.dt.float32r
ACT = mybir.ActivationFunctionType
ALU = mybir.AluOpType
AX = mybir.AxisListType

P = 128
D = 1024
DB = D // P
T = 512
NT = T // P
CTX = 256
T2 = CTX + T
NT2 = T2 // P
GRID_W = 64
RH, HD = 8, 64
RW = RH * HD
RB = RW // P
NE = 32
RING = 6
UNIT = 1024
RMS_EPS, GN_EPS, L2_EPS = 1e-6, 64e-5, 1e-12
DECAY = float(np.exp(-0.5))
NO_ROW = 4095
LEVELS = 7
MG = 6
HY_C = 256
NFREQ = 512
GLA_H, GLA_DK, GLA_DV = 4, 48, 96
GDN_H, GDN_D = 4, 96
VW = 384

def table(*items):
    at, out = 0, {}
    for name, n in items:
        out[name] = (at, n)
        at += n
    return out, at

CONST, N_CONST = table(("ident", P), ("ones", P), ("ones64", P), ("tri_f", 2 * P), ("tri_b", 2 * P),
                       ("attn_f", 4 * P), ("attn_b", 4 * P), ("level_f", LEVELS * P),
                       ("level_b", LEVELS * P))
COL, N_COL = table(("norm1_g", 8), ("mu_prev", 15), ("mu_next", 15), ("a0_f", 4), ("a0_b", 4),
                   ("k_k", 4), ("k_a", 4), ("r_k", 4), ("b_gate", 16), ("norm2_g", 8),
                   ("q_gain", 1), ("k_gain", 1), ("norm1_g_2", 8), ("norm2_g_2", 8), ("b_mod", 48),
                   ("cc", 16), ("hy_w", 18), ("hy_b", 6), ("hy_d", 4), ("gdn_w", 77),
                   ("final_g", 8), ("hy_b1", 1), ("hy_b2", 1), ("hy_f1", 1), ("hy_f2", 1))
ROW, N_ROW = table(("w0_f", RW), ("w0_b", RW), ("lnx_g", RW), ("lnx_b", RW), ("b_router", 36),
                   ("gla_b", 512), ("gla_g", 96), ("gdn_g", 96), ("a_log", 8), ("dt_bias", 8))
MAT, N_MAT = table(("w_up", RW), ("a_up", RW), ("g_up", RW), ("hsum", RB * 8), ("router", DB * 36),
                   ("hy_w1", 64), ("hy_w2", 64), ("hy_w3", 1024), ("gla_a2", 256), ("na_mask", 64),
                   ("gidx", 12), ("slot_vals", 2 * NT + NE))

STREAM, N_UNITS = table(("qk", 8), ("v", 4), ("rwkv", 15), ("gate", 16), ("o", 8), ("out", 8),
                        ("moe", NE * 6), ("hy", 6), ("misc2", 1), ("gla_q", 2), ("gla_k", 2),
                        ("gla_v", 3), ("gla_gate", 3), ("gdn_qk", 8), ("gdn_v", 3), ("gdn_gate", 3),
                        ("out2", 8), ("mlp", 64))


class Signal:

    def __init__(self, sem):
        self.sem, self.base, self.n = sem, 0, 0

    def up(self, by=1):
        self.n += by
        return by

    def at(self, n):
        assert self.base + n > 0
        return self.base + n

    @property
    def last(self):
        return self.base + self.n


class Core:

    def __init__(self, nc, dram, ctx):
        self.nc, self.dram, self.ctx = nc, dram, ctx
        self.signals, self.names = {}, {}
        self.ring = self.sb("ring", [P, RING, UNIT])
        self.landed = [ctx.enter_context(nc.semaphore(f"unit_landed{s}")) for s in range(RING)]
        self.used = ctx.enter_context(nc.semaphore("unit_used"))
        self.issued = self.taken = 0
        self.const = self.sb("const", [P, N_CONST])
        self.cols = self.sb("cols", [P, N_COL])
        self.xT = self.sb("xT", [P, DB, T])
        self.silu_c = self.sb("silu_c", [P, DB, 2])
        self.mod = self.sb("mod", [P, 48, 2])
        self.gain = self.sb("gain", [P, 3, DB])
        self.ps = ctx.enter_context(nc.psum_tensor("ps", [P, 8, 512], F32))

    def sb(self, name, shape, ctx=None, dt=F32):
        self.names[name] = n = self.names.setdefault(name, 0) + 1
        return (ctx or self.ctx).enter_context(self.nc.sbuf_tensor(f"{name}_{n}" if n > 1 else name, shape, dt))

    def sig(self, name):
        if name not in self.signals:
            self.signals[name] = Signal(self.ctx.enter_context(self.nc.semaphore(name)))
        return self.signals[name]

    def stage_end(self):
        for s in self.signals.values():
            s.base, s.n = s.base + s.n, 0

    def c(self, name):
        a, n = CONST[name]
        return self.const[:, a:a + n]

    def col(self, name, i=0, p0=0, p1=P):
        a, n = COL[name]
        return self.cols[p0:p1, a + i:a + i + 1]

    def stream(self, sp, units):
        end = min(self.taken_at_stage + units + RING, N_UNITS)
        while self.issued < end:
            u = self.issued
            if u >= RING:
                sp.wait_ge(self.used, u - RING + 1)
            sp.dma_start(self.ring[:, u % RING, :], self.dram["stream"][u]).then_inc(self.landed[u % RING], 16)
            self.issued += 1

    def take(self):
        u = self.taken
        self.taken += 1
        return self.ring[:, u % RING, :], self.landed[u % RING], 16 * (u // RING + 1)

    def after(self, i):
        return self.taken_at_stage + i + 1

    def block(self):
        self.taken_at_stage = self.taken
        return self.nc.Block()


class Split:

    def __init__(self, k, st):
        self.k = k
        self.hi, self.lo = (k.sb("weights_" + x, [P, 2, UNIT], st, F32R) for x in ("hi", "lo"))
        self.cast, self.done = k.sig("weights_cast"), k.sig("products_done")

    def unit(self, i):
        u = self.k.taken_at_stage + i
        return self.k.ring[:, u % RING, :], self.k.landed[u % RING], 16 * (u // RING + 1)

    def round(self, act, i):
        w, landed, full = self.unit(i)
        act.wait_ge(landed, full)
        if i >= 2:
            act.wait_ge(self.done.sem, self.done.at(i - 1))
        act.copy(self.hi[:, i % 2, :], w).then_inc(self.cast.sem, self.cast.up())

    def rest(self, eng, i):
        eng.wait_ge(self.cast.sem, self.cast.at(i + 1))
        eng.tensor_tensor(self.lo[:, i % 2, :], self.unit(i)[0], self.hi[:, i % 2, :], ALU.subtract).then_inc(self.k.used, 1)

    def ready(self, pe, i):
        self.k.take()
        pe.wait_ge(self.k.used, self.k.after(i))

    def parts(self, i, a, b):
        return self.hi[:, i % 2, a:b], self.lo[:, i % 2, a:b]

    def wait(self, eng, i):
        eng.wait_ge(self.done.sem, self.done.at(i + 1))


def product(pe, out, left, right, start, stop, **kw):
    pe.matmul(out, left[0], right[0], start=start, stop=False, **kw)
    pe.matmul(out, left[0], right[1], start=False, stop=False, **kw)
    return pe.matmul(out, left[1], right[0], start=False, stop=stop, **kw)


def stage_load(k):
    with k.block() as block:
        @block.sync
        def _(sp):
            got = k.sig("load")
            sp.dma_start(k.xT[:, :, :], k.dram["xT"]).then_inc(got.sem, got.up(16))
            sp.dma_start(k.cols[:, :], k.dram["cols"]).then_inc(got.sem, got.up(16))
            sp.dma_start(k.const[:, :], k.dram["const"]).then_inc(got.sem, got.up(16))
            k.stream(sp, 0)
            sp.wait_ge(got.sem, got.at(48))

        @block.scalar
        def _(act):
            got, c_done = k.sig("load"), k.sig("silu_done")
            act.wait_ge(got.sem, got.at(48))
            a = COL["cc"][0]
            act.activation(k.silu_c[:, :, :].rearrange("p b i -> p (b i)"), k.cols[:, a:a + 16], ACT.Silu).then_inc(c_done.sem, c_done.up())
    k.stage_end()


def stage_norm(k, name, src, dst, n, gain, eps=RMS_EPS, shift=None, split=None):
    with ExitStack() as st:
        sq = k.sb(name + "_sq", [P, DB, n], st)
        std = k.sb(name + "_std", [P, n], st)
        with k.block() as block:
            squared, summed, rooted, chain, rounded, rested = (
                k.sig(x) for x in ("squared", "summed", "rooted", "chain_v", "rounded", "rested"))

            @block.scalar
            def _(act):
                for b in range(DB):
                    act.activation(sq[:, b, :], src(b), ACT.Square).then_inc(squared.sem, squared.up())
                act.wait_ge(summed.sem, summed.at(1))
                act.activation(std[:, :], k.ps[:, 0, 0:n], ACT.Sqrt, scale=1.0 / D, bias=eps).then_inc(rooted.sem, rooted.up())
                if split:
                    for b in range(DB):
                        act.wait_ge(chain.sem, chain.at(2 + b + (DB if shift else 0)))
                        act.copy(split(b)[0], dst(b)).then_inc(rounded.sem, rounded.up())

            @block.gpsimd
            def _(pool):
                if split:
                    for b in range(DB):
                        pool.wait_ge(rounded.sem, rounded.at(b + 1))
                        pool.tensor_tensor(split(b)[1], dst(b), split(b)[0], ALU.subtract).then_inc(rested.sem, rested.up())

            @block.tensor
            def _(pe):
                for b in range(DB):
                    pe.wait_ge(squared.sem, squared.at(b + 1))
                    mm = pe.matmul(k.ps[:, 0, 0:n], k.c("ones"), sq[:, b, :], start=b == 0, stop=b == DB - 1)
                mm.then_inc(summed.sem, summed.up())

            @block.vector
            def _(dve):
                dve.wait_ge(rooted.sem, rooted.at(1))
                dve.reciprocal(std[:, :], std[:, :]).then_inc(chain.sem, chain.up())
                dve.wait_ge(chain.sem, chain.last)
                for b in range(DB):
                    dve.scalar_tensor_tensor(dst(b), src(b), gain(b), std[:, :], ALU.mult, ALU.mult).then_inc(chain.sem, chain.up())
                if shift:
                    for b in range(DB):
                        dve.wait_ge(chain.sem, chain.at(2 + b))
                        dve.tensor_scalar(dst(b), dst(b), shift(b), None, ALU.add).then_inc(chain.sem, chain.up())

            @block.sync
            def _(sp):
                k.stream(sp, 0)
        k.stage_end()


OFFS = 14


def stage_qkv(k, h, qT, kT, vt, rel):
    with ExitStack() as st:
        w = Split(k, st)
        mask = k.sb("na_mask", [P, GRID_W], st)
        with k.block() as block:
            copied = [k.sig("copied_act"), k.sig("copied_dve")]
            rel_in, masked = k.sig("rel_in"), k.sig("masked")

            @block.gpsimd
            def _(pool):
                a, n = MAT["na_mask"]
                pool.dma_start(rel[:, :, :], k.dram["rel"]).then_inc(rel_in.sem, rel_in.up(16))
                pool.dma_start(mask[:, :], k.dram["mats"][:, a:a + n]).then_inc(rel_in.sem, rel_in.up(16))
                pool.wait_ge(rel_in.sem, rel_in.at(32))
                v = rel[:, :, :].rearrange("p h (o c) -> p (h o) c", c=GRID_W)
                pool.tensor_tensor(v, v, mask[:, :].unsqueeze(1).broadcast_to([P, RH * OFFS, GRID_W]), ALU.add).then_inc(masked.sem, masked.up())

            @block.tensor
            def _(pe):
                for g in range(8):
                    w.ready(pe, g)
                    for kt in range(DB):
                        mm = product(pe, k.ps[:, g, :], w.parts(g, kt * P, (kt + 1) * P), (h[0][:, kt, :], h[1][:, kt, :]),
                                     kt == 0, kt == DB - 1)
                    mm.then_inc(w.done.sem, w.done.up())
                for u in range(4):
                    w.ready(pe, 8 + u)
                    for j in range(2):
                        kt = 2 * u + j
                        for t in range(NT):
                            if kt == 0:
                                pe.wait_ge(copied[t % 2].sem, copied[t % 2].at(t // 2 + 1))
                            ts = slice(t * P, (t + 1) * P)
                            mm = product(pe, k.ps[:, t, :], (h[0][:, kt, ts], h[1][:, kt, ts]), w.parts(8 + u, j * 512, (j + 1) * 512),
                                         kt == 0, kt == DB - 1, skip_group_check=True)
                    mm.then_inc(w.done.sem, w.done.up())

            def dst(g):
                return qT[:, g, :] if g < 4 else kT[:, g - 4, :] if g < 8 else vt[:, g - 8, :]

            @block.scalar
            def _(act):
                w.round(act, 0)
                for g in range(8):
                    w.round(act, g + 1)
                    if g % 2 == 0:
                        w.wait(act, g)
                        act.copy(dst(g), k.ps[:, g, :]).then_inc(copied[0].sem, copied[0].up())
                for u in range(9, 12):
                    w.round(act, u)
                for g in (8, 10):
                    w.wait(act, 11)
                    act.copy(dst(g), k.ps[:, g % 8, :]).then_inc(copied[0].sem, copied[0].up())

            @block.vector
            def _(dve):
                w.rest(dve, 0)
                for g in range(8):
                    w.rest(dve, g + 1)
                    if g % 2:
                        w.wait(dve, g)
                        dve.tensor_copy(dst(g), k.ps[:, g, :]).then_inc(copied[1].sem, copied[1].up())
                for u in range(9, 12):
                    w.rest(dve, u)
                for g in (9, 11):
                    w.wait(dve, 11)
                    dve.tensor_copy(dst(g), k.ps[:, g % 8, :]).then_inc(copied[1].sem, copied[1].up())

            @block.sync
            def _(sp):
                k.stream(sp, 12)
        k.stage_end()


def stage_qk_norm(k, qT, kT):
    with ExitStack() as st:
        sq = k.sb("qk_sq", [P, 8, T], st)
        std = k.sb("qk_std", [P, 8, T], st)
        with k.block() as block:
            squared, summed, rooted, chain = (k.sig(x) for x in ("squared", "summed", "rooted", "chain_v"))

            def src(g):
                return qT[:, g, :] if g < 4 else kT[:, g - 4, :]

            @block.scalar
            def _(act):
                for g in range(8):
                    act.activation(sq[:, g, :], src(g), ACT.Square).then_inc(squared.sem, squared.up())
                for g in range(8):
                    act.wait_ge(summed.sem, summed.at(g + 1))
                    f = 1.0 if g < 4 else 1.0 / HD
                    act.activation(std[:, g, :], k.ps[:, g, :], ACT.Sqrt, scale=f, bias=f * HD * RMS_EPS).then_inc(rooted.sem, rooted.up())

            @block.tensor
            def _(pe):
                for g in range(8):
                    pe.wait_ge(squared.sem, squared.at(g + 1))
                    pe.matmul(k.ps[:, g, :], k.c("ones64"), sq[:, g, :], start=True, stop=True).then_inc(summed.sem, summed.up())

            @block.vector
            def _(dve):
                for g in range(8):
                    dve.wait_ge(rooted.sem, rooted.at(g + 1))
                    dve.reciprocal(std[:, g, :], std[:, g, :]).then_inc(chain.sem, chain.up())
                    dve.wait_ge(chain.sem, chain.last)
                    dve.scalar_tensor_tensor(src(g), src(g), k.col("q_gain" if g < 4 else "k_gain"),
                                             std[:, g, :], ALU.mult, ALU.mult).then_inc(chain.sem, chain.up())
        k.stage_end()


def stage_attention(k, qT, kT, vt, rel, yT):
    with ExitStack() as st:
        s_sb = k.sb("na_s", [P, 2, T], st)
        p_sb = k.sb("na_p", [P, 2, T], st)
        pT = k.sb("na_pT", [P, 2, T], st)
        y = k.sb("na_y", [P, NT, RW], st)
        stat = k.sb("na_stat", [P, 4, RH * NT], st)
        N = RH * NT
        with k.block() as block:
            s_ready, biased, p_ready = k.sig("s_ready"), k.sig("biased"), k.sig("p_ready")
            t_ready, pt_ready, o_ready, o_done = (k.sig(x) for x in ("t_ready", "pt_ready", "o_ready", "o_done"))
            chain, y_ready, y_copied = k.sig("chain_v"), k.sig("y_ready"), k.sig("y_copied")

            @block.tensor
            def _(pe):
                for i in range(N + 2):
                    if i < N:
                        h, t = divmod(i, NT)
                        a = HD * (h % 2)
                        if i >= 2:
                            pe.wait_ge(biased.sem, biased.at(i - 1))
                        pe.matmul(k.ps[:, i % 2, :], qT[a:a + HD, h // 2, t * P:(t + 1) * P],
                                  kT[a:a + HD, h // 2, :], start=True, stop=True).then_inc(s_ready.sem, s_ready.up())
                    if 1 <= i <= N:
                        j = i - 1
                        pe.wait_ge(p_ready.sem, p_ready.at(j + 1))
                        if j >= 2:
                            pe.wait_ge(pt_ready.sem, pt_ready.at(j - 1))
                        for q in range(NT):
                            mm = pe.transpose(k.ps[:, 2 + j % 2, q * P:(q + 1) * P],
                                              p_sb[:, j % 2, q * P:(q + 1) * P], k.c("ident"))
                        mm.then_inc(t_ready.sem, t_ready.up())
                    if i >= 2:
                        j = i - 2
                        h = j // NT
                        pe.wait_ge(pt_ready.sem, pt_ready.at(j + 1))
                        if j >= 2:
                            pe.wait_ge(o_done.sem, o_done.at(j - 1))
                        for q in range(NT):
                            mm = pe.matmul(k.ps[:, 4 + j % 2, 0:HD], pT[:, j % 2, q * P:(q + 1) * P],
                                           vt[:, q, h * HD:(h + 1) * HD], start=q == 0, stop=q == NT - 1)
                        mm.then_inc(o_ready.sem, o_ready.up())
                pe.wait_ge(o_done.sem, o_done.at(N))
                for b in range(RB):
                    for t in range(NT):
                        mm = pe.transpose(k.ps[:, b, t * P:(t + 1) * P], y[:, t, b * P:(b + 1) * P], k.c("ident"))
                    mm.then_inc(y_ready.sem, y_ready.up())

            @block.vector
            def _(dve):
                for i in range(N + 2):
                    if i < N:
                        h, t = divmod(i, NT)
                        dve.wait_ge(s_ready.sem, s_ready.at(i + 1))
                        if i >= 2:
                            dve.wait_ge(p_ready.sem, p_ready.at(i - 1))
                        off = (6 - 2 * t) * GRID_W
                        dve.tensor_tensor(s_sb[:, i % 2, :], k.ps[:, i % 2, :],
                                          rel[:, h, off:off + T], ALU.add).then_inc(biased.sem, biased.up())
                        dve.wait_ge(biased.sem, biased.at(i + 1))
                        dve.tensor_reduce(stat[:, 0, i:i + 1], s_sb[:, i % 2, :], AX.X, ALU.max, negate=True).then_inc(chain.sem, chain.up())
                    if i >= 2:
                        j = i - 2
                        h, t = divmod(j, NT)
                        dve.wait_ge(p_ready.sem, p_ready.at(j + 1))
                        dve.reciprocal(stat[:, 2, j:j + 1], stat[:, 1, j:j + 1]).then_inc(k.sig("chain_w").sem, k.sig("chain_w").up())
                        dve.wait_ge(k.sig("chain_w").sem, k.sig("chain_w").last)
                        dve.wait_ge(o_ready.sem, o_ready.at(j + 1))
                        dve.tensor_scalar(y[:, t, h * HD:(h + 1) * HD], k.ps[:, 4 + j % 2, 0:HD],
                                          stat[:, 2, j:j + 1], None, ALU.mult).then_inc(o_done.sem, o_done.up())

            @block.scalar
            def _(act):
                for i in range(N + 1):
                    if i < N:
                        act.wait_ge(chain.sem, chain.at(i + 1))
                        if i >= 2:
                            act.wait_ge(t_ready.sem, t_ready.at(i - 1))
                        act.activation(p_sb[:, i % 2, :], s_sb[:, i % 2, :], ACT.Exp,
                                       bias=stat[:, 0, i:i + 1], accum_out=stat[:, 1, i:i + 1]).then_inc(p_ready.sem, p_ready.up())
                    if i >= 1:
                        j = i - 1
                        act.wait_ge(t_ready.sem, t_ready.at(j + 1))
                        if j >= 2:
                            act.wait_ge(o_ready.sem, o_ready.at(j - 1))
                        act.copy(pT[:, j % 2, :], k.ps[:, 2 + j % 2, :]).then_inc(pt_ready.sem, pt_ready.up())
                for b in range(RB):
                    act.wait_ge(y_ready.sem, y_ready.at(b + 1))
                    act.copy(yT[:, b, :], k.ps[:, b, :]).then_inc(y_copied.sem, y_copied.up())
        k.stage_end()


def stage_rwkv_in(k, h, rT, kT, vT, lora):
    with ExitStack() as st:
        keep = k.sb("keep", [P, 15], st)
        w = Split(k, st)
        with k.block() as block:
            kept, scaled, shifted = k.sig("kept"), k.sig("scaled"), k.sig("shifted")

            def dst(g):
                return [rT, kT, vT][g // 4][:, g % 4, :] if g < 12 else lora[:, g - 12, :]

            @block.tensor
            def _(pe):
                for g in range(15):
                    w.ready(pe, g)
                    if g >= 8:
                        pe.wait_ge(shifted.sem, shifted.at(2 * (g - 7)))
                    for kt in range(DB):
                        mm = product(pe, k.ps[:, g % 8, :], w.parts(g, kt * P, (kt + 1) * P), (h[0][:, kt, :], h[1][:, kt, :]),
                                     kt == 0, kt == DB - 1)
                    mm.then_inc(w.done.sem, w.done.up())

            @block.scalar
            def _(act):
                w.round(act, 0)
                act.wait_ge(kept.sem, kept.at(2))
                for g in range(15):
                    if g < 14:
                        w.round(act, g + 1)
                    w.wait(act, g)
                    act.activation(dst(g), k.ps[:, g % 8, :], ACT.Copy, scale=keep[:, g:g + 1]).then_inc(scaled.sem, scaled.up())

            @block.vector
            def _(dve):
                a, b = COL["mu_prev"][0], COL["mu_next"][0]
                dve.tensor_scalar(keep[:, :], k.cols[:, a:a + 15], -1.0, 1.0, ALU.mult, ALU.add).then_inc(kept.sem, kept.up())
                dve.wait_ge(kept.sem, kept.last)
                dve.tensor_tensor(keep[:, :], keep[:, :], k.cols[:, b:b + 15], ALU.subtract).then_inc(kept.sem, kept.up())
                w.rest(dve, 0)
                for g in range(15):
                    if g < 14:
                        w.rest(dve, g + 1)
                    dve.wait_ge(scaled.sem, scaled.at(g + 1))
                    src, out = k.ps[:, g % 8, :], dst(g)
                    dve.scalar_tensor_tensor(out[:, 1:], src[:, :T - 1], k.col("mu_prev", g),
                                             out[:, 1:], ALU.mult, ALU.add).then_inc(shifted.sem, shifted.up())
                    dve.wait_ge(shifted.sem, shifted.last)
                    dve.scalar_tensor_tensor(out[:, :T - 1], src[:, 1:], k.col("mu_next", g),
                                             out[:, :T - 1], ALU.mult, ALU.add).then_inc(shifted.sem, shifted.up())

            @block.sync
            def _(sp):
                k.stream(sp, 15)
        k.stage_end()


def solve_pe(k, pe, n, n_half, w):
    masked, y_ready, y_copied, z_ready, updated = (k.sig(x) for x in SOLVE)
    for h2 in range(2):
        pe.wait_ge(masked.sem, masked.at(h2 + 1))
        for j in range(n_half):
            mm = pe.matmul(k.ps[:, 2 + h2, j * P:(j + 1) * P], w["M"][:, h2 * n_half + j, :], k.c("ident"), start=True, stop=True)
        mm.then_inc(z_ready.sem, z_ready.up())
    for lv in range(1, LEVELS):
        for h2 in range(2):
            i = 2 * lv + h2
            pe.wait_ge(masked.sem, masked.at(i + 1))
            pe.wait_ge(updated.sem, updated.at(2 * i - 2))
            for j in range(n_half):
                h = h2 * n_half + j
                mm = pe.matmul(k.ps[:, h2, j * P:(j + 1) * P], w["M"][:, h, :], w["X"][:, h, :], start=True, stop=True)
            mm.then_inc(y_ready.sem, y_ready.up())
        for h2 in range(2):
            i = 2 * lv + h2
            pe.wait_ge(y_copied.sem, y_copied.at(i - 1))
            for j in range(n_half):
                h = h2 * n_half + j
                if lv < LEVELS - 1:
                    pe.matmul(k.ps[:, 2 + h2, j * P:(j + 1) * P], w["XT"][:, h, :], w["Y"][:, h, :], start=True, stop=True)
                mm = pe.matmul(k.ps[:, 4 + h2, j * P:(j + 1) * P], w["Y"][:, h, :], w["XT"][:, h, :], start=True, stop=True)
            mm.then_inc(z_ready.sem, z_ready.up())


SOLVE = ("solve_masked", "solve_y_ready", "solve_y_copied", "solve_z_ready", "solve_updated")


def solve_act(k, act, n_half, w):
    masked, y_ready, y_copied, z_ready, updated = (k.sig(x) for x in SOLVE)
    for i in range(2 * (LEVELS - 1)):
        h2 = i % 2
        act.wait_ge(y_ready.sem, y_ready.at(i + 1))
        act.copy(w["Y"][:, h2 * n_half:(h2 + 1) * n_half, :],
                 k.ps[:, h2, 0:n_half * P].rearrange("p (h t) -> p h t", t=P)).then_inc(y_copied.sem, y_copied.up())


def solve_pool(k, pool, n_half, w, lt, lower, ready):
    masked, y_ready, y_copied, z_ready, updated = (k.sig(x) for x in SOLVE)
    ready(pool)
    for i in range(2 * LEVELS):
        lv, h2 = divmod(i, 2)
        hs = slice(h2 * n_half, (h2 + 1) * n_half)
        if lv == 1:
            pool.wait_ge(z_ready.sem, z_ready.at(h2 + 1))
            pool.wait_ge(updated.sem, updated.at(2 * h2 + 1))
        elif lv:
            pool.wait_ge(y_ready.sem, y_ready.at(i - 3))
        a = CONST["level_b" if lower[h2] else "level_f"][0] + lv * P
        m = k.const[:, a:a + P].unsqueeze(1).broadcast_to([P, n_half, P])
        pool.tensor_tensor(w["M"][:, hs, :], lt(h2), m, ALU.mult).then_inc(masked.sem, masked.up())


def solve_dve(k, dve, n_half, w):
    masked, y_ready, y_copied, z_ready, updated = (k.sig(x) for x in SOLVE)
    one = k.c("ident").unsqueeze(1).broadcast_to([P, n_half, P])
    for i in range(2 * LEVELS):
        lv, h2 = divmod(i, 2)
        hs = slice(h2 * n_half, (h2 + 1) * n_half)
        if lv == 0:
            dve.wait_ge(masked.sem, masked.at(h2 + 1))
            dve.tensor_tensor(w["XT"][:, hs, :], one, w["M"][:, hs, :], ALU.subtract).then_inc(updated.sem, updated.up())
        dve.wait_ge(z_ready.sem, z_ready.at(i + 1))
        if lv:
            dve.wait_ge(updated.sem, updated.at(2 * i - 2))
        for bank, x in ((2 + h2, "X"), (4 + h2, "XT")):
            if (lv, x) in ((0, "XT"), (LEVELS - 1, "X")):
                continue
            z = k.ps[:, bank, 0:n_half * P].rearrange("p (h t) -> p h t", t=P)
            dve.tensor_tensor(w[x][:, hs, :], w[x][:, hs, :] if lv else one, z, ALU.subtract).then_inc(updated.sem, updated.up())


def stage_solve(k, w, n, lt, lower):
    with k.block() as block:
        @block.gpsimd
        def _(pool):
            solve_pool(k, pool, n // 2, w, lt, lower, lambda e: None)

        @block.tensor
        def _(pe):
            solve_pe(k, pe, n, n // 2, w)

        @block.scalar
        def _(act):
            solve_act(k, act, n // 2, w)

        @block.vector
        def _(dve):
            solve_dve(k, dve, n // 2, w)
    k.stage_end()


def stage_rwkv(k, rT, kT, vT, lora, yT):
    with ExitStack() as st:
        up = k.sb("w_up", [P, 3, RW], st)
        hsum = k.sb("hsum", [P, RB * 8], st)
        row = k.sb("rw_rows", [P, 4, RW], st)
        kkT = k.sb("kkT", [P, RB, T], st)
        aT = k.sb("aT", [P, RB, T], st)
        vt = k.sb("rw_v", [P, NT, RW], st)
        y = yT
        bonus = k.sb("bonus", [P, NT, RH], st)
        lora_prep(k, st, up, hsum, row, lora, rT, kT, vT, kkT, vt)
        M = k.sb("rw_state", [P, RB, HD], st)
        refs = k.sb("rw_refs", [P, 4, RB], st)
        for d, order in (("f", range(NT)), ("b", range(NT - 1, -1, -1))):
            stage_rwkv_dir(k, d, aT, lora, up, kT, rT, kkT, bonus, hsum)
            for n, c in enumerate(order):
                with ExitStack() as s2:
                    A = k.sb("rw_A", [P, RH, 4 * P], s2)
                    kr = k.sb("rw_kr", [P, RB, 2, P], s2)
                    tok = k.sb("rw_tok", [P, 2, RW], s2)
                    with ExitStack() as s3:
                        stage_rwkv_chunk(k, d, c, row, up, lora, aT, kT, rT, kkT, A, kr, tok, refs, s3)
                    w = {x: k.sb("rw_" + x, [P, RH, P], s2) for x in ("X", "XT")}
                    with ExitStack() as s3:
                        w["M"] = k.sb("rw_M", [P, RH, P], s3)
                        w["Y"] = k.sb("rw_Y", [P, RH, P], s3)
                        stage_solve(k, w, RH, lambda h2: A[:, 4 * h2:4 * h2 + 4, 0:P], (d == "b", d == "b"))
                    with ExitStack() as s3:
                        stage_rwkv_step(k, d, c, n, A, w["XT"], kr, tok, vt, M, refs, y, s3)
        stage_rwkv_out(k, y, vt, bonus, row, up, lora, yT, st)


def lora_prep(k, st, up, hsum, row, lora, rT, kT, vT, kkT, vt):
    with ExitStack() as s2:
        sq = k.sb("kk_sq", [P, RB, T], s2)
        with k.block() as block:
            got, squashed, scaled = k.sig("load"), k.sig("squashed"), k.sig("scaled")
            squared, summed, rooted, chain = (k.sig(x) for x in ("squared", "summed", "rooted", "chain_v"))
            v_ready, v_copied = k.sig("v_ready"), k.sig("v_copied")

            @block.sync
            def _(sp):
                for i, name in enumerate(("w_up", "a_up", "g_up")):
                    a, n = MAT[name]
                    sp.dma_start(up[:, i, :], k.dram["mats"][:, a:a + n]).then_inc(got.sem, got.up(16))
                a, n = MAT["hsum"]
                sp.dma_start(hsum[:, :], k.dram["mats"][:, a:a + n]).then_inc(got.sem, got.up(16))
                for i, name in enumerate(("w0_f", "w0_b", "lnx_g", "lnx_b")):
                    a, n = ROW[name]
                    sp.dma_start(row[:, i, :], k.dram["rows"][:, a:a + n].broadcast_to([P, n])).then_inc(got.sem, got.up(16))
                sp.wait_ge(got.sem, got.at(128))

            @block.scalar
            def _(act):
                act.activation(lora[:, 0, :], lora[:, 0, :], ACT.Tanh).then_inc(squashed.sem, squashed.up())
                act.activation(lora[:, 2, :], lora[:, 2, :], ACT.Sigmoid).then_inc(squashed.sem, squashed.up())
                for b in range(RB):
                    act.wait_ge(scaled.sem, scaled.at(b + 1))
                    act.activation(sq[:, b, :], kkT[:, b, :], ACT.Square).then_inc(squared.sem, squared.up())
                for b in range(RB):
                    act.wait_ge(summed.sem, summed.at(b + 1))
                    act.activation(sq[:, b, :], k.ps[:, b, :], ACT.Sqrt, bias=L2_EPS).then_inc(rooted.sem, rooted.up())

            @block.tensor
            def _(pe):
                for b in range(RB):
                    pe.wait_ge(squared.sem, squared.at(b + 1))
                    pe.matmul(k.ps[:, b, :], k.c("ones64"), sq[:, b, :], start=True, stop=True).then_inc(summed.sem, summed.up())
                for t in range(NT):
                    for b in range(RB):
                        mm = pe.transpose(k.ps[:, 4 + t, b * P:(b + 1) * P], vT[:, b, t * P:(t + 1) * P], k.c("ident"))
                    mm.then_inc(v_ready.sem, v_ready.up())

            @block.vector
            def _(dve):
                for b in range(RB):
                    dve.tensor_scalar(kkT[:, b, :], kT[:, b, :], k.col("k_k", b), None, ALU.mult).then_inc(scaled.sem, scaled.up())
                for b in range(RB):
                    dve.wait_ge(rooted.sem, rooted.at(b + 1))
                    dve.reciprocal(sq[:, b, :], sq[:, b, :]).then_inc(chain.sem, chain.up())
                    dve.wait_ge(chain.sem, chain.last)
                    dve.tensor_tensor(kkT[:, b, :], kkT[:, b, :], sq[:, b, :], ALU.mult).then_inc(chain.sem, chain.up())
                for t in range(NT):
                    dve.wait_ge(v_ready.sem, v_ready.at(t + 1))
                    dve.tensor_copy(vt[:, t, :], k.ps[:, 4 + t, :]).then_inc(v_copied.sem, v_copied.up())
        k.stage_end()


def stage_rwkv_dir(k, d, aT, lora, up, kT, rT, kkT, bonus, hsum):
    p0 = 0 if d == "f" else HD
    with ExitStack() as st:
        prod = k.sb("bonus_prod", [P, RB, T], st)
        ka1 = k.sb("ka1", [P, RB], st)
        with k.block() as block:
            a_ready, a_done, chain = k.sig("a_ready"), k.sig("a_done"), k.sig("chain_v")
            prod_done, b_ready, b_done = k.sig("prod_done"), k.sig("bonus_ready"), k.sig("bonus_done")

            @block.tensor
            def _(pe):
                for b in range(RB):
                    pe.matmul(k.ps[:, b, :], up[p0:p0 + HD, 1, b * P:(b + 1) * P],
                              lora[p0:p0 + HD, 1, :], start=True, stop=True).then_inc(a_ready.sem, a_ready.up())
                pe.wait_ge(prod_done.sem, prod_done.at(RB))
                for t in range(NT):
                    for b in range(RB):
                        mm = pe.matmul(k.ps[:, 4, t * 8:t * 8 + 8], prod[:, b, t * P:(t + 1) * P],
                                       hsum[:, b * 8:b * 8 + 8], start=b == 0, stop=b == RB - 1)
                mm.then_inc(b_ready.sem, b_ready.up())

            @block.scalar
            def _(act):
                for b in range(RB):
                    act.wait_ge(a_ready.sem, a_ready.at(b + 1))
                    act.activation(aT[:, b, :], k.ps[:, b, :], ACT.Sigmoid, bias=k.col("a0_" + d, b)).then_inc(a_done.sem, a_done.up())

            @block.vector
            def _(dve):
                a = COL["k_a"][0]
                dve.tensor_scalar(ka1[:, :], k.cols[:, a:a + RB], -1.0, 1.0, ALU.mult, ALU.add).then_inc(chain.sem, chain.up())
                dve.wait_ge(chain.sem, chain.last)
                for b in range(RB):
                    dve.wait_ge(a_done.sem, a_done.at(b + 1))
                    dve.tensor_scalar(prod[:, b, :], aT[:, b, :], k.col("k_a", b), ka1[:, b:b + 1],
                                      ALU.mult, ALU.add).then_inc(chain.sem, chain.up())
                    dve.wait_ge(chain.sem, chain.last)
                    dve.tensor_tensor(prod[:, b, :], prod[:, b, :], kT[:, b, :], ALU.mult).then_inc(chain.sem, chain.up())
                    dve.wait_ge(chain.sem, chain.last)
                    dve.scalar_tensor_tensor(prod[:, b, :], prod[:, b, :], k.col("r_k", b),
                                             rT[:, b, :], ALU.mult, ALU.mult).then_inc(prod_done.sem, prod_done.up())
                dve.wait_ge(b_ready.sem, b_ready.at(1))
                flat = bonus[:, :, :].rearrange("p t h -> p (t h)")
                if d == "f":
                    dve.tensor_copy(flat, k.ps[:, 4, 0:NT * 8]).then_inc(b_done.sem, b_done.up())
                else:
                    dve.tensor_tensor(flat, flat, k.ps[:, 4, 0:NT * 8], ALU.add).then_inc(b_done.sem, b_done.up())
        k.stage_end()


def stage_rwkv_chunk(k, d, c, row, up, lora, aT, kT, rT, kkT, A, kr, tok, refs, st):
    p0 = 0 if d == "f" else HD
    mid, end = (P // 2, P - 1) if d == "f" else (P // 2 - 1, 0)
    ts = slice(c * P, (c + 1) * P)
    lw = k.sb("rw_lw", [P, RW], st)
    ex = k.sb("rw_ex", [P, RB, 2, P], st)
    ek = k.sb("rw_ek", [P, RB, P], st)
    bk = k.sb("rw_bk", [P, 2, RB, P], st)
    kd = k.sb("rw_kd", [P, RB, P], st)
    ka1 = k.sb("rw_ka1", [P, RB], st)
    with k.block() as block:
        w_ready, w_biased, w_done = k.sig("w_ready"), k.sig("w_biased"), k.sig("w_done")
        g_ready, ref_done, ex_done, ends_done = k.sig("g_ready"), k.sig("ref_done"), k.sig("ex_done"), k.sig("ends_done")
        chain, kr_done, bk_done = k.sig("chain_v"), k.sig("kr_done"), k.sig("bk_done")
        s_ready, s_masked, t_ready, t_copied = k.sig("s_ready"), k.sig("s_masked"), k.sig("t_ready"), k.sig("t_copied")
        kd_done = k.sig("kd_done")

        @block.tensor
        def _(pe):
            pe.matmul(k.ps[:, 0, :], lora[p0:p0 + HD, 0, ts], up[p0:p0 + HD, 0, :], start=True, stop=True).then_inc(w_ready.sem, w_ready.up())
            pe.wait_ge(w_done.sem, w_done.at(1))
            for b in range(RB):
                mm = pe.matmul(k.ps[:, 1 + b // 2, (b % 2) * 256:(b % 2) * 256 + 256], lw[:, b * P:(b + 1) * P],
                               k.c("tri_" + d), start=True, stop=True)
            mm.then_inc(g_ready.sem, g_ready.up())
            pe.wait_ge(bk_done.sem, bk_done.at(2))
            for i in range(2):
                for b in range(RB):
                    mm = pe.transpose(k.ps[:, 3 + i, b * P:(b + 1) * P], bk[:, i, b, :], k.c("ident"))
                mm.then_inc(t_ready.sem, t_ready.up())
            pe.wait_ge(kr_done.sem, kr_done.at(2))
            for h in range(RH):
                a, b = HD * (h % 2), h // 2
                if h >= 3:
                    pe.wait_ge(s_masked.sem, s_masked.at(h - 2))
                bank = 5 + h % 3
                for i in range(2):
                    mm = pe.matmul(k.ps[:, bank, i * 256:(i + 1) * 256], bk[a:a + HD, i, b, :],
                                   kr[a:a + HD, b, :, :].rearrange("p i t -> p (i t)"), start=True, stop=True)
                mm.then_inc(s_ready.sem, s_ready.up())

        @block.scalar
        def _(act):
            act.wait_ge(w_biased.sem, w_biased.at(1))
            act.activation(lw[:, :], lw[:, :], ACT.Sigmoid).then_inc(w_done.sem, w_done.up())
            act.wait_ge(ref_done.sem, ref_done.at(2))
            for b in range(RB):
                g = k.ps[:, 1 + b // 2, (b % 2) * 256:(b % 2) * 256 + 256]
                act.activation(ex[:, b, :, :].rearrange("p i t -> p (i t)"), g, ACT.Exp,
                               scale=-DECAY, bias=refs[:, 1, b:b + 1]).then_inc(ex_done.sem, ex_done.up())
                act.activation(ek[:, b, :], g[:, 0:P], ACT.Exp, scale=DECAY, bias=refs[:, 0, b:b + 1]).then_inc(ex_done.sem, ex_done.up())
            act.activation(refs[:, 2, :], refs[:, 0, :], ACT.Exp).then_inc(ends_done.sem, ends_done.up())
            for i in range(2):
                act.wait_ge(t_ready.sem, t_ready.at(i + 1))
                act.copy(tok[:, i, :], k.ps[:, 3 + i, :]).then_inc(t_copied.sem, t_copied.up())

        @block.vector
        def _(dve):
            dve.wait_ge(w_ready.sem, w_ready.at(1))
            dve.tensor_tensor(lw[:, :], k.ps[:, 0, :], row[:, 0 if d == "f" else 1, :], ALU.add).then_inc(w_biased.sem, w_biased.up())
            dve.wait_ge(g_ready.sem, g_ready.at(1))
            gm = k.ps[:, 1:3, :].rearrange("p a (b n) -> p a b n", n=256)
            for i, f in ((0, -DECAY), (1, DECAY)):
                dve.tensor_scalar(refs[:, i, :].rearrange("p (a b) -> p a b", a=2), gm[:, :, :, mid],
                                  f, None, ALU.mult).then_inc(ref_done.sem, ref_done.up())
            dve.wait_ge(ex_done.sem, ex_done.at(2 * RB))
            dve.tensor_copy(refs[:, 3, :], ex[:, :, 0, end]).then_inc(ends_done.sem, ends_done.up())
            dve.tensor_tensor(kr[:, :, 0, :], kkT[:, :, ts], ex[:, :, 1, :], ALU.mult).then_inc(kr_done.sem, kr_done.up())
            dve.tensor_tensor(kr[:, :, 1, :], rT[:, :, ts], ex[:, :, 0, :], ALU.mult).then_inc(kr_done.sem, kr_done.up())
            for h in range(RH):
                dve.wait_ge(s_ready.sem, s_ready.at(h + 1))
                dve.tensor_tensor(A[:, h, :], k.ps[:, 5 + h % 3, :], k.c("attn_" + d), ALU.mult).then_inc(s_masked.sem, s_masked.up())

        @block.gpsimd
        def _(pool):
            a0 = COL["k_a"][0]
            pool.tensor_scalar(ka1[:, :], k.cols[:, a0:a0 + RB], -1.0, 1.0, ALU.mult, ALU.add).then_inc(kd_done.sem, kd_done.up())
            pool.wait_ge(kd_done.sem, kd_done.last)
            for b in range(RB):
                pool.tensor_scalar(kd[:, b, :], aT[:, b, ts], k.col("k_a", b), ka1[:, b:b + 1], ALU.mult, ALU.add).then_inc(kd_done.sem, kd_done.up())
            pool.wait_ge(kd_done.sem, kd_done.at(1 + RB))
            pool.tensor_tensor(kd[:, :, :], kd[:, :, :], kT[:, :, ts], ALU.mult).then_inc(kd_done.sem, kd_done.up())
            pool.wait_ge(kd_done.sem, kd_done.last)
            pool.tensor_tensor(bk[:, 0, :, :], kkT[:, :, ts], aT[:, :, ts], ALU.mult).then_inc(kd_done.sem, kd_done.up())
            pool.wait_ge(kd_done.sem, kd_done.last)
            pool.wait_ge(ex_done.sem, ex_done.at(2 * RB))
            pool.tensor_tensor(bk[:, 0, :, :], bk[:, 0, :, :], ek[:, :, :], ALU.mult).then_inc(bk_done.sem, bk_done.up())
            pool.tensor_tensor(bk[:, 1, :, :], kd[:, :, :], ek[:, :, :], ALU.mult).then_inc(bk_done.sem, bk_done.up())
    k.stage_end()


def stage_rwkv_step(k, d, c, n, A, XT, kr, tok, vt, M, refs, y, st):
    w_sb = k.sb("rw_w", [P, 2, RB, HD], st)
    u_sb = k.sb("rw_u", [P, RW], st)
    Ms = k.sb("rw_Ms", [P, RB, HD], st)
    with k.block() as block:
        scaled, w_ready, w_done, u_ready, u_done = (k.sig(x) for x in ("state_scaled", "w_ready", "w_done", "u_ready", "u_done"))
        y_ready, y_done, m_ready, m_done = (k.sig(x) for x in ("y_ready", "y_done", "m_ready", "m_done"))

        @block.tensor
        def _(pe):
            pe.wait_ge(scaled.sem, scaled.at(1))
            for h in range(RH):
                a, b = HD * (h % 2), h // 2
                out = k.ps[:, h % 2, b * HD:(b + 1) * HD]
                pe.matmul(out, kr[a:a + HD, b, 0, :], Ms[a:a + HD, b, :], start=True, stop=False)
                mm = pe.matmul(out, A[:, h, 2 * P:3 * P], vt[:, c, h * HD:(h + 1) * HD], start=False, stop=True)
            mm.then_inc(w_ready.sem, w_ready.up())
            pe.wait_ge(w_done.sem, w_done.at(1))
            for h in range(RH):
                hs = slice(h * HD, (h + 1) * HD)
                mm = pe.matmul(k.ps[:, 2, hs], XT[:, h, :], w_sb[:, h % 2, h // 2, :], start=True, stop=True)
            mm.then_inc(u_ready.sem, u_ready.up())
            pe.wait_ge(u_done.sem, u_done.at(1))
            for h in range(RH):
                a, b = HD * (h % 2), h // 2
                hs = slice(h * HD, (h + 1) * HD)
                pe.matmul(k.ps[a:a + HD, 3, b * HD:(b + 1) * HD], tok[:, 0, hs], u_sb[:, hs], start=True, stop=False)
                mm = pe.matmul(k.ps[a:a + HD, 3, b * HD:(b + 1) * HD], tok[:, 1, hs], vt[:, c, hs], start=False, stop=True)
            mm.then_inc(m_ready.sem, m_ready.up())
            for h in range(RH):
                a, b = HD * (h % 2), h // 2
                hs = slice(h * HD, (h + 1) * HD)
                out = k.ps[:, 4 + h % 2, b * HD:(b + 1) * HD]
                pe.matmul(out, kr[a:a + HD, b, 1, :], Ms[a:a + HD, b, :], start=True, stop=False)
                pe.matmul(out, A[:, h, P:2 * P], u_sb[:, hs], start=False, stop=False)
                mm = pe.matmul(out, A[:, h, 3 * P:4 * P], vt[:, c, hs], start=False, stop=True)
            mm.then_inc(y_ready.sem, y_ready.up())

        def halves(bank):
            return k.ps[:, bank:bank + 2, 0:RB * HD].rearrange("p i (b v) -> p i b v", v=HD)

        @block.scalar
        def _(act):
            act.wait_ge(w_ready.sem, w_ready.at(1))
            act.activation(w_sb[:, :, :, :], halves(0), ACT.Copy, scale=-1.0).then_inc(w_done.sem, w_done.up())
            act.wait_ge(u_ready.sem, u_ready.at(1))
            act.copy(u_sb[:, :], k.ps[:, 2, :]).then_inc(u_done.sem, u_done.up())

        @block.vector
        def _(dve):
            if n == 0:
                dve.memset(Ms[:, :, :], 0.0).then_inc(scaled.sem, scaled.up())
            else:
                dve.tensor_tensor(Ms[:, :, :], M[:, :, :],
                                  refs[:, 2, :].unsqueeze(2).broadcast_to([P, RB, HD]), ALU.mult).then_inc(scaled.sem, scaled.up())
            dve.wait_ge(m_ready.sem, m_ready.at(1))
            dve.wait_ge(scaled.sem, scaled.at(1))
            dve.tensor_tensor(M[:, :, :], Ms[:, :, :],
                              k.ps[:, 3, 0:RB * HD].rearrange("p (b v) -> p b v", v=HD), ALU.add).then_inc(m_done.sem, m_done.up())
            dve.wait_ge(m_done.sem, m_done.last)
            dve.tensor_tensor(M[:, :, :], M[:, :, :],
                              refs[:, 3, :].unsqueeze(2).broadcast_to([P, RB, HD]), ALU.mult).then_inc(m_done.sem, m_done.up())
            dve.wait_ge(y_ready.sem, y_ready.at(1))
            out = y[:, c, :].rearrange("p (b i v) -> p i b v", i=2, v=HD)
            if d == "f":
                dve.tensor_copy(out, halves(4)).then_inc(y_done.sem, y_done.up())
            else:
                dve.tensor_tensor(out, out, halves(4), ALU.add).then_inc(y_done.sem, y_done.up())
    k.stage_end()


def stage_rwkv_out(k, y, vt, bonus, row, up, lora, yT, st):
    sq = k.sb("gn_sq", [P, NT, RW], st)
    stat = k.sb("gn_stat", [P, 2, NT * RH], st)
    with k.block() as block:
        g_ready, chain, rooted, y_done, y_ready, y_copied, var_done = (
            k.sig(x) for x in ("g_ready", "chain_v", "rooted", "y_done", "y_ready", "y_copied", "var_done"))

        @block.tensor
        def _(pe):
            for t in range(NT):
                pe.matmul(k.ps[:, t, :], lora[:, 2, t * P:(t + 1) * P], up[:, 2, :], start=True, stop=True).then_inc(g_ready.sem, g_ready.up())
            pe.wait_ge(y_done.sem, y_done.at(NT))
            for b in range(RB):
                for t in range(NT):
                    mm = pe.transpose(k.ps[:, 4 + b, t * P:(t + 1) * P], y[:, t, b * P:(b + 1) * P], k.c("ident"))
                mm.then_inc(y_ready.sem, y_ready.up())

        @block.scalar
        def _(act):
            act.wait_ge(var_done.sem, var_done.at(1))
            act.activation(stat[:, 1, :], stat[:, 1, :], ACT.Sqrt, scale=1.0 / HD, bias=GN_EPS).then_inc(rooted.sem, rooted.up())
            act.wait_ge(y_ready.sem, y_ready.at(RB))
            for b in range(RB):
                act.copy(yT[:, b, :], k.ps[:, 4 + b, :]).then_inc(y_copied.sem, y_copied.up())

        @block.vector
        def _(dve):
            yh = y[:, :, :].rearrange("p t (h c) -> p (t h) c", c=HD)
            vh = vt[:, :, :].rearrange("p t (h c) -> p (t h) c", c=HD)
            sh = sq[:, :, :].rearrange("p t (h c) -> p (t h) c", c=HD)

            def wide(x):
                return x.unsqueeze(2).broadcast_to([P, NT * RH, HD])
            dve.tensor_reduce(stat[:, 0, :], yh, AX.X, ALU.add).then_inc(chain.sem, chain.up())
            dve.wait_ge(chain.sem, chain.last)
            dve.tensor_scalar(stat[:, 0, :], stat[:, 0, :], 1.0 / HD, None, ALU.mult).then_inc(chain.sem, chain.up())
            dve.wait_ge(chain.sem, chain.last)
            dve.tensor_tensor(yh, yh, wide(stat[:, 0, :]), ALU.subtract).then_inc(chain.sem, chain.up())
            dve.wait_ge(chain.sem, chain.last)
            dve.tensor_tensor(sh, yh, yh, ALU.mult).then_inc(chain.sem, chain.up())
            dve.wait_ge(chain.sem, chain.last)
            dve.tensor_reduce(stat[:, 1, :], sh, AX.X, ALU.add).then_inc(var_done.sem, var_done.up())
            dve.wait_ge(rooted.sem, rooted.at(1))
            dve.reciprocal(stat[:, 1, :], stat[:, 1, :]).then_inc(chain.sem, chain.up())
            dve.wait_ge(chain.sem, chain.last)
            dve.tensor_tensor(yh, yh, wide(stat[:, 1, :]), ALU.mult).then_inc(chain.sem, chain.up())
            dve.wait_ge(chain.sem, chain.last)
            dve.tensor_tensor(y[:, :, :], y[:, :, :], row[:, 2:3, :].broadcast_to([P, NT, RW]), ALU.mult).then_inc(chain.sem, chain.up())
            dve.wait_ge(chain.sem, chain.last)
            dve.tensor_tensor(y[:, :, :], y[:, :, :], row[:, 3:4, :].broadcast_to([P, NT, RW]), ALU.add).then_inc(chain.sem, chain.up())
            dve.wait_ge(chain.sem, chain.last)
            dve.tensor_tensor(sh, vh, wide(bonus[:, :, :].rearrange("p t h -> p (t h)")), ALU.mult).then_inc(chain.sem, chain.up())
            dve.wait_ge(chain.sem, chain.last)
            dve.tensor_tensor(y[:, :, :], y[:, :, :], sq[:, :, :], ALU.add).then_inc(chain.sem, chain.up())
            dve.wait_ge(chain.sem, chain.last)
            dve.wait_ge(g_ready.sem, g_ready.at(NT))
            for t in range(NT):
                dve.tensor_tensor(y[:, t, :], y[:, t, :], k.ps[:, t, :], ALU.mult).then_inc(y_done.sem, y_done.up())
    k.stage_end()


def stage_merge(k, h, yaT, ybT, mod_part):
    MB = 4
    M_UNITS, C_UNITS = MG * DB, 2 * DB
    with ExitStack() as st:
        wm = k.sb("w_mod_ring", [P, MB, UNIT], st)
        g = k.sb("gates", [P, 16, T], st)
        yab = mix = h
        w = Split(k, st)
        with k.block() as block:
            g_done, m_done, h_done, x_done = k.sig("g_done"), k.sig("mix_done"), k.sig("half_done"), k.sig("x_done")
            y_rounded, y_rested, rounded, rested = (k.sig(x) for x in ("y_rounded", "y_rested", "rounded", "rested"))
            mod_seq, mod_ctx = k.sig("mod_summed"), k.sig("mod_summed_context")
            mod_in = [k.sig(f"mod_landed{i}") for i in range(MB)]

            @block.tensor
            def _(pe):
                for i in range(16):
                    w.ready(pe, i)
                    if i >= 8:
                        pe.wait_ge(g_done.sem, g_done.at(i - 7))
                    for kt in range(DB):
                        mm = product(pe, k.ps[:, i % 8, :], w.parts(i, kt * P, (kt + 1) * P), (h[0][:, kt, :], h[1][:, kt, :]),
                                     kt == 0, kt == DB - 1)
                    mm.then_inc(w.done.sem, w.done.up())
                for i in range(8):
                    w.ready(pe, 16 + i)
                    pe.wait_ge(g_done.sem, g_done.at(10 + 2 * (i % 4)))
                    if i >= 4:
                        pe.wait_ge(m_done.sem, m_done.at(i - 3))
                    for j in range(2):
                        for kt in range(4):
                            if i == 0:
                                pe.wait_ge(y_rested.sem, y_rested.at(4 * j + kt + 1))
                            mm = product(pe, k.ps[:, 2 * (i % 4) + j, :], w.parts(16 + i, (4 * j + kt) * P, (4 * j + kt + 1) * P),
                                         (yab[0][:, 4 * j + kt, :], yab[1][:, 4 * j + kt, :]), kt == 0, kt == 3)
                    mm.then_inc(w.done.sem, w.done.up())
                pe.wait_ge(m_done.sem, m_done.at(8))
                for i in range(8):
                    w.ready(pe, 24 + i)
                    for kt in range(DB):
                        if i == 0:
                            pe.wait_ge(rested.sem, rested.at(kt + 1))
                        mm = product(pe, k.ps[:, i, :], w.parts(24 + i, kt * P, (kt + 1) * P), (mix[0][:, kt, :], mix[1][:, kt, :]),
                                     kt == 0, kt == DB - 1)
                    mm.then_inc(w.done.sem, w.done.up())

            @block.scalar
            def _(act):
                def load(u):
                    if u >= MB:
                        act.wait_ge(mod_seq.sem, mod_seq.at(u - MB + 1))
                        if u - MB < C_UNITS:
                            act.wait_ge(mod_ctx.sem, mod_ctx.at(u - MB + 1))
                    act.dma_start(wm[:, u % MB, :], k.dram["w_mod"][u]).then_inc(mod_in[u % MB].sem, mod_in[u % MB].up(16))

                w.round(act, 0)
                for i in range(16):
                    w.round(act, i + 1)
                    load(2 * i)
                    load(2 * i + 1)
                    w.wait(act, i)
                    act.activation(g[:, i, :], k.ps[:, i % 8, :], ACT.Sigmoid, bias=k.col("b_gate", i)).then_inc(g_done.sem, g_done.up())
                for b in range(DB):
                    act.copy(yab[0][:, b, :], (yaT if b < 4 else ybT)[:, b % 4, :]).then_inc(y_rounded.sem, y_rounded.up())
                for i in range(8):
                    load(32 + 2 * i)
                    load(33 + 2 * i)
                    w.round(act, 17 + i)
                w.wait(act, 23)
                for i in range(8):
                    act.wait_ge(m_done.sem, m_done.at(i + 1))
                    act.copy(mix[0][:, i, :], g[:, i, :]).then_inc(rounded.sem, rounded.up())
                for i in range(25, 32):
                    w.round(act, i)

            def mod_sum(eng, done, u, part, which):
                eng.wait_ge(mod_in[u % MB].sem, mod_in[u % MB].at(16 * (u // MB + 1)))
                c = k.silu_c[:, u % DB, which:which + 1]
                if u % DB == 0:
                    eng.tensor_scalar(part, wm[:, u % MB, :], c, None, ALU.mult).then_inc(done.sem, done.up())
                else:
                    eng.wait_ge(done.sem, done.at(u))
                    eng.scalar_tensor_tensor(part, wm[:, u % MB, :], c, part, ALU.mult, ALU.add).then_inc(done.sem, done.up())

            @block.gpsimd
            def _(pool):
                for b in range(DB):
                    pool.wait_ge(y_rounded.sem, y_rounded.at(b + 1))
                    pool.tensor_tensor(yab[1][:, b, :], (yaT if b < 4 else ybT)[:, b % 4, :], yab[0][:, b, :],
                                       ALU.subtract).then_inc(y_rested.sem, y_rested.up())
                for i in range(8):
                    pool.wait_ge(rounded.sem, rounded.at(i + 1))
                    pool.tensor_tensor(mix[1][:, i, :], g[:, i, :], mix[0][:, i, :], ALU.subtract).then_inc(rested.sem, rested.up())

            @block.vector
            def _(dve):
                w.rest(dve, 0)
                for i in range(16):
                    w.rest(dve, i + 1)
                    for u in (2 * i, 2 * i + 1):
                        mod_sum(dve, mod_seq, u, mod_part[:, u // DB, :], 0)
                        if u < C_UNITS:
                            mod_sum(dve, mod_ctx, u, mod_part[:, MG + u // DB, :], 1)
                for i in range(8):
                    w.rest(dve, 17 + i)
                    u = 32 + 2 * i
                    mod_sum(dve, mod_seq, u, mod_part[:, u // DB, :], 0)
                    mod_sum(dve, mod_seq, u + 1, mod_part[:, u // DB, :], 0)
                    w.wait(dve, 16 + i)
                    for j in range(2):
                        dve.tensor_tensor(g[:, 8 * j + i, :], g[:, 8 * j + i, :], k.ps[:, 2 * (i % 4) + j, :], ALU.mult).then_inc(h_done.sem, h_done.up())
                    dve.wait_ge(h_done.sem, h_done.at(2 * i + 2))
                    dve.tensor_tensor(g[:, i, :], g[:, i, :], g[:, 8 + i, :], ALU.add).then_inc(m_done.sem, m_done.up())
                for i in range(8):
                    if i < 7:
                        w.rest(dve, 25 + i)
                    w.wait(dve, 24 + i)
                    dve.tensor_tensor(k.xT[:, i, :], k.xT[:, i, :], k.ps[:, i, :], ALU.add).then_inc(x_done.sem, x_done.up())

            @block.sync
            def _(sp):
                k.stream(sp, 32)
        k.stage_end()


def stage_router(k, hT, comb, hot, wt):
    with ExitStack() as st:
        wr = k.sb("w_router", [P, DB, 36], st)
        br = k.sb("b_router", [P, 36], st)
        gidx = k.sb("gidx", [P, 12], st)
        lg = k.sb("logits", [P, NT, 36], st)
        small = k.sb("router_small", [P, 8, NT], st)
        g4 = k.sb("router_g4", [P, 3, NT, 4], st)
        e8 = k.sb("router_e8", [P, 5, NT, 8], st)
        pick = k.sb("router_pick", [P, NT * 4, 8], st)
        with k.block() as block:
            got, l_ready, chain = k.sig("load"), k.sig("l_ready"), k.sig("chain_v")
            diff_done, exp_done = k.sig("diff_done"), k.sig("exp_done")

            @block.sync
            def _(sp):
                for dst, src in ((wr[:, :, :].rearrange("p b n -> p (b n)"), ("mats", MAT["router"])),
                                 (gidx[:, :], ("mats", MAT["gidx"]))):
                    a, n = src[1]
                    sp.dma_start(dst, k.dram["mats"][:, a:a + n]).then_inc(got.sem, got.up(16))
                a, n = ROW["b_router"]
                sp.dma_start(br[:, :], k.dram["rows"][:, a:a + n].broadcast_to([P, n])).then_inc(got.sem, got.up(16))

            @block.tensor
            def _(pe):
                pe.wait_ge(got.sem, got.at(48))
                for t in range(NT):
                    for b in range(DB):
                        mm = pe.matmul(k.ps[:, 0, t * 36:(t + 1) * 36], hT[:, b, t * P:(t + 1) * P], wr[:, b, :],
                                       start=b == 0, stop=b == DB - 1)
                mm.then_inc(l_ready.sem, l_ready.up())

            @block.scalar
            def _(act):
                act.wait_ge(diff_done.sem, diff_done.at(1))
                act.activation(g4[:, 0, :, :], g4[:, 0, :, :], ACT.Exp).then_inc(exp_done.sem, exp_done.up())
                act.wait_ge(diff_done.sem, diff_done.at(2))
                act.activation(small[:, 4, :], small[:, 4, :], ACT.Exp).then_inc(exp_done.sem, exp_done.up())

            @block.vector
            def _(dve):
                def go(ins):
                    ins.then_inc(chain.sem, chain.up())
                    dve.wait_ge(chain.sem, chain.last)

                def over(x, n):
                    return x.unsqueeze(2).broadcast_to([P, NT, n])

                def one_hot(out, values, top, order, n):
                    go(dve.tensor_tensor(out, values, over(top, n), ALU.is_equal))
                    go(dve.tensor_tensor(out, out, order.unsqueeze(1).broadcast_to([P, NT, n]), ALU.mult))
                    go(dve.tensor_reduce(small[:, 7, :], out, AX.X, ALU.max))
                    go(dve.tensor_tensor(out, out, over(small[:, 7, :], n), ALU.is_equal))

                dve.wait_ge(got.sem, got.at(48))
                dve.wait_ge(l_ready.sem, l_ready.at(1))
                go(dve.tensor_tensor(lg[:, :, :], k.ps[:, 0, 0:NT * 36].rearrange("p (t n) -> p t n", n=36),
                                     br[:, :].unsqueeze(1).broadcast_to([P, NT, 36]), ALU.add))
                gmax, gsum, v1, v2, ediff = (small[:, i, :] for i in range(5))
                w1, w2 = wt[:, 0, :], wt[:, 1, :]
                go(dve.tensor_reduce(gmax, lg[:, :, 0:4], AX.X, ALU.max))
                dve.tensor_tensor(g4[:, 0, :, :], lg[:, :, 0:4], over(gmax, 4), ALU.subtract).then_inc(diff_done.sem, diff_done.up())
                one_hot(g4[:, 1, :, :], lg[:, :, 0:4], gmax, gidx[:, 0:4], 4)
                dve.wait_ge(exp_done.sem, exp_done.at(1))
                go(dve.tensor_reduce(gsum, g4[:, 0, :, :], AX.X, ALU.add))
                go(dve.reciprocal(gsum, gsum))
                go(dve.tensor_copy(pick[:, :, :].rearrange("p (t g) e -> p t (g e)", g=4), lg[:, :, 4:36]))
                group = g4[:, 1, :, :].rearrange("p t g -> p (t g)").unsqueeze(2).broadcast_to([P, NT * 4, 8])
                go(dve.tensor_tensor(pick[:, :, :], pick[:, :, :], group, ALU.mult))
                go(dve.tensor_reduce(e8[:, 0, :, :], pick[:, :, :].rearrange("p (t g) e -> p t e g", g=4), AX.X, ALU.add))
                go(dve.tensor_reduce(v1, e8[:, 0, :, :], AX.X, ALU.max))
                one_hot(e8[:, 1, :, :], e8[:, 0, :, :], v1, gidx[:, 4:12], 8)
                go(dve.tensor_scalar(e8[:, 3, :, :], e8[:, 1, :, :], -1e30, None, ALU.mult))
                go(dve.tensor_tensor(e8[:, 3, :, :], e8[:, 3, :, :], e8[:, 0, :, :], ALU.add))
                go(dve.tensor_reduce(v2, e8[:, 3, :, :], AX.X, ALU.max))
                one_hot(e8[:, 2, :, :], e8[:, 3, :, :], v2, gidx[:, 4:12], 8)
                dve.tensor_tensor(ediff, v2, v1, ALU.subtract).then_inc(diff_done.sem, diff_done.up())
                dve.wait_ge(exp_done.sem, exp_done.at(2))
                go(dve.tensor_scalar(w1, ediff, 1.0, None, ALU.add))
                go(dve.reciprocal(w1, w1))
                go(dve.tensor_tensor(w1, w1, gsum, ALU.mult))
                go(dve.tensor_tensor(w2, w1, ediff, ALU.mult))
                for n in range(2):
                    for g in range(4):
                        go(dve.tensor_tensor(hot[:, n, :, g * 8:(g + 1) * 8], e8[:, 1 + n, :, :],
                                             over(g4[:, 1, :, g], 8), ALU.mult))
                go(dve.tensor_tensor(e8[:, 1, :, :], e8[:, 1, :, :], over(w1, 8), ALU.mult))
                go(dve.tensor_tensor(e8[:, 2, :, :], e8[:, 2, :, :], over(w2, 8), ALU.mult))
                go(dve.tensor_tensor(e8[:, 1, :, :], e8[:, 1, :, :], e8[:, 2, :, :], ALU.add))
                for g in range(4):
                    go(dve.tensor_tensor(comb[:, :, g * 8:(g + 1) * 8], e8[:, 1, :, :], over(g4[:, 1, :, g], 8), ALU.mult))
        k.stage_end()


def stage_dispatch(k, hT, hot, slot_row, slot_tok, count):
    with ExitStack() as st:
        both = k.sb("hot_both", [P, NT, NE], st)
        work = k.sb("hot_work", [P, 2, NT, NE], st)
        pos = k.sb("slot_pos", [P, NT, NE], st)
        where = k.sb("slot_where", [P, 2, 2 * NT], st)
        flat = k.sb("slot_flat", [P, 2 * NT], st, U32)
        vals = k.sb("slot_vals", [P, 2 * NT + NE], st)
        empty = k.sb("slot_empty", [P, NE], st)
        table = k.sb("slot_table", [P, 2, NE], st)
        cnt = k.sb("slot_cnt", [P, 1], st)
        h_tok = k.sb("h_by_token", [P, NT, D], st)
        with k.block() as block:
            got, chain, both_done, pos_ready, flat_done = (k.sig(x) for x in ("load", "chain_v", "both_done", "pos_ready", "flat_done"))
            blank, cleared, put, back, h_ready, h_saved = (k.sig(x) for x in ("blank", "cleared", "put", "back", "h_ready", "h_saved"))
            h_done = [k.sig("turned_act"), k.sig("turned_dve")]

            @block.sync
            def _(sp):
                a, n = MAT["slot_vals"]
                sp.dma_start(vals[:, :], k.dram["mats"][:, a:a + n]).then_inc(got.sem, got.up(16))
                for t in range(NT):
                    for i in range(2):
                        sp.wait_ge(h_done[i].sem, h_done[i].at(t + 1))
                    sp.dma_start(k.dram["h_tok"][t * P:(t + 1) * P, :], h_tok[:, t, :]).then_inc(h_saved.sem, h_saved.up(16))
                sp.wait_ge(h_saved.sem, h_saved.at(16 * NT))

            @block.tensor
            def _(pe):
                pe.wait_ge(both_done.sem, both_done.at(1))
                tri = k.c("tri_f")[:, P:2 * P]
                for t in range(NT):
                    mm = pe.matmul(k.ps[:, 0, t * NE:(t + 1) * NE], tri, both[:, t, :], start=True, stop=t == 0)
                    for u in range(t):
                        mm = pe.matmul(k.ps[:, 0, t * NE:(t + 1) * NE], k.c("ones"), both[:, u, :], start=False, stop=u == t - 1)
                for u in range(NT):
                    mm = pe.matmul(k.ps[:, 0, NT * NE:(NT + 1) * NE], k.c("ones"), both[:, u, :], start=u == 0, stop=u == NT - 1)
                mm.then_inc(pos_ready.sem, pos_ready.up())
                for t in range(NT):
                    for i in range(2):
                        if t >= 3:
                            pe.wait_ge(h_done[i].sem, h_done[i].at(t - 2))
                        for b in range(4):
                            mm = pe.transpose(k.ps[:, 1 + 2 * (t % 3) + i, b * P:(b + 1) * P],
                                              hT[:, 4 * i + b, t * P:(t + 1) * P], k.c("ident"))
                        mm.then_inc(h_ready.sem, h_ready.up())

            @block.scalar
            def _(act):
                for t in range(NT):
                    act.wait_ge(h_ready.sem, h_ready.at(2 * t + 1))
                    act.copy(h_tok[:, t, 0:512], k.ps[:, 1 + 2 * (t % 3), :]).then_inc(h_done[0].sem, h_done[0].up())

            @block.vector
            def _(dve):
                def go(ins):
                    ins.then_inc(chain.sem, chain.up())
                    dve.wait_ge(chain.sem, chain.last)

                dve.memset(empty[:, :], float(NO_ROW)).then_inc(blank.sem, blank.up())
                dve.tensor_tensor(both[:, :, :], hot[:, 0, :, :], hot[:, 1, :, :], ALU.add).then_inc(both_done.sem, both_done.up())
                dve.wait_ge(got.sem, got.at(16))
                dve.wait_ge(pos_ready.sem, pos_ready.at(1))
                go(dve.tensor_copy(pos[:, :, :], k.ps[:, 0, 0:NT * NE].rearrange("p (t e) -> p t e", e=NE)))
                go(dve.tensor_reduce(cnt[:, :], k.ps[:, 0, NT * NE:(NT + 1) * NE], AX.X, ALU.max))
                go(dve.tensor_copy(count[:, :], cnt[:, :]))
                number = vals[:, 2 * NT:2 * NT + NE].unsqueeze(1).broadcast_to([P, NT, NE])
                for i, other in enumerate((pos[:, :, :], number)):
                    for pick in range(2):
                        go(dve.tensor_tensor(work[:, pick, :, :], hot[:, pick, :, :], other, ALU.mult))
                    go(dve.tensor_reduce(where[:, i, :].rearrange("p (a t) -> p a t", a=2), work[:, :, :, :], AX.X, ALU.add))
                go(dve.scalar_tensor_tensor(where[:, 0, :], where[:, 0, :], float(NE), where[:, 1, :], ALU.mult, ALU.add))
                dve.tensor_copy(flat[:, :], where[:, 0, :]).then_inc(flat_done.sem, flat_done.up())
                for t in range(NT):
                    dve.wait_ge(h_ready.sem, h_ready.at(2 * t + 2))
                    dve.tensor_copy(h_tok[:, t, 512:D], k.ps[:, 2 + 2 * (t % 3), :]).then_inc(h_done[1].sem, h_done[1].up())
                dve.wait_ge(back.sem, back.at(16))
                go(dve.tensor_copy(slot_row[:, :], table[:, 0, :]))
                go(dve.tensor_scalar(table[:, 1, :], table[:, 0, :], float(T), -float(T), ALU.is_ge, ALU.mult))
                go(dve.tensor_tensor(table[:, 1, :], table[:, 1, :], table[:, 0, :], ALU.add))
                go(dve.tensor_copy(slot_tok[:, :], table[:, 1, :]))

            @block.gpsimd
            def _(pool):
                slots = k.dram["slots"]
                pool.wait_ge(blank.sem, blank.at(1))
                pool.dma_start(slots.rearrange("(s e) one -> s (e one)", e=NE), empty[:, :]).then_inc(cleared.sem, cleared.up(16))
                pool.wait_ge(cleared.sem, cleared.at(16))
                pool.wait_ge(flat_done.sem, flat_done.at(1))
                for i in range(2 * NT):
                    pool.indirect_dma_start(slots, bass.IndirectOffsetOnAxis(flat[:, i:i + 1], 0), vals[:, i:i + 1], None,
                                            bounds_check=P * NE - 1, oob_is_err=False).then_inc(put.sem, put.up(16))
                pool.wait_ge(put.sem, put.at(16 * 2 * NT))
                pool.dma_start(table[:, 0, :], slots.rearrange("(s e) one -> s (e one)", e=NE)).then_inc(back.sem, back.up(16))
        k.stage_end()


def stage_moe(k, hT, comb, acc, slot_row, slot_tok, count, wt):
    PER, UPE = 4, 6
    U = PER * UPE
    ROUNDS = NE // PER
    first = STREAM["moe"][0]
    FULL = P + 1
    with ExitStack() as st:
        sg = k.sb("moe_silu", [P, 2, T], st)
        heT = k.sb("moe_he", [P, 2, 2, T], st)
        rows = k.sb("sp_rows", [P, 2, D], st)
        rowsT = k.sb("sp_rowsT", [P, 2, D], st)
        he = k.sb("sp_he", [P, 2, 256], st)
        sgs = k.sb("sp_silu", [P, 2, 256], st)
        hesT = k.sb("sp_heT", [P, 2, 256], st)
        ys = k.sb("sp_y", [P, 2, D], st)
        yy = k.sb("sp_picks", [P, 2, 2, D], st)
        with k.block() as block:
            silu_done, he_done, d_ready, acc_done = (k.sig("dense_" + x) for x in ("silu_done", "he_done", "down_ready", "acc_done"))
            filled, t_ready, t_copied_a, t_copied_v, s_done, h_done, ht_ready, ht_copied, y_done_a, y_done_v, summed = (
                k.sig("own_" + x) for x in ("filled", "t_ready", "t_copied_a", "t_copied_v", "silu_done", "he_done",
                                            "ht_ready", "ht_copied", "y_done_a", "y_done_v", "summed"))
            gathered, scattered, picks = ([k.sig(f"own_{x}{i}") for i in range(2)] for x in ("gathered", "scattered", "picks"))
            assert k.taken == first and first > 2 * UPE
            assert all(s.base == 0 for n, s in k.signals.items() if n.startswith(("own_", "dense_")))

            def rounds(eng, body):
                with eng.Fori(0, ROUNDS) as r:
                    for j in range(PER):
                        body(r, j)

            @block.sync
            def _(sp):
                with sp.Fori(0, ROUNDS) as r:
                    for i in range(U):
                        sp.wait_ge(k.used, r * U + (first + i + 1))
                        s = (first + i) % RING
                        sp.dma_start(k.ring[:, s, :], k.dram["stream"][bass.ds(r * U + (first + RING + i), 1)]
                                     .rearrange("a p n -> (a p) n")).then_inc(k.landed[s], 16)
                k.issued += ROUNDS * U
                few = sp.value_load(count[0:1, 0:1], min_val=0, max_val=T)
                with sp.If(few < FULL):
                    for i in range(2):
                        sp.wait_ge(scattered[i].sem, 16 + 16 * NE // 2)
                    for t in range(NT):
                        if t >= 2:
                            sp.wait_ge(summed.sem, 2 * (t - 1))
                        sp.dma_start(yy[:, t % 2, :, :], k.dram["picks"].rearrange("(a t p) n -> t p a n", a=2, p=P)[t]
                                     ).then_inc(picks[t % 2].sem, 16)

            @block.tensor
            def _(pe):
                def landed(r, u):
                    return r * (16 * U // RING) + 16 * (u // RING + 1)

                def own(r, j):
                    for u4 in range(4):
                        u = first + j * UPE + u4
                        pe.wait_ge(k.landed[u % RING], landed(r, u))
                        w = k.ring[:, u % RING, :]
                        if u4 == 0:
                            pe.wait_ge(t_copied_a.sem, r * PER + (j + 1))
                            pe.wait_ge(t_copied_v.sem, r * PER + (j + 1))
                            pe.wait_ge(h_done.sem, r * PER + (j + 1))
                        for kk in range(2):
                            kt = 2 * u4 + kk
                            mm = pe.matmul(k.ps[:, 0, :], rowsT[:, j % 2, kt * P:(kt + 1) * P], w[:, kk * 512:(kk + 1) * 512],
                                           start=kt == 0, stop=kt == DB - 1)
                        mm.then_inc(k.used, 1)
                    pe.wait_ge(gathered[(j + 1) % 2].sem, r * (8 * PER) + 16 * ((j + 1) // 2 + 1))
                    turn((j + 1) % 2)
                    pe.wait_ge(h_done.sem, r * PER + (j + 2))
                    pe.wait_ge(ht_copied.sem, r * PER + (j + 1))
                    for f in range(2):
                        mm = pe.transpose(k.ps[:, 3, f * P:(f + 1) * P], he[:, j % 2, f * P:(f + 1) * P], k.c("ident"))
                    mm.then_inc(ht_ready.sem, 1)
                    pe.wait_ge(ht_copied.sem, r * PER + (j + 2))
                    for f in range(2):
                        u = first + j * UPE + 4 + f
                        pe.wait_ge(k.landed[u % RING], landed(r, u))
                        w = k.ring[:, u % RING, :]
                        for n in range(2):
                            if f == 0:
                                done = (y_done_a, y_done_v)[n]
                                pe.wait_ge(done.sem, r * PER + (j + 1))
                            mm = pe.matmul(k.ps[:, 4 + 2 * (j % 2) + n, :], hesT[:, j % 2, f * P:(f + 1) * P],
                                           w[:, n * 512:(n + 1) * 512], start=f == 0, stop=f == 1)
                        mm.then_inc(k.used, 1)

                def turn(buf):
                    for i in range(2):
                        for b in range(4):
                            mm = pe.transpose(k.ps[:, 1 + i, b * P:(b + 1) * P], rows[:, buf, (4 * i + b) * P:(4 * i + b + 1) * P],
                                              k.c("ident"))
                        mm.then_inc(t_ready.sem, 1)

                def dense(r, j):
                    for u4 in range(4):
                        u = first + j * UPE + u4
                        pe.wait_ge(k.landed[u % RING], landed(r, u))
                        w = k.ring[:, u % RING, :]
                        if u4 == 0:
                            pe.wait_ge(he_done.sem, r * (2 * PER) + (2 * j + 2))
                        for kk in range(2):
                            kt = 2 * u4 + kk
                            for g in range(4):
                                mm = pe.matmul(k.ps[:, g, :], w[:, kk * 512 + g * P:kk * 512 + (g + 1) * P], hT[:, kt, :],
                                               start=kt == 0, stop=kt == DB - 1)
                        mm.then_inc(k.used, 1)
                    for half in range(2):
                        for f in range(2):
                            u = first + j * UPE + 4 + f
                            pe.wait_ge(k.landed[u % RING], landed(r, u))
                            w = k.ring[:, u % RING, :]
                            pe.wait_ge(he_done.sem, r * (2 * PER) + (2 * j + f + 3))
                            for i in range(4):
                                t, n = divmod(4 * half + i, 2)
                                if f == 0:
                                    pe.wait_ge(acc_done.sem, r * (8 * PER) + (8 * j + 4 * half + i + 5))
                                mm = pe.matmul(k.ps[:, 4 + i, :], heT[:, j % 2, f, t * P:(t + 1) * P],
                                               w[:, n * 512:(n + 1) * 512], start=f == 0, stop=f == 1)
                                if f == 1 and (half, i) != (1, 3):
                                    mm.then_inc(d_ready.sem, 1)
                                elif (half, i) == (1, 3):
                                    mm.then_inc(k.used, 1)

                few = pe.value_load(count[0:1, 0:1], min_val=0, max_val=T)
                with pe.If(few < FULL):
                    pe.wait_ge(gathered[0].sem, 16)
                    turn(0)
                    rounds(pe, own)
                with pe.Else():
                    rounds(pe, dense)
                k.taken += ROUNDS * U

            @block.scalar
            def _(act):
                def own(r, j):
                    act.wait_ge(k.used, r * U + (first + j * UPE + 4))
                    act.wait_ge(h_done.sem, r * PER + (j + 1))
                    act.activation(sgs[:, j % 2, :], k.ps[:, 0, 0:256], ACT.Silu).then_inc(s_done.sem, 1)
                    copy_turned(r, j + 1)
                    act.wait_ge(ht_ready.sem, r * PER + (j + 1))
                    act.copy(hesT[:, j % 2, :], k.ps[:, 3, 0:256]).then_inc(ht_copied.sem, 1)
                    act.wait_ge(k.used, r * U + (first + (j + 1) * UPE))
                    act.wait_ge(scattered[j % 2].sem, r * (8 * PER) + 16 * (j // 2) + 16)
                    act.copy(ys[:, j % 2, 0:512], k.ps[:, 4 + 2 * (j % 2), :]).then_inc(y_done_a.sem, 1)

                def copy_turned(r, j):
                    act.wait_ge(t_ready.sem, r * (2 * PER) + (2 * j + 1))
                    act.copy(rowsT[:, j % 2, 0:512], k.ps[:, 1, :]).then_inc(t_copied_a.sem, 1)

                def dense(r, j):
                    for f in range(2):
                        act.wait_ge(k.used, r * U + (first + j * UPE + 4))
                        act.wait_ge(he_done.sem, r * (2 * PER) + (2 * j + f + 1))
                        act.activation(sg[:, f, :], k.ps[:, f, :], ACT.Silu).then_inc(silu_done.sem, 1)

                few = act.value_load(count[0:1, 0:1], min_val=0, max_val=T)
                with act.If(few < FULL):
                    copy_turned(0, 0)
                    rounds(act, own)
                with act.Else():
                    rounds(act, dense)

            @block.vector
            def _(dve):
                def own(r, j):
                    dve.wait_ge(s_done.sem, r * PER + (j + 1))
                    dve.tensor_tensor(he[:, j % 2, :], sgs[:, j % 2, :], k.ps[:, 0, 256:512], ALU.mult).then_inc(h_done.sem, 1)
                    copy_turned(r, j + 1)
                    dve.wait_ge(k.used, r * U + (first + (j + 1) * UPE))
                    dve.wait_ge(scattered[j % 2].sem, r * (8 * PER) + 16 * (j // 2) + 16)
                    dve.tensor_copy(ys[:, j % 2, 512:D], k.ps[:, 5 + 2 * (j % 2), :]).then_inc(y_done_v.sem, 1)

                def copy_turned(r, j):
                    dve.wait_ge(t_ready.sem, r * (2 * PER) + (2 * j + 2))
                    dve.tensor_copy(rowsT[:, j % 2, 512:D], k.ps[:, 2, :]).then_inc(t_copied_v.sem, 1)

                def dense(r, j):
                    dve.wait_ge(k.used, r * U + (first + (j - 1) * UPE))
                    dve.wait_ge(he_done.sem, r * (2 * PER) + (2 * j + 2))
                    for f in range(2):
                        dve.wait_ge(silu_done.sem, r * (2 * PER) + (2 * j + f + 1))
                        dve.wait_ge(k.used, r * U + (first + j * UPE + 4))
                        dve.tensor_tensor(heT[:, j % 2, f, :], sg[:, f, :], k.ps[:, 2 + f, :], ALU.mult).then_inc(he_done.sem, 1)
                    for i in range(8):
                        t, n = divmod(i, 2)
                        if i < 7:
                            dve.wait_ge(d_ready.sem, r * (7 * PER) + (7 * j + i + 1))
                        else:
                            dve.wait_ge(k.used, r * U + (first + (j + 1) * UPE))
                        a = acc[:, t, n * 512:(n + 1) * 512]
                        dve.wait_ge(acc_done.sem, r * (8 * PER) + (8 * j + i + 1))
                        dve.scalar_tensor_tensor(a, k.ps[:, 4 + i % 4, :], comb[:, t, bass.ds(r * PER + j, 1)],
                                                 a, ALU.mult, ALU.add).then_inc(acc_done.sem, 1)

                few = dve.value_load(count[0:1, 0:1], min_val=0, max_val=T)
                with dve.If(few < FULL):
                    dve.memset(rows[:, :, :], 0.0).then_inc(filled.sem, 1)
                    dve.memset(sgs[:, 0, :], 0.0).then_inc(y_done_a.sem, 1)
                    dve.memset(sgs[:, 1, :], 0.0).then_inc(y_done_v.sem, 1)
                    dve.memset(hesT[:, :, :], 0.0).then_inc(ht_copied.sem, 1)
                    dve.memset(he[:, :, :], 0.0).then_inc(h_done.sem, 1)
                    copy_turned(0, 0)
                    rounds(dve, own)
                    for t in range(NT):
                        dve.wait_ge(picks[t % 2].sem, 16 * (t // 2 + 1))
                        a = acc[:, t, :]
                        dve.tensor_scalar(a, yy[:, t % 2, 0, :], wt[:, 0, t:t + 1], None, ALU.mult).then_inc(summed.sem, 1)
                        dve.wait_ge(summed.sem, 2 * t + 1)
                        dve.scalar_tensor_tensor(a, yy[:, t % 2, 1, :], wt[:, 1, t:t + 1], a, ALU.mult, ALU.add).then_inc(summed.sem, 1)
                with dve.Else():
                    for f in range(2):
                        dve.memset(heT[:, :, f, :], 0.0).then_inc(he_done.sem, 1)
                    for i in range(8):
                        t, n = divmod(i, 2)
                        dve.memset(acc[:, t, n * 512:(n + 1) * 512], 0.0).then_inc(acc_done.sem, 1)
                    rounds(dve, dense)

            @block.gpsimd
            def _(pool):
                def gather(e):
                    if e >= 2:
                        pool.wait_ge(t_ready.sem, 2 * (e - 1))
                    col = min(e, NE - 1)
                    pool.indirect_dma_start(rows[:, e % 2, :], None, k.dram["h_tok"],
                                            bass.IndirectOffsetOnAxis(slot_tok[:, col:col + 1], 0),
                                            bounds_check=T - 1, oob_is_err=False).then_inc(gathered[e % 2].sem, 16)

                few = pool.value_load(count[0:1, 0:1], min_val=0, max_val=T)
                with pool.If(few < FULL):
                    pool.wait_ge(filled.sem, 1)
                    for i in range(2):
                        pool.dma_start(ys[0:1, i, :], k.dram["h_tok"][0:1, :]).then_inc(scattered[i].sem, 16)
                    gather(0)
                    gather(1)
                    for e in range(NE):
                        if e + 2 <= NE:
                            gather(e + 2)
                        pool.wait_ge(y_done_a.sem, e + 2)
                        pool.wait_ge(y_done_v.sem, e + 2)
                        pool.indirect_dma_start(k.dram["picks"], bass.IndirectOffsetOnAxis(slot_row[:, e:e + 1], 0), ys[:, e % 2, :], None,
                                                bounds_check=2 * T - 1, oob_is_err=False).then_inc(scattered[e % 2].sem, 16)
        k.stage_end()


def stage_add_tokens(k, acc):
    with k.block() as block:
        ready, done = k.sig("y_ready"), k.sig("x_done")

        @block.tensor
        def _(pe):
            for b in range(DB):
                for t in range(NT):
                    mm = pe.transpose(k.ps[:, b, t * P:(t + 1) * P], acc[:, t, b * P:(b + 1) * P], k.c("ident"))
                mm.then_inc(ready.sem, ready.up())

        @block.vector
        def _(dve):
            for b in range(DB):
                dve.wait_ge(ready.sem, ready.at(b + 1))
                dve.tensor_tensor(k.xT[:, b, :], k.xT[:, b, :], k.ps[:, b, :], ALU.add).then_inc(done.sem, done.up())
    k.stage_end()


def stage_mod(k, mod_part):
    mod, gain = k.mod, k.gain
    NB = UNIT // P
    with k.block() as block:
        m_ready, m_done, chain = k.sig("mod_ready"), k.sig("mod_done"), k.sig("chain_v")

        @block.tensor
        def _(pe):
            for m in range((MG + 2) * NB):
                mm = pe.matmul(k.ps[:, 0, m:m + 1], mod_part[:, m // NB, m % NB * P:(m % NB + 1) * P], k.c("ones")[:, 0:1],
                               start=True, stop=True)
            mm.then_inc(m_ready.sem, m_ready.up())

        @block.vector
        def _(dve):
            dve.wait_ge(m_ready.sem, m_ready.at(1))
            a = COL["b_mod"][0]
            for i, (at, n) in enumerate(((0, MG * NB), (MG * NB, 2 * NB))):
                dve.tensor_tensor(mod[:, 0:n, i], k.ps[:, 0, at:at + n], k.cols[:, a:a + n], ALU.add).then_inc(chain.sem, chain.up())
            dve.wait_ge(chain.sem, chain.last)
            for i, (name, scale, which) in enumerate((("norm1_g_2", 8, 0), ("norm1_g_2", 8, 1), ("norm2_g_2", 32, 0))):
                g = COL[name][0]
                dve.tensor_scalar(gain[:, i, :], mod[:, scale:scale + 8, which], 1.0, None, ALU.add).then_inc(chain.sem, chain.up())
                dve.wait_ge(chain.sem, chain.last)
                dve.tensor_tensor(gain[:, i, :], gain[:, i, :], k.cols[:, g:g + 8], ALU.mult).then_inc(m_done.sem, m_done.up())

        @block.sync
        def _(sp):
            k.stream(sp, 0)
    k.stage_end()


def stage_load_ctx(k, hT2):
    with k.block() as block:
        @block.sync
        def _(sp):
            got = k.sig("load")
            sp.dma_start(hT2[:, :, 0:CTX], k.dram["ctxT"]).then_inc(got.sem, got.up(16))
            sp.wait_ge(got.sem, got.at(16))
    k.stage_end()


def stage_project(k, h, items, convs=None, taps=None, bias=None):
    convs = convs or [[] for _ in items]
    K = taps.count if taps else 0
    N = len(items)
    with ExitStack() as st:
        w = Split(k, st)
        with k.block() as block:
            done, done2, first, chain = k.sig("proj_done"), k.sig("proj_ctx_done"), k.sig("conv_first"), k.sig("chain_v")
            ctx_before = np.cumsum([0] + [it[1] is not None for it in items]).tolist()

            def middle(act, i):
                for dst, src, seg, n, np_ in convs[i]:
                    act.wait_ge(done.sem, done.at(i + 1))
                    if items[i][1] is not None:
                        act.wait_ge(done2.sem, done2.at(ctx_before[i + 1]))
                    act.activation(dst, src, ACT.Identity, scale=taps(n, K // 2)[0:np_, :],
                                   bias=bias(n)[0:np_, :] if bias else 0.0).then_inc(first.sem, first.up())

            def others(dve, i):
                done_before = sum(len(c) for c in convs[:i])
                for m, (dst, src, seg, n, np_) in enumerate(convs[i]):
                    dve.wait_ge(first.sem, first.at(done_before + m + 1))
                    d = dst.rearrange("p (s x) -> p s x", s=seg)
                    s = src.rearrange("p (s x) -> p s x", s=seg)
                    L = s.shape[2]
                    for j in range(K):
                        o = j - K // 2
                        if o:
                            lo, hi = max(0, -o), L - max(0, o)
                            dve.scalar_tensor_tensor(d[:, :, lo:hi], s[:, :, lo + o:hi + o],
                                                     taps(n, j)[0:np_, :], d[:, :, lo:hi], ALU.mult, ALU.add).then_inc(chain.sem, chain.up())
                            dve.wait_ge(chain.sem, chain.last)

            @block.tensor
            def _(pe):
                for i, (lat, cx, _, _) in enumerate(items):
                    w.ready(pe, i)
                    if i >= 4:
                        pe.wait_ge(done.sem, done.at(i - 3))
                        if ctx_before[i - 3]:
                            pe.wait_ge(done2.sem, done2.at(ctx_before[i - 3]))
                    for kt in range(DB):
                        mm = product(pe, k.ps[:, 2 * (i % 4), :], w.parts(i, kt * P, (kt + 1) * P), (h[0][:, kt, CTX:T2], h[1][:, kt, CTX:T2]),
                                     kt == 0, kt == DB - 1)
                    if cx is not None:
                        for kt in range(DB):
                            mm = product(pe, k.ps[:, 2 * (i % 4) + 1, 0:CTX], w.parts(i, kt * P, (kt + 1) * P),
                                         (h[0][:, kt, 0:CTX], h[1][:, kt, 0:CTX]), kt == 0, kt == DB - 1)
                    mm.then_inc(w.done.sem, w.done.up())

            @block.scalar
            def _(act):
                w.round(act, 0)
                for i, (lat, cx, func, factor) in enumerate(items):
                    if i < N - 1:
                        w.round(act, i + 1)
                    w.wait(act, i)
                    act.activation(lat, k.ps[:, 2 * (i % 4), :], func, scale=factor).then_inc(done.sem, done.up())
                    if i:
                        middle(act, i - 1)
                middle(act, N - 1)

            @block.vector
            def _(dve):
                w.rest(dve, 0)
                for i, (lat, cx, func, factor) in enumerate(items):
                    if i < N - 1:
                        w.rest(dve, i + 1)
                    if cx is not None:
                        w.wait(dve, i)
                        dve.tensor_scalar(cx, k.ps[:, 2 * (i % 4) + 1, 0:CTX], factor, None, ALU.mult).then_inc(done2.sem, done2.up())
                    if i:
                        others(dve, i - 1)
                others(dve, N - 1)

            @block.sync
            def _(sp):
                k.stream(sp, N)
        k.stage_end()


class Taps:
    def __init__(self, k, name, count):
        self.k, self.name, self.count = k, name, count

    def __call__(self, i, j):
        return self.k.col(self.name, i * self.count + j)


def stage_hyena(k, u, yT):
    TWO_PI = 2 * float(np.pi)
    HI = 6.28125
    LO = TWO_PI - HI
    ROUND = 1.5 * 2 ** 23
    with ExitStack() as st:
        dft = k.sb("hy_dft", [P, NT, 2 * NFREQ], st)
        H = k.sb("hy_H", [P, 8, 512], st)
        with ExitStack() as s2:
            win = k.sb("hy_win", [P, NT, 512], s2)
            w1, w2 = k.sb("hy_w1", [P, 64], s2), k.sb("hy_w2", [P, 64], s2)
            w3 = k.sb("hy_w3", [P, 1024], s2)
            z = k.sb("hy_z", [P, T], s2)
            h = k.sb("hy_h", [P, 3, T], s2)
            taps = k.sb("hy_taps", [P, 2, 512], s2)
            both = k.sb("hy_both", [P, NT, 2, 512], s2)
            with k.block() as block:
                got, chain = k.sig("load"), k.sig("chain_v")
                a_ready, a_done, sin_done = k.sig("a_ready"), k.sig("a_done"), k.sig("sin_done")
                t_ready, t_done, both_done = k.sig("t_ready"), k.sig("taps_done"), k.sig("both_done")
                H_ready, H_done = k.sig("H_ready"), [k.sig("H_done_a"), k.sig("H_done_v")]

                @block.sync
                def _(sp):
                    for dst, name in ((w1, "hy_w1"), (w2, "hy_w2"), (w3, "hy_w3")):
                        a, n = MAT[name]
                        sp.dma_start(dst[:, :], k.dram["mats"][:, a:a + n]).then_inc(got.sem, got.up(16))
                    sp.dma_start(z[:, :], k.dram["hy_z"]).then_inc(got.sem, got.up(16))
                    sp.dma_start(win[:, :, :], k.dram["hy_win"]).then_inc(got.sem, got.up(16))
                    sp.dma_start(dft[:, :, :], k.dram["dft"]).then_inc(got.sem, got.up(16))

                @block.tensor
                def _(pe):
                    pe.wait_ge(got.sem, got.at(96))
                    pe.matmul(k.ps[0:64, 0, :], w1[0:33, :], z[0:33, :], start=True, stop=True).then_inc(a_ready.sem, a_ready.up())
                    pe.wait_ge(sin_done.sem, sin_done.at(1))
                    pe.matmul(k.ps[0:64, 0, :], w2[0:64, :], h[0:64, 0, :], start=True, stop=True).then_inc(a_ready.sem, a_ready.up())
                    pe.wait_ge(sin_done.sem, sin_done.at(2))
                    for t in range(NT):
                        if t >= 2:
                            pe.wait_ge(t_done.sem, t_done.at(2 * (t - 1)))
                        for o in range(2):
                            mm = pe.matmul(k.ps[:, 2 * (t % 2) + o, :], h[0:64, 0, t * P:(t + 1) * P],
                                           w3[0:64, o * 512:(o + 1) * 512], start=True, stop=True)
                        mm.then_inc(t_ready.sem, t_ready.up())
                    pe.wait_ge(both_done.sem, both_done.at(4 * NT))
                    for f in range(8):
                        for t in range(NT):
                            mm = pe.matmul(k.ps[:, f, :], dft[:, t, f * P:(f + 1) * P], both[:, t, f // 4, :],
                                           start=t == 0, stop=t == NT - 1)
                        mm.then_inc(H_ready.sem, H_ready.up())

                @block.scalar
                def _(act):
                    for i in range(2):
                        act.wait_ge(a_done.sem, a_done.at(i + 1))
                        act.activation(h[0:64, 0, :], h[0:64, 1, :], ACT.Sin).then_inc(sin_done.sem, sin_done.up())
                    for f in range(0, 8, 2):
                        act.wait_ge(H_ready.sem, H_ready.at(f + 1))
                        act.copy(H[:, f, :], k.ps[:, f, :]).then_inc(H_done[0].sem, H_done[0].up())

                @block.vector
                def _(dve):
                    dve.wait_ge(got.sem, got.at(96))
                    for i, (b, f) in enumerate((("hy_b1", "hy_f1"), ("hy_b2", "hy_f2"))):
                        dve.wait_ge(a_ready.sem, a_ready.at(i + 1))
                        arg, n = h[0:64, 1, :], h[0:64, 2, :]
                        dve.tensor_scalar(arg, k.ps[0:64, 0, :], k.col(b, 0, 0, 64), k.col(f, 0, 0, 64),
                                          ALU.add, ALU.mult).then_inc(chain.sem, chain.up())
                        dve.wait_ge(chain.sem, chain.last)
                        dve.tensor_scalar(n, arg, 1 / TWO_PI, ROUND, ALU.mult, ALU.add).then_inc(chain.sem, chain.up())
                        dve.wait_ge(chain.sem, chain.last)
                        dve.tensor_scalar(n, n, ROUND, None, ALU.subtract).then_inc(chain.sem, chain.up())
                        dve.wait_ge(chain.sem, chain.last)
                        dve.scalar_tensor_tensor(arg, n, -HI, arg, ALU.mult, ALU.add).then_inc(chain.sem, chain.up())
                        dve.wait_ge(chain.sem, chain.last)
                        dve.scalar_tensor_tensor(arg, n, -LO, arg, ALU.mult, ALU.add).then_inc(chain.sem, chain.up())
                        dve.wait_ge(chain.sem, chain.last)
                        lim = float(np.float32(3.1415925))
                        dve.tensor_scalar(arg, arg, lim, -lim, ALU.min, ALU.max).then_inc(a_done.sem, a_done.up())
                    for t in range(NT):
                        dve.wait_ge(t_ready.sem, t_ready.at(t + 1))
                        if t:
                            dve.wait_ge(both_done.sem, both_done.at(4 * t))
                        for o in range(2):
                            dve.tensor_tensor(taps[:, o, :], k.ps[:, 2 * (t % 2) + o, :], win[:, t, :], ALU.mult).then_inc(t_done.sem, t_done.up())
                        dve.wait_ge(t_done.sem, t_done.at(2 * t + 2))
                        for o in range(2):
                            for i, op in ((0, ALU.add), (1, ALU.subtract)):
                                dve.tensor_tensor(both[:, t, i, o * HY_C:(o + 1) * HY_C], taps[:, o, 0:HY_C],
                                                  taps[:, o, HY_C:512], op).then_inc(both_done.sem, both_done.up())
                    for f in range(1, 8, 2):
                        dve.wait_ge(H_ready.sem, H_ready.at(f + 1))
                        dve.tensor_copy(H[:, f, :], k.ps[:, f, :]).then_inc(H_done[1].sem, H_done[1].up())
            k.stage_end()
        with ExitStack() as s2:
            inv = k.sb("hy_inv", [P, 8, T], s2)
            vt = k.sb("hy_vt", [P, NT, HY_C], s2)
            Y = k.sb("hy_Y", [P, 8, HY_C], s2)
            tmp = k.sb("hy_tmp", [P, 2, 4, HY_C], s2)
            for o in range(2):
                src = u[:, 0:2, :]
                gate, dst = (u[:, 2:4, :], src) if o == 0 else (u[:, 4:6, :], yT)
                with k.block() as block:
                    got, chain = k.sig("load"), k.sig("chain_v")
                    v_ready, v_done, V_ready = k.sig("v_ready"), k.sig("v_copied"), k.sig("V_ready")
                    Y_done, c_ready, y_done = k.sig("Y_done"), k.sig("c_ready"), k.sig("y_done")

                    @block.sync
                    def _(sp):
                        if o == 0:
                            sp.dma_start(inv[:, :, :], k.dram["inv"]).then_inc(got.sem, got.up(16))

                    @block.tensor
                    def _(pe):
                        for b in range(2):
                            for t in range(NT):
                                mm = pe.transpose(k.ps[:, b, t * P:(t + 1) * P], src[:, b, t * P:(t + 1) * P], k.c("ident"))
                            mm.then_inc(v_ready.sem, v_ready.up())
                        pe.wait_ge(v_done.sem, v_done.at(2))
                        for f in range(4):
                            for i in range(2):
                                for t in range(NT):
                                    mm = pe.matmul(k.ps[:, 2 + f, i * HY_C:(i + 1) * HY_C],
                                                   dft[:, t, (4 * i + f) * P:(4 * i + f + 1) * P], vt[:, t, :],
                                                   start=t == 0, stop=t == NT - 1)
                        mm.then_inc(V_ready.sem, V_ready.up())
                        if o == 0:
                            pe.wait_ge(got.sem, got.at(16))
                        pe.wait_ge(Y_done.sem, Y_done.at(2))
                        for b in range(2):
                            for f in range(8):
                                mm = pe.matmul(k.ps[:, b, :], Y[:, f, b * P:(b + 1) * P], inv[:, f, :],
                                               start=f == 0, stop=f == 7)
                            mm.then_inc(c_ready.sem, c_ready.up())

                    @block.scalar
                    def _(act):
                        for b in range(2):
                            act.wait_ge(v_ready.sem, v_ready.at(b + 1))
                            act.copy(vt[:, :, b * P:(b + 1) * P], k.ps[:, b, :].rearrange("p (t c) -> p t c", c=P)).then_inc(v_done.sem, v_done.up())

                    @block.vector
                    def _(dve):
                        dve.wait_ge(V_ready.sem, V_ready.at(1))
                        re, im = (k.ps[:, 2:6, i * HY_C:(i + 1) * HY_C] for i in range(2))
                        Hr, Hi = (H[:, 4 * i:4 * i + 4, o * HY_C:(o + 1) * HY_C] for i in range(2))
                        dve.tensor_tensor(tmp[:, 0, :, :], re, Hr, ALU.mult).then_inc(chain.sem, chain.up())
                        dve.tensor_tensor(tmp[:, 1, :, :], im, Hi, ALU.mult).then_inc(chain.sem, chain.up())
                        dve.wait_ge(chain.sem, chain.last)
                        dve.tensor_tensor(Y[:, 0:4, :], tmp[:, 0, :, :], tmp[:, 1, :, :], ALU.subtract).then_inc(Y_done.sem, Y_done.up())
                        dve.wait_ge(Y_done.sem, Y_done.at(1))
                        dve.tensor_tensor(tmp[:, 0, :, :], re, Hi, ALU.mult).then_inc(chain.sem, chain.up())
                        dve.tensor_tensor(tmp[:, 1, :, :], im, Hr, ALU.mult).then_inc(chain.sem, chain.up())
                        dve.wait_ge(chain.sem, chain.last)
                        dve.tensor_tensor(Y[:, 4:8, :], tmp[:, 0, :, :], tmp[:, 1, :, :], ALU.add).then_inc(Y_done.sem, Y_done.up())
                        for b in range(2):
                            dve.wait_ge(c_ready.sem, c_ready.at(b + 1))
                            dve.scalar_tensor_tensor(dst[:, b, :], src[:, b, :], k.col("hy_d", 2 * o + b),
                                                     k.ps[:, b, :], ALU.mult, ALU.add).then_inc(chain.sem, chain.up())
                            dve.wait_ge(chain.sem, chain.last)
                            dve.tensor_tensor(dst[:, b, :], dst[:, b, :], gate[:, b, :], ALU.mult).then_inc(y_done.sem, y_done.up())
                k.stage_end()


def stage_to_tokens(k, jobs):
    with k.block() as block:
        ready, done = k.sig("y_ready"), [k.sig("turned_act"), k.sig("turned_dve")]

        @block.tensor
        def _(pe):
            for i, (dst, src, *at) in enumerate(jobs):
                if i >= 8:
                    pe.wait_ge(done[i % 2].sem, done[i % 2].at((i - 8) // 2 + 1))
                n, p0 = src.shape[0], at[0] if at else 0
                pe.transpose(k.ps[:, i % 8, 0:n], src, k.c("ident")[p0:p0 + n, p0:p0 + n]).then_inc(ready.sem, ready.up())

        @block.scalar
        def _(act):
            for i in range(0, len(jobs), 2):
                act.wait_ge(ready.sem, ready.at(i + 1))
                dst = jobs[i][0]
                act.copy(dst, k.ps[:, i % 8, 0:dst.shape[1]]).then_inc(done[0].sem, done[0].up())

        @block.vector
        def _(dve):
            for i in range(1, len(jobs), 2):
                dve.wait_ge(ready.sem, ready.at(i + 1))
                dst = jobs[i][0]
                dve.tensor_copy(dst, k.ps[:, i % 8, 0:dst.shape[1]]).then_inc(done[1].sem, done[1].up())
    k.stage_end()


def stage_gates(k, aT, gt, la, ldec, beta):
    with ExitStack() as st:
        a2 = k.sb("gla_a2", [P, 256], st)
        row = k.sb("gate_rows", [P, 512 + 16], st)
        sp1 = k.sb("softplus", [P, NT2, 256], st)
        d1 = k.sb("gdn_pre", [P, 3, NT2, 8], st)
        with k.block() as block:
            got, chain = k.sig("load"), k.sig("chain_v")
            x_ready, x_done, e_done, d_done = k.sig("x_ready"), k.sig("x_done"), k.sig("e_done"), k.sig("d_done")

            @block.sync
            def _(sp):
                a, n = MAT["gla_a2"]
                sp.dma_start(a2[:, :], k.dram["mats"][:, a:a + n]).then_inc(got.sem, got.up(16))
                a, n = ROW["gla_b"]
                sp.dma_start(row[:, 0:512], k.dram["rows"][:, a:a + n].broadcast_to([P, n])).then_inc(got.sem, got.up(16))
                a, n = ROW["a_log"][0], 16
                sp.dma_start(row[:, 512:528], k.dram["rows"][:, a:a + n].broadcast_to([P, n])).then_inc(got.sem, got.up(16))

            @block.tensor
            def _(pe):
                pe.wait_ge(got.sem, got.at(48))
                for d in range(2):
                    p0 = 32 * d
                    for t in range(NT2):
                        mm = pe.matmul(k.ps[:, 4 * d + t // 2, (t % 2) * 256:(t % 2) * 256 + 256],
                                       aT[p0:p0 + 16, t * P:(t + 1) * P], a2[p0:p0 + 16, :], start=True, stop=True)
                    mm.then_inc(x_ready.sem, x_ready.up())

            @block.vector
            def _(dve):
                dve.wait_ge(got.sem, got.at(48))
                x, ax, sp_ = d1[:, 0, :, :], d1[:, 1, :, :], d1[:, 2, :, :]
                dve.tensor_tensor(x, gt[:, :, 0:8], row[:, 520:528].unsqueeze(1).broadcast_to([P, NT2, 8]), ALU.add).then_inc(chain.sem, chain.up())
                dve.wait_ge(chain.sem, chain.last)
                dve.tensor_scalar(ax, x, -1.0, None, ALU.mult).then_inc(chain.sem, chain.up())
                dve.wait_ge(chain.sem, chain.last)
                dve.tensor_tensor(ax, ax, x, ALU.min).then_inc(d_done.sem, d_done.up())
                for d in range(2):
                    dve.wait_ge(x_ready.sem, x_ready.at(d + 1))
                    bias = row[:, d * 256:(d + 1) * 256]
                    l = la[:, d, :, :]
                    for a in range(3):
                        xx = k.ps[:, 4 * d + a, :].rearrange("p (t n) -> p t n", n=256)
                        dve.tensor_tensor(l[:, 2 * a:2 * a + 2, :], xx,
                                          bias.unsqueeze(1).broadcast_to([P, 2, 256]), ALU.add).then_inc(x_done.sem, x_done.up())
                    dve.wait_ge(x_done.sem, x_done.at(3 * d + 3))
                    dve.wait_ge(e_done.sem, e_done.at(3 * d + 3))
                    dve.tensor_scalar(l, l, 0.0, None, ALU.min).then_inc(chain.sem, chain.up())
                    dve.wait_ge(chain.sem, chain.last)
                    dve.tensor_tensor(l, l, sp1[:, :, :], ALU.subtract).then_inc(chain.sem, chain.up())
                    dve.wait_ge(chain.sem, chain.last)
                dve.wait_ge(e_done.sem, e_done.at(10))
                dve.tensor_scalar(x, x, 0.0, None, ALU.max).then_inc(chain.sem, chain.up())
                dve.wait_ge(chain.sem, chain.last)
                dve.tensor_tensor(x, x, sp_, ALU.add).then_inc(chain.sem, chain.up())
                dve.wait_ge(chain.sem, chain.last)
                dve.scalar_tensor_tensor(ldec[:, :, :], x, -1.0, row[:, 512:520].unsqueeze(1).broadcast_to([P, NT2, 8]),
                                         ALU.mult, ALU.mult).then_inc(chain.sem, chain.up())
                dve.wait_ge(chain.sem, chain.last)

            @block.scalar
            def _(act):
                for d in range(2):
                    act.wait_ge(x_done.sem, x_done.at(3 * d + 3))
                    if d:
                        act.wait_ge(chain.sem, chain.at(4))
                    l = la[:, d, :, :]
                    for f, src, kw in ((ACT.Abs, l, {}), (ACT.Exp, sp1[:, :, :], {"scale": -1.0}),
                                       (ACT.Ln, sp1[:, :, :], {"bias": 1.0})):
                        act.activation(sp1[:, :, :], src, f, **kw).then_inc(e_done.sem, e_done.up())
                        act.wait_ge(e_done.sem, e_done.last)
                act.wait_ge(got.sem, got.at(48))
                act.wait_ge(d_done.sem, d_done.at(1))
                act.activation(d1[:, 2, :, :], d1[:, 1, :, :], ACT.Exp).then_inc(e_done.sem, e_done.up())
                act.wait_ge(e_done.sem, e_done.last)
                act.activation(d1[:, 2, :, :], d1[:, 2, :, :], ACT.Ln, bias=1.0).then_inc(e_done.sem, e_done.up())
                act.wait_ge(e_done.sem, e_done.last)
                act.activation(row[:, 512:520], row[:, 512:520], ACT.Exp).then_inc(e_done.sem, e_done.up())
                act.wait_ge(e_done.sem, e_done.last)
                act.activation(beta[:, :, :], gt[:, :, 8:16], ACT.Sigmoid).then_inc(e_done.sem, e_done.up())
                act.wait_ge(e_done.sem, e_done.last)
        k.stage_end()


def stage_gla_chunk(k, d, c, n, qT, kT, vt, la, S, y):
    mid, end = (P // 2, P - 1) if d == "f" else (P // 2 - 1, 0)
    lat = c >= 2
    di = 0 if d == "f" else 1
    H2 = GLA_H // 2
    V = GLA_DV
    with ExitStack() as st:
        refs = k.sb("gla_refs", [P, 4, H2], st)
        ex = k.sb("gla_ex", [P, 2, H2, P], st)
        qs = k.sb("gla_qs", [P, 2, H2, P], st)
        A = k.sb("gla_A", [P, 2, H2, P], st)
        tok = k.sb("gla_tok", [P, H2 * P], st)
        Ss = k.sb("gla_Ss", [P, H2, V], st)
        with k.block() as block:
            g_ready, ref_done, ex_done, chain, scaled = (k.sig(x) for x in ("g_ready", "ref_done", "ex_done", "chain_v", "state_scaled"))
            qk_done, s_ready, s_masked, t_ready, t_copied = (k.sig(x) for x in ("qk_done", "s_ready", "s_masked", "t_ready", "t_copied"))
            m_ready, y_ready, y_done = k.sig("m_ready"), k.sig("y_ready"), k.sig("y_done")

            @block.tensor
            def _(pe):
                for b in range(H2):
                    mm = pe.matmul(k.ps[:, 0, b * P:(b + 1) * P], la[:, di, c, b * P:(b + 1) * P],
                                   k.c("tri_" + d)[:, 0:P], start=True, stop=True)
                mm.then_inc(g_ready.sem, g_ready.up())
                pe.wait_ge(qk_done.sem, qk_done.at(2 if lat else 1))
                for b in range(H2):
                    mm = pe.transpose(k.ps[:, 1, b * P:(b + 1) * P], qs[:, 1, b, :], k.c("ident"))
                mm.then_inc(t_ready.sem, t_ready.up())
                if lat:
                    for h in range(GLA_H):
                        a, b = 64 * (h % 2), h // 2
                        mm = pe.matmul(k.ps[:, 2 + h % 2, b * P:(b + 1) * P], qs[a:a + 64, 1, b, :], qs[a:a + 64, 0, b, :],
                                       start=True, stop=True)
                    mm.then_inc(s_ready.sem, s_ready.up())
                pe.wait_ge(t_copied.sem, t_copied.at(1))
                for h in range(GLA_H):
                    a, b = 64 * (h % 2), h // 2
                    mm = pe.matmul(k.ps[a:a + 64, 6, b * V:(b + 1) * V], tok[:, h * 64:(h + 1) * 64],
                                   vt[:, c, h * V:(h + 1) * V], start=True, stop=True)
                mm.then_inc(m_ready.sem, m_ready.up())
                if lat:
                    pe.wait_ge(s_masked.sem, s_masked.at(1))
                    pe.wait_ge(scaled.sem, scaled.at(1))
                    for h in range(GLA_H):
                        a, b = 64 * (h % 2), h // 2
                        out = k.ps[:, 4 + h % 2, b * V:(b + 1) * V]
                        pe.matmul(out, qs[a:a + 64, 0, b, :], Ss[a:a + 64, b, :], start=True, stop=False)
                        mm = pe.matmul(out, A[:, h % 2, b, :], vt[:, c, h * V:(h + 1) * V], start=False, stop=True)
                    mm.then_inc(y_ready.sem, y_ready.up())

            @block.scalar
            def _(act):
                act.wait_ge(ref_done.sem, ref_done.at(2))
                g = k.ps[:, 0, 0:H2 * P].rearrange("p (b t) -> p b t", t=P)
                for b in range(H2):
                    act.activation(ex[:, 0, b, :], g[:, b, :], ACT.Exp, scale=1 / 16, bias=refs[:, 1, b:b + 1]).then_inc(ex_done.sem, ex_done.up())
                    act.activation(ex[:, 1, b, :], g[:, b, :], ACT.Exp, scale=-1 / 16, bias=refs[:, 0, b:b + 1]).then_inc(ex_done.sem, ex_done.up())
                act.activation(refs[:, 2, :], refs[:, 0, :], ACT.Exp).then_inc(ex_done.sem, ex_done.up())
                act.wait_ge(t_ready.sem, t_ready.at(1))
                act.copy(tok[:, :], k.ps[:, 1, 0:H2 * P]).then_inc(t_copied.sem, t_copied.up())

            @block.vector
            def _(dve):
                dve.wait_ge(g_ready.sem, g_ready.at(1))
                g = k.ps[:, 0, 0:H2 * P].rearrange("p (b t) -> p b t", t=P)
                for i, f in ((0, 1 / 16), (1, -1 / 16)):
                    dve.tensor_scalar(refs[:, i, :], g[:, :, mid], f, None, ALU.mult).then_inc(ref_done.sem, ref_done.up())
                dve.wait_ge(ex_done.sem, ex_done.at(2 * H2 + 1))
                ts = slice(c * P, (c + 1) * P)
                if lat:
                    dve.tensor_tensor(qs[:, 0, :, :], qT[:, :, (c - 2) * P:(c - 1) * P], ex[:, 0, :, :], ALU.mult).then_inc(qk_done.sem, qk_done.up())
                dve.tensor_tensor(qs[:, 1, :, :], kT[:, :, ts], ex[:, 1, :, :], ALU.mult).then_inc(qk_done.sem, qk_done.up())
                if n == 0:
                    dve.memset(Ss[:, :, :], 0.0).then_inc(scaled.sem, scaled.up())
                else:
                    dve.tensor_tensor(Ss[:, :, :], S[:, :, :], refs[:, 2, :].unsqueeze(2).broadcast_to([P, H2, V]), ALU.mult).then_inc(scaled.sem, scaled.up())
                if lat:
                    dve.wait_ge(s_ready.sem, s_ready.at(1))
                    m = k.c("attn_" + d)[:, P:2 * P].unsqueeze(1).broadcast_to([P, H2, P])
                    for i in range(2):
                        ins = dve.tensor_tensor(A[:, i, :, :], k.ps[:, 2 + i, 0:H2 * P].rearrange("p (b t) -> p b t", t=P), m, ALU.mult)
                    ins.then_inc(s_masked.sem, s_masked.up())
                dve.wait_ge(m_ready.sem, m_ready.at(1))
                dve.wait_ge(scaled.sem, scaled.at(1))
                dve.tensor_tensor(S[:, :, :], Ss[:, :, :], k.ps[:, 6, 0:H2 * V].rearrange("p (b v) -> p b v", v=V), ALU.add).then_inc(chain.sem, chain.up())
                dve.wait_ge(chain.sem, chain.last)
                dve.tensor_tensor(S[:, :, :], S[:, :, :], ex[:, 0, :, end].unsqueeze(2).broadcast_to([P, H2, V]), ALU.mult).then_inc(chain.sem, chain.up())
                if lat:
                    dve.wait_ge(y_ready.sem, y_ready.at(1))
                    out = y[:, c - 2, :].rearrange("p (b i v) -> p i b v", i=2, v=V)
                    got = k.ps[:, 4:6, 0:H2 * V].rearrange("p i (b v) -> p i b v", v=V)
                    if d == "f":
                        dve.tensor_copy(out, got).then_inc(y_done.sem, y_done.up())
                    else:
                        dve.tensor_tensor(out, out, got, ALU.add).then_inc(y_done.sem, y_done.up())
        k.stage_end()


def stage_head_norm(k, y, name, gateT, yT, b0):
    HV = 96
    N = NT * 4
    with ExitStack() as st:
        sq = k.sb("hn_sq", [P, NT, VW], st)
        stat = k.sb("hn_stat", [P, N], st)
        row = k.sb("hn_row", [P, HV], st)
        with k.block() as block:
            got, chain, v_done, rooted, y_done, y_ready, y_copied = (
                k.sig(x) for x in ("load", "chain_v", "var_done", "rooted", "y_done", "y_ready", "y_copied"))

            @block.sync
            def _(sp):
                a, n = ROW[name]
                sp.dma_start(row[:, :], k.dram["rows"][:, a:a + n].broadcast_to([P, n])).then_inc(got.sem, got.up(16))

            @block.tensor
            def _(pe):
                pe.wait_ge(y_done.sem, y_done.at(1))
                for b in range(3):
                    for t in range(NT):
                        mm = pe.transpose(k.ps[:, b, t * P:(t + 1) * P], y[:, t, b * P:(b + 1) * P], k.c("ident"))
                    mm.then_inc(y_ready.sem, y_ready.up())

            @block.scalar
            def _(act):
                act.wait_ge(v_done.sem, v_done.at(1))
                act.activation(stat[:, :], stat[:, :], ACT.Sqrt, scale=1.0 / HV, bias=RMS_EPS).then_inc(rooted.sem, rooted.up())

            @block.vector
            def _(dve):
                yh = y[:, :, :].rearrange("p t (h c) -> p (t h) c", c=HV)
                sh = sq[:, :, :].rearrange("p t (h c) -> p (t h) c", c=HV)
                dve.tensor_tensor(sh, yh, yh, ALU.mult).then_inc(chain.sem, chain.up())
                dve.wait_ge(chain.sem, chain.last)
                dve.tensor_reduce(stat[:, :], sh, AX.X, ALU.add).then_inc(v_done.sem, v_done.up())
                dve.wait_ge(rooted.sem, rooted.at(1))
                dve.reciprocal(stat[:, :], stat[:, :]).then_inc(chain.sem, chain.up())
                dve.wait_ge(chain.sem, chain.last)
                dve.tensor_tensor(yh, yh, stat[:, :].unsqueeze(2).broadcast_to([P, N, HV]), ALU.mult).then_inc(chain.sem, chain.up())
                dve.wait_ge(chain.sem, chain.last)
                dve.wait_ge(got.sem, got.at(16))
                dve.tensor_tensor(yh, yh, row[:, :].unsqueeze(1).broadcast_to([P, N, HV]), ALU.mult).then_inc(y_done.sem, y_done.up())
                for b in range(3):
                    dve.wait_ge(y_ready.sem, y_ready.at(b + 1))
                    dve.tensor_tensor(yT[:, b0 + b, :], k.ps[:, b, :], gateT[:, b, :], ALU.mult).then_inc(y_copied.sem, y_copied.up())
        k.stage_end()


def stage_l2(k, qT, kT):
    D6 = GDN_D
    with ExitStack() as st:
        sq = k.sb("l2_sq", [P, GDN_H, T2], st)
        with k.block() as block:
            silu_done, squared, summed, rooted, chain = (k.sig(x) for x in ("silu_done", "squared", "summed", "rooted", "chain_v"))
            @block.scalar
            def _(act):
                for i, (x, n, f) in enumerate(((kT, T2, 1.0), (qT, T, float(D6)))):
                    act.activation(x[0:D6, :, :], x[0:D6, :, :], ACT.Silu).then_inc(silu_done.sem, silu_done.up())
                    act.wait_ge(silu_done.sem, silu_done.last)
                    if i:
                        act.wait_ge(chain.sem, chain.at(2))
                    act.activation(sq[0:D6, :, 0:n], x[0:D6, :, :], ACT.Square).then_inc(squared.sem, squared.up())
                    act.wait_ge(summed.sem, summed.at(i + 1))
                    act.wait_ge(squared.sem, squared.at(i + 1))
                    act.activation(sq[0:D6, :, 0:512], k.ps[0:D6, 0:4, :], ACT.Sqrt, scale=f, bias=f * 1e-6).then_inc(rooted.sem, rooted.up())
                    if n > 512:
                        act.activation(sq[0:D6, :, 512:n], k.ps[0:D6, 4:8, 0:n - 512], ACT.Sqrt, scale=f, bias=f * 1e-6).then_inc(rooted.sem, rooted.up())

            @block.tensor
            def _(pe):
                for i, n in enumerate((T2, T)):
                    pe.wait_ge(squared.sem, squared.at(i + 1))
                    if i:
                        pe.wait_ge(rooted.sem, rooted.at(2))
                    for h in range(GDN_H):
                        mm = pe.matmul(k.ps[0:D6, h, :], k.c("ones")[0:D6, 0:D6], sq[0:D6, h, 0:512], start=True, stop=True)
                        if n > 512:
                            mm = pe.matmul(k.ps[0:D6, 4 + h, 0:n - 512], k.c("ones")[0:D6, 0:D6], sq[0:D6, h, 512:n],
                                           start=True, stop=True)
                    mm.then_inc(summed.sem, summed.up())

            @block.vector
            def _(dve):
                for i, (x, n) in enumerate(((kT, T2), (qT, T))):
                    dve.wait_ge(rooted.sem, rooted.at(2 + i))
                    dve.reciprocal(sq[0:D6, :, 0:n], sq[0:D6, :, 0:n]).then_inc(chain.sem, chain.up())
                    dve.wait_ge(chain.sem, chain.last)
                    dve.tensor_tensor(x[0:D6, :, :], x[0:D6, :, :], sq[0:D6, :, 0:n], ALU.mult).then_inc(chain.sem, chain.up())
                    dve.wait_ge(chain.sem, chain.last)
        k.stage_end()


def stage_gdn_chunk(k, pair, qT, kT, ldec, beta, LT, AT, eg):
    with ExitStack() as st:
        dec = k.sb("gdn_dec", [P, 2, GDN_H, P], st)
        decs = k.sb("gdn_decs", [P, 2, GDN_H, P], st)
        with k.block() as block:
            g_ready, g_done, r_done, ex_done, s_ready = (
                [k.sig(x), k.sig(x + "_back")] for x in ("g_ready", "g_done", "row_done", "ex_done", "s_ready"))
            chain, s_masked = k.sig("chain_v"), k.sig("s_masked")

            @block.tensor
            def _(pe):
                for i, (d, c) in enumerate(pair):
                    tri = k.c("tri_" + d)[:, 0:P]
                    hs = slice(4 * i, 4 * i + 4)
                    pe.matmul(k.ps[:, 4 * i, 0:4], tri, ldec[:, c, hs], start=True, stop=True)
                    pe.matmul(k.ps[:, 4 * i, 4:8], k.c("ones"), ldec[:, c, hs], start=True, stop=True)
                    for h in range(GDN_H):
                        g = ldec[:, c, 4 * i + h:4 * i + h + 1].broadcast_to([P, P])
                        mm = pe.matmul(k.ps[:, 4 * i + 1, h * P:(h + 1) * P], g, tri, start=True, stop=True)
                    mm.then_inc(g_ready[i].sem, g_ready[i].up())
                for i, (d, c) in enumerate(pair):
                    ts = slice(c * P, (c + 1) * P)
                    for h in range(GDN_H):
                        kk = kT[0:GDN_D, h, ts]
                        mm = pe.matmul(k.ps[:, 4 * i + 2, h * P:(h + 1) * P], kk, kk, start=True, stop=True)
                        if c >= 2:
                            mm = pe.matmul(k.ps[:, 4 * i + 3, h * P:(h + 1) * P], kk, qT[0:GDN_D, h, (c - 2) * P:(c - 1) * P],
                                           start=True, stop=True)
                    mm.then_inc(s_ready[i].sem, s_ready[i].up())

            @block.scalar
            def _(act):
                for i in range(2):
                    act.wait_ge(g_done[i].sem, g_done[i].at(2))
                    act.activation(eg[:, i, 1, :], eg[:, i, 1, :], ACT.Exp).then_inc(ex_done[i].sem, ex_done[i].up())
                    act.activation(eg[:, i, 0, :], eg[:, i, 3, :], ACT.Exp).then_inc(ex_done[i].sem, ex_done[i].up())
                    act.activation(eg[:, i, 2, :], k.ps[:, 4 * i, 4:8], ACT.Exp).then_inc(ex_done[i].sem, ex_done[i].up())
                    act.wait_ge(r_done[i].sem, r_done[i].at(GDN_H))
                    act.activation(dec[:, i, :, :], dec[:, i, :, :], ACT.Exp).then_inc(ex_done[i].sem, ex_done[i].up())

            @block.vector
            def _(dve):
                for i in range(2):
                    dve.wait_ge(g_ready[i].sem, g_ready[i].at(1))
                    dve.tensor_copy(eg[:, i, 3, :], k.ps[:, 4 * i, 0:4]).then_inc(g_done[i].sem, g_done[i].up())
                    dve.wait_ge(g_done[i].sem, g_done[i].last)
                    dve.tensor_tensor(eg[:, i, 1, :], k.ps[:, 4 * i, 4:8], eg[:, i, 3, :], ALU.subtract).then_inc(g_done[i].sem, g_done[i].up())
                    for h in range(GDN_H):
                        dve.tensor_scalar(dec[:, i, h, :], k.ps[:, 4 * i + 1, h * P:(h + 1) * P], eg[:, i, 3, h:h + 1], 0.0,
                                          ALU.subtract, ALU.min).then_inc(r_done[i].sem, r_done[i].up())
                for i, (d, c) in enumerate(pair):
                    dve.wait_ge(ex_done[i].sem, ex_done[i].at(4))
                    m = k.c("attn_" + d)
                    dve.tensor_tensor(decs[:, i, :, :], dec[:, i, :, :], m[:, 0:P].unsqueeze(1).broadcast_to([P, GDN_H, P]), ALU.mult).then_inc(chain.sem, chain.up())
                    dve.wait_ge(chain.sem, chain.last)
                    dve.wait_ge(s_ready[i].sem, s_ready[i].at(1))
                    for h in range(GDN_H):
                        dve.scalar_tensor_tensor(LT[:, i, h, :], k.ps[:, 4 * i + 2, h * P:(h + 1) * P],
                                                 beta[:, c, 4 * i + h:4 * i + h + 1], decs[:, i, h, :], ALU.mult, ALU.mult).then_inc(s_masked.sem, s_masked.up())
                    if c >= 2:
                        dve.tensor_tensor(dec[:, i, :, :], dec[:, i, :, :], m[:, P:2 * P].unsqueeze(1).broadcast_to([P, GDN_H, P]), ALU.mult).then_inc(chain.sem, chain.up())
                        dve.wait_ge(chain.sem, chain.last)
                        dve.tensor_tensor(AT[:, i, :, :], k.ps[:, 4 * i + 3, :].rearrange("p (h t) -> p h t", t=P), dec[:, i, :, :], ALU.mult).then_inc(s_masked.sem, s_masked.up())
        k.stage_end()


def stage_gdn_step(k, pair, n, seen, qT, kT, kt, vt, w, AT, eg, beta, S, y):
    V = GDN_D
    with ExitStack() as st:
        W = k.sb("gdn_W", [P, 2, GDN_H, V], st)
        U = k.sb("gdn_U", [P, 2, 2, GDN_H, V], st)
        with k.block() as block:
            z_done = k.sig("state_scaled")
            w_ready, w_done, u_ready, u_done, m_ready, y_ready = (
                [k.sig(x), k.sig(x + "_back")] for x in ("w_ready", "w_done", "u_ready", "u_done", "m_ready", "y_ready"))
            chain, y_done = k.sig("chain_v"), k.sig("y_done")

            def bank(i, j):
                return k.ps[:, 4 * i + j, 0:GDN_H * V].rearrange("p (h v) -> p h v", v=V)

            def o1(i):
                return w["M"][:, i * GDN_H:(i + 1) * GDN_H, 0:V]

            def wide(x, p=P):
                return x.unsqueeze(2).broadcast_to([p, GDN_H, V])

            @block.tensor
            def _(pe):
                if n == 0:
                    pe.wait_ge(z_done.sem, z_done.at(1))
                for i, (d, c) in enumerate(pair):
                    for h in range(GDN_H):
                        if c >= 2:
                            pe.matmul(bank(i, 3)[:, h, :], qT[0:V, h, (c - 2) * P:(c - 1) * P], S[0:V, i, h, :], start=True, stop=True)
                        mm = pe.matmul(bank(i, 0)[:, h, :], kT[0:V, h, c * P:(c + 1) * P], S[0:V, i, h, :], start=True, stop=True)
                    mm.then_inc(w_ready[i].sem, w_ready[i].up())
                for i, (d, c) in enumerate(pair):
                    pe.wait_ge(w_done[i].sem, w_done[i].at(1))
                    for h in range(GDN_H):
                        mm = pe.matmul(bank(i, 1)[:, h, :], w["XT"][:, i * GDN_H + h, :], W[:, i, h, :], start=True, stop=True)
                    mm.then_inc(u_ready[i].sem, u_ready[i].up())
                for i, (d, c) in enumerate(pair):
                    pe.wait_ge(u_done[i].sem, u_done[i].at(2))
                    for h in range(GDN_H):
                        mm = pe.matmul(bank(i, 2)[0:V, h, :], kt[:, c, h, :], U[:, i, 1, h, :], start=True, stop=True)
                    mm.then_inc(m_ready[i].sem, m_ready[i].up())
                    if c >= 2:
                        pe.wait_ge(w_done[i].sem, w_done[i].at(2))
                        for h in range(GDN_H):
                            mm = pe.matmul(bank(i, 0)[:, h, :], AT[:, i, h, :], U[:, i, 0, h, :], start=True, stop=True)
                        mm.then_inc(y_ready[i].sem, y_ready[i].up())

            @block.vector
            def _(dve):
                if n == 0:
                    dve.memset(S[:, :, :, :], 0.0).then_inc(z_done.sem, z_done.up())
                for i, (d, c) in enumerate(pair):
                    dve.wait_ge(w_ready[i].sem, w_ready[i].at(1))
                    dve.tensor_tensor(W[:, i, :, :], bank(i, 0), wide(eg[:, i, 0, :]), ALU.mult).then_inc(chain.sem, chain.up())
                    dve.wait_ge(chain.sem, chain.last)
                    dve.tensor_tensor(W[:, i, :, :], vt[:, c, :].rearrange("p (h v) -> p h v", v=V), W[:, i, :, :], ALU.subtract).then_inc(w_done[i].sem, w_done[i].up())
                    if c >= 2:
                        dve.tensor_tensor(o1(i), bank(i, 3), wide(eg[:, i, 0, :]), ALU.mult).then_inc(w_done[i].sem, w_done[i].up())
                for i, (d, c) in enumerate(pair):
                    dve.wait_ge(u_ready[i].sem, u_ready[i].at(1))
                    dve.tensor_tensor(U[:, i, 0, :, :], bank(i, 1), wide(beta[:, c, 4 * i:4 * i + 4]), ALU.mult).then_inc(u_done[i].sem, u_done[i].up())
                    dve.wait_ge(u_done[i].sem, u_done[i].last)
                    dve.tensor_tensor(U[:, i, 1, :, :], U[:, i, 0, :, :], wide(eg[:, i, 1, :]), ALU.mult).then_inc(u_done[i].sem, u_done[i].up())
                for i, (d, c) in enumerate(pair):
                    dve.wait_ge(m_ready[i].sem, m_ready[i].at(1))
                    dve.tensor_tensor(S[0:V, i, :, :], S[0:V, i, :, :], wide(eg[0:V, i, 2, :], V), ALU.mult).then_inc(chain.sem, chain.up())
                    dve.wait_ge(chain.sem, chain.last)
                    dve.tensor_tensor(S[0:V, i, :, :], S[0:V, i, :, :], bank(i, 2)[0:V], ALU.add).then_inc(chain.sem, chain.up())
                    if c >= 2:
                        dve.wait_ge(y_ready[i].sem, y_ready[i].at(1))
                        dve.wait_ge(w_done[i].sem, w_done[i].at(2))
                        out = y[:, c - 2, :].rearrange("p (h v) -> p h v", v=V)
                        if c not in seen:
                            dve.tensor_tensor(out, o1(i), bank(i, 0), ALU.add).then_inc(y_done.sem, y_done.up())
                        else:
                            dve.tensor_tensor(o1(i), o1(i), bank(i, 0), ALU.add).then_inc(chain.sem, chain.up())
                            dve.wait_ge(chain.sem, chain.last)
                            dve.tensor_tensor(out, out, o1(i), ALU.add).then_inc(y_done.sem, y_done.up())
        k.stage_end()


def stage_out(k, src, factor):
    with ExitStack() as st:
        w = Split(k, st)
        hi, lo = (k.sb("src_" + x, [P, DB, T], st, F32R) for x in ("hi", "lo"))
        with k.block() as block:
            x_done, rounded, rested = k.sig("x_done"), k.sig("rounded"), k.sig("rested")

            @block.tensor
            def _(pe):
                for i in range(DB):
                    w.ready(pe, i)
                    for kt in range(DB):
                        if i == 0:
                            pe.wait_ge(rested.sem, rested.at(kt + 1))
                        mm = product(pe, k.ps[:, i, :], w.parts(i, kt * P, (kt + 1) * P), (hi[:, kt, :], lo[:, kt, :]), kt == 0, kt == DB - 1)
                    mm.then_inc(w.done.sem, w.done.up())

            @block.scalar
            def _(act):
                w.round(act, 0)
                for kt in range(DB):
                    act.copy(hi[:, kt, :], src[:, kt, :]).then_inc(rounded.sem, rounded.up())
                for i in range(1, DB):
                    w.round(act, i)

            @block.vector
            def _(dve):
                w.rest(dve, 0)
                for kt in range(DB):
                    dve.wait_ge(rounded.sem, rounded.at(kt + 1))
                    dve.tensor_tensor(lo[:, kt, :], src[:, kt, :], hi[:, kt, :], ALU.subtract).then_inc(rested.sem, rested.up())
                for i in range(DB):
                    if i < DB - 1:
                        w.rest(dve, i + 1)
                    w.wait(dve, i)
                    dve.scalar_tensor_tensor(k.xT[:, i, :], k.ps[:, i, :], factor(i), k.xT[:, i, :], ALU.mult, ALU.add).then_inc(x_done.sem, x_done.up())

            @block.sync
            def _(sp):
                k.stream(sp, DB)
        k.stage_end()


def stage_mlp(k, h, factor):
    HB = 16
    U2 = 2 * DB
    with ExitStack() as st:
        w = Split(k, st)
        hi, lo = (k.sb("mlp_" + x, [P, HB, T], st, F32R) for x in ("hi", "lo"))
        relu, hid = k.sb("mlp_relu", [P, 2, T], st), k.sb("mlp_hid", [P, 2, T], st)
        with k.block() as block:
            relu_done, h_done, x_done, rounded, rested = (k.sig(x) for x in ("relu_done", "he_done", "x_done", "rounded", "rested"))
            N = 2 * (HB + U2)

            def unit(half, i):
                return half * (HB + U2) + i

            @block.tensor
            def _(pe):
                for half in range(2):
                    for i in range(HB):
                        u = unit(half, i)
                        w.ready(pe, u)
                        if i >= 8:
                            pe.wait_ge(relu_done.sem, relu_done.at(half * HB + i - 7))
                        elif half:
                            pe.wait_ge(x_done.sem, x_done.at(i + 1))
                        for kt in range(DB):
                            mm = product(pe, k.ps[:, i % 8, :], w.parts(u, kt * P, (kt + 1) * P), (h[0][:, kt, :], h[1][:, kt, :]),
                                         kt == 0, kt == DB - 1)
                        mm.then_inc(w.done.sem, w.done.up())
                    for i in range(DB):
                        pe.wait_ge(relu_done.sem, relu_done.at(half * HB + 9 + i))
                        for j in range(2):
                            u = unit(half, HB + 2 * i + j)
                            w.ready(pe, u)
                            for kt in range(8):
                                f = 8 * j + kt
                                if i == 0:
                                    pe.wait_ge(rested.sem, rested.at(half * HB + f + 1))
                                mm = product(pe, k.ps[:, i, :], w.parts(u, kt * P, (kt + 1) * P), (hi[:, f, :], lo[:, f, :]), f == 0, f == HB - 1)
                            mm.then_inc(w.done.sem, w.done.up())

            @block.scalar
            def _(act):
                w.round(act, 0)
                for half in range(2):
                    for i in range(HB):
                        w.round(act, unit(half, i) + 1)
                        n = half * HB + i
                        w.wait(act, unit(half, i))
                        if n >= 2:
                            act.wait_ge(h_done.sem, h_done.at(n - 1))
                        act.activation(relu[:, n % 2, :], k.ps[:, i % 8, :], ACT.Relu).then_inc(relu_done.sem, relu_done.up())
                        act.wait_ge(h_done.sem, h_done.at(n + 1))
                        act.copy(hi[:, i, :], hid[:, n % 2, :]).then_inc(rounded.sem, rounded.up())
                    for i in range(U2):
                        if unit(half, HB + i) + 1 < N:
                            w.round(act, unit(half, HB + i) + 1)

            @block.gpsimd
            def _(pool):
                for n in range(2 * HB):
                    pool.wait_ge(relu_done.sem, relu_done.at(n + 1))
                    if n >= 2:
                        pool.wait_ge(rested.sem, rested.at(n - 1))
                    pool.tensor_tensor(hid[:, n % 2, :], relu[:, n % 2, :], relu[:, n % 2, :], ALU.mult).then_inc(h_done.sem, h_done.up())

            @block.vector
            def _(dve):
                w.rest(dve, 0)
                for half in range(2):
                    for i in range(HB):
                        w.rest(dve, unit(half, i) + 1)
                        n = half * HB + i
                        dve.wait_ge(rounded.sem, rounded.at(n + 1))
                        dve.tensor_tensor(lo[:, i, :], hid[:, n % 2, :], hi[:, i, :], ALU.subtract).then_inc(rested.sem, rested.up())
                    for i in range(U2):
                        if unit(half, HB + i) + 1 < N:
                            w.rest(dve, unit(half, HB + i) + 1)
                        if i % 2:
                            b = i // 2
                            w.wait(dve, unit(half, HB + i))
                            if half:
                                dve.wait_ge(x_done.sem, x_done.at(b + 1))
                            dve.scalar_tensor_tensor(k.xT[:, b, :], k.ps[:, b, :], factor(b), k.xT[:, b, :], ALU.mult, ALU.add).then_inc(x_done.sem, x_done.up())

            @block.sync
            def _(sp):
                k.stream(sp, N)
        k.stage_end()


def stage_store(k):
    with k.block() as block:
        @block.sync
        def _(sp):
            stored = k.sig("stored")
            sp.dma_start(k.dram["out"], k.xT[:, :, :]).then_inc(stored.sem, stored.up(16))
            sp.wait_ge(stored.sem, stored.at(16))
    k.stage_end()


def stage_silu(k, x):
    with k.block() as block:
        @block.scalar
        def _(act):
            act.activation(x[:, :, :], x[:, :, :], ACT.Silu).then_inc(k.sig("silu_done").sem, k.sig("silu_done").up())
    k.stage_end()


def program(nc, dram):
    dram["slots"], dram["h_tok"], dram["picks"] = (
        nc.dram_tensor(n, shape, F32).ap() for n, shape in (("slots", (P * NE, 1)), ("h_tok", (T, D)), ("picks", (2 * T, D))))
    with ExitStack() as ctx:
        k = Core(nc, dram, ctx)
        stage_load(k)
        with ExitStack() as b1:
            h = [k.sb("h_" + x, [P, DB, T], b1, F32R) for x in ("hi", "lo")]
            with ExitStack() as pre:
                hT = k.sb("hT", [P, DB, T], pre)
                stage_norm(k, "n1", lambda b: k.xT[:, b, :], lambda b: hT[:, b, :], T, lambda b: k.col("norm1_g", b),
                           split=lambda b: (h[0][:, b, :], h[1][:, b, :]))
            ybT = k.sb("ybT", [P, RB, T], b1)
            with ExitStack() as na:
                qT, kT, vt = (k.sb(n, [P, 4, T], na) for n in ("qT", "kT", "vt"))
                rel = k.sb("na_rel", [P, RH, OFFS * GRID_W], na)
                stage_qkv(k, h, qT, kT, vt, rel)
                stage_qk_norm(k, qT, kT)
                stage_attention(k, qT, kT, vt, rel, ybT)
            yaT = k.sb("yaT", [P, RB, T], b1)
            with ExitStack() as rw:
                rT, kT = (k.sb(n, [P, RB, T], rw) for n in ("rT", "rkT"))
                lora = k.sb("lora", [P, 3, T], rw)
                stage_rwkv_in(k, h, rT, kT, yaT, lora)
                stage_rwkv(k, rT, kT, yaT, lora, yaT)
            mod_part = k.sb("mod_part", [P, MG + 2, UNIT], b1)
            stage_merge(k, h, yaT, ybT, mod_part)
            stage_mod(k, mod_part)
        with ExitStack() as b1:
            hT = k.sb("h2T", [P, DB, T], b1)
            comb = k.sb("comb", [P, NT, NE], b1)
            stage_norm(k, "n2", lambda b: k.xT[:, b, :], lambda b: hT[:, b, :], T, lambda b: k.col("norm2_g", b))
            hot, wt = k.sb("hot", [P, 2, NT, NE], b1), k.sb("pick_weight", [P, 2, NT], b1)
            slot_row, slot_tok = (k.sb(n, [P, NE], b1, U32) for n in ("slot_row", "slot_tok"))
            count = k.sb("count", [P, 1], b1, U32)
            stage_router(k, hT, comb, hot, wt)
            stage_dispatch(k, hT, hot, slot_row, slot_tok, count)
            acc = k.sb("acc", [P, NT, D], b1)
            stage_moe(k, hT, comb, acc, slot_row, slot_tok, count, wt)
            stage_add_tokens(k, acc)
        with ExitStack() as b2:
            mod, gain = k.mod, k.gain
            with ExitStack() as mixer:
                mixT = k.sb("mixT", [P, DB, T], mixer)
                h = [k.sb("hm_" + x, [P, DB, T2], mixer, F32R) for x in ("hi", "lo")]
                with ExitStack() as pre:
                    hT = k.sb("hmT", [P, DB, T2], pre)
                    stage_load_ctx(k, hT)
                    stage_norm(k, "n3", lambda b: hT[:, b, 0:CTX], lambda b: hT[:, b, 0:CTX], CTX,
                               lambda b: gain[:, 1, b:b + 1], shift=lambda b: mod[:, b, 1:2],
                               split=lambda b: (h[0][:, b, 0:CTX], h[1][:, b, 0:CTX]))
                    stage_norm(k, "n4", lambda b: k.xT[:, b, :], lambda b: hT[:, b, CTX:T2], T,
                               lambda b: gain[:, 0, b:b + 1], shift=lambda b: mod[:, b, 0:1],
                               split=lambda b: (h[0][:, b, CTX:T2], h[1][:, b, CTX:T2]))
                with ExitStack() as hy:
                    u = k.sb("hy_u", [P, 6, T], hy)
                    with ExitStack() as raw:
                        z = k.sb("hy_raw", [P, 6, T], raw)
                        stage_project(k, h, [(z[:, i, :], None, ACT.Copy, 1.0) for i in range(6)],
                                      [[(u[:, i, :], z[:, i, :], T // GRID_W, i, P)] for i in range(6)], Taps(k, "hy_w", 3),
                                      lambda i: k.col("hy_b", i))
                    stage_hyena(k, u, mixT)
                ldec, beta = k.sb("ldec", [P, NT2, 8], mixer), k.sb("beta", [P, NT2, 8], mixer)
                with ExitStack() as gla:
                    la = k.sb("gla_la", [P, 2, NT2, 256], gla)
                    with ExitStack() as pre:
                        aT = k.sb("aT2", [P, T2], pre)
                        gt = k.sb("gt", [P, NT2, 16], pre)
                        stage_project(k, h, [(aT[:, CTX:T2], aT[:, 0:CTX], ACT.Copy, 1.0)])
                        stage_to_tokens(k, [(gt[:, t, :], aT[64:80, t * P:(t + 1) * P], 64) for t in range(NT2)])
                        stage_gates(k, aT, gt, la, ldec, beta)
                    qT, kT = k.sb("gla_q", [P, 2, T], gla), k.sb("gla_k", [P, 2, T2], gla)
                    vt, gateT = k.sb("gla_v", [P, NT2, VW], gla), k.sb("gla_gate", [P, 3, T], gla)
                    y = k.sb("gla_y", [P, NT, VW], gla)
                    with ExitStack() as pre:
                        vT = k.sb("gla_vT", [P, 3, T2], pre)
                        stage_project(k, h, [(qT[:, b, :], None, ACT.Copy, GLA_DK ** -0.5) for b in range(2)] +
                                      [(kT[:, b, CTX:T2], kT[:, b, 0:CTX], ACT.Copy, 1.0) for b in range(2)] +
                                      [(vT[:, b, CTX:T2], vT[:, b, 0:CTX], ACT.Copy, 1.0) for b in range(3)] +
                                      [(gateT[:, b, :], None, ACT.Silu, 1.0) for b in range(3)])
                        stage_to_tokens(k, [(vt[:, t, b * P:(b + 1) * P], vT[:, b, t * P:(t + 1) * P])
                                            for t in range(NT2) for b in range(3)])
                    S = k.sb("gla_S", [P, 2, GLA_DV], gla)
                    for d, order in (("f", (0, 1, 2, 3, 4, 5)), ("b", (1, 0, 5, 4, 3, 2))):
                        for n, c in enumerate(order):
                            stage_gla_chunk(k, d, c, n, qT, kT, vt, la, S, y)
                    stage_head_norm(k, y, "gla_g", gateT, mixT, 2)
                with ExitStack() as gdn:
                    qT, kT = k.sb("gdn_q", [P, 4, T], gdn), k.sb("gdn_k", [P, 4, T2], gdn)
                    vt, gateT = k.sb("gdn_v", [P, NT2, VW], gdn), k.sb("gdn_gate", [P, 3, T], gdn)
                    taps = Taps(k, "gdn_w", 7)

                    def conv(dst, z, b, i, n):
                        return [(dst[0:n, b, CTX:T2], z[0:n, b, CTX:T2], T // GRID_W, i, n),
                                (dst[0:n, b, 0:CTX], z[0:n, b, 0:CTX], 1, i, n)]
                    with ExitStack() as pre:
                        z = k.sb("gdn_z", [P, 4, T2], pre)
                        stage_project(k, h, [(z[:, b, CTX:T2], None, ACT.Copy, 1.0) for b in range(4)],
                                      [[(qT[0:96, b, :], z[0:96, b, CTX:T2], T // GRID_W, b, 96)] for b in range(4)], taps)
                        stage_project(k, h, [(z[:, b, CTX:T2], z[:, b, 0:CTX], ACT.Copy, 1.0) for b in range(4)],
                                      [conv(kT, z, b, 4 + b, 96) for b in range(4)], taps)
                        vT = k.sb("gdn_vT", [P, 3, T2], pre)
                        stage_project(k, h, [(z[:, b, CTX:T2], z[:, b, 0:CTX], ACT.Copy, 1.0) for b in range(3)] +
                                      [(gateT[:, b, :], None, ACT.Silu, 1.0) for b in range(3)],
                                      [conv(vT, z, b, 8 + b, P) for b in range(3)] + [[]] * 3, taps)
                        stage_to_tokens(k, [(vt[:, t, b * P:(b + 1) * P], vT[:, b, t * P:(t + 1) * P])
                                            for t in range(NT2) for b in range(3)])
                        stage_silu(k, vt)
                        stage_l2(k, qT, kT)
                    kt = k.sb("gdn_kt", [P, NT2, GDN_H, GDN_D], gdn)
                    stage_to_tokens(k, [(kt[:, t, h, :], kT[0:GDN_D, h, t * P:(t + 1) * P])
                                        for t in range(NT2) for h in range(GDN_H)])
                    y = k.sb("gdn_y", [P, NT, VW], gdn)
                    S = k.sb("gdn_S", [P, 2, GDN_H, GDN_D], gdn)
                    LT, AT = k.sb("gdn_LT", [P, 2, GDN_H, P], gdn), k.sb("gdn_AT", [P, 2, GDN_H, P], gdn)
                    eg = k.sb("gdn_eg", [P, 2, 4, GDN_H], gdn)
                    w = {x: k.sb("gdn_" + x, [P, 2 * GDN_H, P], gdn) for x in ("X", "XT", "M", "Y")}
                    seen = set()
                    for n in range(NT2):
                        pair = [("f", n), ("b", (1, 0, 5, 4, 3, 2)[n])]
                        stage_gdn_chunk(k, pair, qT, kT, ldec, beta, LT, AT, eg)
                        stage_solve(k, w, 2 * GDN_H, lambda h2: LT[:, h2, :, :], (False, True))
                        stage_gdn_step(k, pair, n, seen, qT, kT, kt, vt, w, AT, eg, beta, S, y)
                        seen |= {c for _, c in pair}
                    stage_head_norm(k, y, "gdn_g", gateT, mixT, 5)
                stage_out(k, mixT, lambda i: mod[:, 16 + i, 0:1])
            with ExitStack() as ml:
                h = [k.sb("h4_" + x, [P, DB, T], ml, F32R) for x in ("hi", "lo")]
                with ExitStack() as pre:
                    hT = k.sb("h4T", [P, DB, T], pre)
                    stage_norm(k, "n5", lambda b: k.xT[:, b, :], lambda b: hT[:, b, :], T,
                               lambda b: gain[:, 2, b:b + 1], shift=lambda b: mod[:, 24 + b, 0:1],
                               split=lambda b: (h[0][:, b, :], h[1][:, b, :]))
                stage_mlp(k, h, lambda i: mod[:, 40 + i, 0:1])
        stage_norm(k, "n6", lambda b: k.xT[:, b, :], lambda b: k.xT[:, b, :], T, lambda b: k.col("final_g", b))
        stage_store(k)
        assert k.taken == k.issued == N_UNITS


def _blocks(w, cols=P):
    kk, n = w.shape
    return w.reshape(kk // P, P, n // P, P).transpose(2, 1, 0, 3).reshape(n // P, P, kk)


def _tok_units(w):
    n = w.shape[1]
    return w.reshape(DB, P, n).transpose(1, 0, 2).reshape(P, -1, UNIT).transpose(1, 0, 2)


def _slots(w, heads, width, slot):
    out = np.zeros((w.shape[0], heads, slot), np.float32)
    out[:, :, :width] = w.reshape(w.shape[0], heads, width)
    return out.reshape(w.shape[0], heads * slot)


def _colmajor(v):
    return v.reshape(-1, P).T


def host_constants():
    i = np.arange(P)
    s, t = i[:, None], i[None, :]
    f = np.float32
    part = {"ident": s == t, "ones": np.ones((P, P)), "ones64": s // HD == t // HD}
    lvl = []
    for lv in range(LEVELS):
        half = 1 << lv
        lvl.append((s // (2 * half) == t // (2 * half)) & (s % (2 * half) < half) & (t % (2 * half) >= half))
    part["tri_f"] = np.hstack([s <= t, s < t])
    part["tri_b"] = np.hstack([s >= t, s > t])
    part["attn_f"] = np.hstack([s < t, s <= t] * 2)
    part["attn_b"] = np.hstack([s > t, s >= t] * 2)
    part["level_f"] = np.hstack(lvl)
    part["level_b"] = np.hstack([m.T for m in lvl])
    const = np.hstack([part[n] for n in CONST]).astype(f)
    hsum = np.zeros((P, RB, 8), f)
    for b in range(RB):
        hsum[i, b, 2 * b + i // HD] = 1
    cols = np.arange(GRID_W)
    start = np.clip(cols - 8, 0, GRID_W - 16)
    seen = (cols[None] >= start[:, None]) & (cols[None] < start[:, None] + 16)
    na = np.where(seen, 0, -1e30).astype(f)
    gidx = np.broadcast_to(np.concatenate([4 - np.arange(4), 8 - np.arange(8)]), (P, 12)).astype(f)
    rows = (np.arange(2)[:, None] * T + np.arange(NT)[None] * P).reshape(1, -1) + i[:, None]
    slot_vals = np.hstack([rows, np.broadcast_to(np.arange(NE), (P, NE))]).astype(f)
    n = 2 * T - 1
    ang = 2 * np.pi * ((np.arange(T)[:, None] * np.arange(NFREQ)[None]) % n) / n
    dft = np.hstack([np.cos(ang), -np.sin(ang)])
    wt = np.where(np.arange(NFREQ) == 0, 1.0, 2.0)[:, None] / n
    inv = np.vstack([np.cos(ang.T) * wt, -np.sin(ang.T) * wt])
    dft = dft.reshape(NT, P, 2 * NFREQ).transpose(1, 0, 2)
    inv = inv.reshape(8, P, T).transpose(1, 0, 2)
    tl = np.linspace(0.0, 1.0, T, dtype=f)[:, None]
    fr = np.linspace(1e-4, 15, 16, dtype=f)
    w = (2 * np.pi * np.arange(T, dtype=f) / T).astype(f)
    an = w[:, None] * fr[None]
    z = np.concatenate([tl, np.cos(an), -np.sin(an)], -1).T
    deltas = np.abs(np.linspace(np.log(1e-2) / 1.5, np.log(1e-2) / 0.3, HY_C, dtype=f))
    win = np.exp(-tl * deltas[None])
    back = win.copy()
    back[0] = 0
    win = np.hstack([win, back]).reshape(NT, P, 2 * HY_C).transpose(1, 0, 2)
    hy = np.zeros((P, T), f)
    hy[:33] = z
    return {"const": const, "hsum": hsum.reshape(P, -1), "na_mask": np.vstack([na, na]), "gidx": gidx,
            "slot_vals": slot_vals,
            "dft": dft.astype(f), "inv": inv.astype(f), "hy_z": hy, "hy_win": win.astype(f)}


def host_layout(a):
    f = np.float32
    hc = host_constants()
    l = {n: (v[0] if n not in ("x", "c_2", "ctx_2", "c_ctx_2", "final_norm_g_2") else v) for n, v in a.items()}
    w_in, w_in2 = l["w_in"], l["w_in_2"]
    o = 1920
    q, kk, v, gate = w_in[:, o:o + 512], w_in[:, o + 512:o + 1024], w_in[:, o + 1024:o + 1536], w_in[:, o + 1536:]
    wo = np.concatenate([l["w_o_rwkv"], l["w_o_na"]])
    gu = np.concatenate([l["w_gate_e"], l["w_up_e"]], 2).reshape(NE, 4, 2, P, 512).transpose(0, 1, 3, 2, 4)
    moe = np.concatenate([gu.reshape(NE, 4, P, UNIT), l["w_down_e"].reshape(NE, 2, P, D)], 1)
    hy, gla, gdn = w_in2[:, :768], w_in2[:, 768:768 + 1184], w_in2[:, 768 + 1184:]
    misc = np.zeros((D, P), f)
    misc[:, 0:16], misc[:, 32:48], misc[:, 64:80] = gla[:, 1152:1168], gla[:, 1168:1184], gdn[:, 1536:1552]
    mlp1 = _blocks(l["w_mlp1_2"]).reshape(2, 16, P, UNIT)
    mlp2 = l["w_mlp2_2"].reshape(2, 2, 8, P, 8, P).transpose(0, 4, 1, 3, 2, 5).reshape(2, 16, P, UNIT)
    parts = {
        "qk": _blocks(np.hstack([q, kk])), "v": _tok_units(v), "rwkv": _blocks(w_in[:, :o]),
        "gate": _blocks(gate), "o": _blocks(wo), "out": _blocks(l["w_out"]), "moe": moe.reshape(-1, P, UNIT),
        "hy": _blocks(hy), "misc2": _blocks(misc),
        "gla_q": _blocks(_slots(gla[:, 0:192], 4, 48, 64)), "gla_k": _blocks(_slots(gla[:, 192:384], 4, 48, 64)),
        "gla_v": _blocks(gla[:, 384:768]), "gla_gate": _blocks(gla[:, 768:1152]),
        "gdn_qk": _blocks(_slots(gdn[:, 0:768], 8, 96, 128)), "gdn_v": _blocks(gdn[:, 768:1152]),
        "gdn_gate": _blocks(gdn[:, 1152:1536]),
        "out2": _blocks(l["w_out_2"]), "mlp": np.concatenate([mlp1, mlp2], 1).reshape(64, P, UNIT),
    }
    for n, (at, units) in STREAM.items():
        assert parts[n].shape == (units, P, UNIT), (n, parts[n].shape)
    stream = np.concatenate([parts[n] for n in STREAM])

    def pad(v, n=P):
        out = np.zeros((n, v.shape[1]), f)
        out[:len(v)] = v
        return out
    gw = l["gdn_conv_w_2"]
    gdn_w = np.zeros((P, 11, 7), f)
    gdn_w[:96, :8] = gw[:, :768].reshape(7, 8, 96).transpose(2, 1, 0)
    gdn_w[:, 8:] = gw[:, 768:].reshape(7, 3, P).transpose(2, 1, 0)
    col = {
        **{n: _colmajor(l[n]) for n in ("norm1_g", "mu_prev", "mu_next", "a0_f", "a0_b", "k_k", "k_a", "b_gate",
                                        "norm2_g", "norm1_g_2", "norm2_g_2")},
        "r_k": _colmajor(l["r_k"].reshape(-1)), "b_mod": _colmajor(l["b_mod_2"]),
        "q_gain": np.concatenate([l["q_gain"]] * 2)[:, None], "k_gain": np.concatenate([l["k_gain"]] * 2)[:, None],
        "cc": np.stack([_colmajor(l["c_2"][0]), _colmajor(l["c_ctx_2"])], 2).reshape(P, 16),
        "hy_w": l["hy_conv_w_2"].reshape(3, 6, P).transpose(2, 1, 0).reshape(P, 18),
        "hy_b": _colmajor(l["hy_conv_b_2"]), "hy_d": _colmajor(l["hy_d_2"].reshape(-1)),
        "gdn_w": gdn_w.reshape(P, 77), "final_g": _colmajor(l["final_norm_g_2"]),
        "hy_b1": pad(l["hy_f_b1_2"][:, None]), "hy_b2": pad(l["hy_f_b2_2"][:, None]),
        "hy_f1": pad(l["hy_sin_freq_2"][0][:, None]), "hy_f2": pad(l["hy_sin_freq_2"][1][:, None]),
    }
    row = {
        "w0_f": l["w0_f"], "w0_b": l["w0_b"], "lnx_g": l["lnx_g"], "lnx_b": l["lnx_b"],
        "b_router": np.concatenate([l["b_router_group"], l["b_router_expert"]]),
        "gla_b": np.concatenate([_slots(l["gla_b_a_2"][d][None], 4, 48, 64)[0] for d in range(2)]),
        "gla_g": l["gla_norm_g_2"], "gdn_g": l["gdn_norm_g_2"], "a_log": l["gdn_a_log_2"].reshape(-1),
        "dt_bias": l["gdn_dt_bias_2"].reshape(-1),
    }
    router = np.hstack([l["w_router_group"], l["w_router_expert"]]).reshape(DB, P, 36).transpose(1, 0, 2)
    a2 = np.zeros((P, 256), f)
    a2[0:16], a2[32:48] = (_slots(l["gla_w_a2_2"][d], 4, 48, 64) for d in range(2))
    mat = {
        "w_up": np.vstack([l["w_up_f"], l["w_up_b"]]), "a_up": np.vstack([l["a_up_f"], l["a_up_b"]]),
        "g_up": l["g_up"], "hsum": hc["hsum"], "router": router.reshape(P, -1), "hy_w1": pad(l["hy_f_w1_2"]),
        "hy_w2": pad(l["hy_f_w2_2"]), "hy_w3": pad(l["hy_f_w3_2"]), "gla_a2": a2, "na_mask": hc["na_mask"],
        "gidx": hc["gidx"], "slot_vals": hc["slot_vals"],
    }
    rpb = l["rpb"]
    cols = np.arange(GRID_W)
    off = np.clip(cols[None] - cols[:, None] + 15, 0, 30)
    e = rpb[:, :, off]
    rel = np.stack([e[:, 1:15], e[:, 0:14]]).transpose(0, 3, 1, 2, 4).reshape(P, RH, 14 * GRID_W)

    def chan(x):
        return x.T.reshape(DB, P, -1).transpose(1, 0, 2)
    w_mod = l["w_mod_2"].reshape(DB, P, MG, UNIT).transpose(2, 0, 1, 3).reshape(MG * DB, P, UNIT)
    return {"stream": stream, "w_mod": w_mod, "xT": chan(l["x"][0]), "ctxT": chan(l["ctx_2"][0]), "const": hc["const"],
            "cols": np.hstack([col[n] for n in COL]), "rows": np.concatenate([row[n] for n in ROW])[None],
            "mats": np.hstack([mat[n] for n in MAT]), "rel": rel,
            "dft": hc["dft"], "inv": hc["inv"], "hy_z": hc["hy_z"], "hy_win": hc["hy_win"]}


def kernel(**inputs):
    import concourse.bacc as bacc
    from concourse.bass_utils import run_bass_kernel_spmd

    nc = bacc.Bacc("TRN2", target_bir_lowering=False, num_devices=1)
    arrays, dram = {}, {}
    for name, a in host_layout({n: np.asarray(v) for n, v in inputs.items()}).items():
        a = np.ascontiguousarray(a, dtype=np.float32)
        arrays[name + "_in"] = a
        dram[name] = nc.dram_tensor(name + "_in", a.shape, F32, kind="ExternalInput").ap()
    dram["out"] = nc.dram_tensor("out_0", (P, DB, T), F32, kind="ExternalOutput").ap()
    program(nc, dram)
    r = run_bass_kernel_spmd(nc, [arrays], core_ids=[0])
    out = r.results[0]["out_0"]
    return out.transpose(2, 1, 0).reshape(1, T, D)
```
